# Optimizing a Trainium2 kernel written in Bass

```python
import jax
import jax.numpy as jnp
from jax import lax
import numpy as np
import jax, jax.numpy as jnp

D_MODEL = 1024
BATCH = 1
SEQ = 1024
DEPTH = 1

D_MIX = D_MODEL
SB_HEAD_DIM = 64
D_SB = D_MIX // 2
SB_HEADS = D_SB // SB_HEAD_DIM
BLOCK_Q = 128
D_LRU = D_MIX // 4
LRU_BLOCKS = 4
LRU_BLOCK = D_LRU // LRU_BLOCKS
LRU_CONV_WIDTH = 4
LRU_C = 8.0
D_CONF = D_MIX // 4
CONF_CONV_WIDTH = 31
D_IN = 3 * D_SB + 2 * D_LRU + 2 * D_CONF
N_GROUPS = 4
EXPERTS_PER_GROUP = 8
N_EXPERTS = N_GROUPS * EXPERTS_PER_GROUP
TOP_K_FINE = 2
D_EXPERT = D_MODEL // 2
MOE_BLOCK = 256
EPS = 1e-6


def rms_norm(x, g):
    xf = x.astype(jnp.float32)
    y = xf * lax.rsqrt(jnp.mean(xf * xf, axis=-1, keepdims=True) + EPS)
    return (y * g.astype(jnp.float32)).astype(x.dtype)

def layer_norm(x, g, b):
    xf = x.astype(jnp.float32)
    mu = jnp.mean(xf, axis=-1, keepdims=True)
    xc = xf - mu
    var = jnp.mean(xc * xc, axis=-1, keepdims=True)
    return xc * lax.rsqrt(var + EPS) * g.astype(jnp.float32) + b.astype(jnp.float32)

def causal_depthwise_conv(x, w, b):
    k_width, chans = w.shape
    y = lax.conv_general_dilated(
        x, w.astype(x.dtype)[:, None, :], window_strides=(1,),
        padding=[(k_width - 1, 0)], dimension_numbers=('NWC', 'WIO', 'NWC'),
        feature_group_count=chans)
    return y + b.astype(x.dtype)

def stick_breaking_attention(q, k, v):
    seq = q.shape[2]
    scale = SB_HEAD_DIM ** -0.5
    outs = []
    for i in range(seq // BLOCK_Q):
        q0 = i * BLOCK_Q
        kv_len = q0 + BLOCK_Q
        qb = q[:, :, q0:kv_len]
        kb = k[:, :, :kv_len]
        vb = v[:, :, :kv_len]
        z = jnp.einsum('bhqd,bhkd->bhqk', qb, kb, preferred_element_type=jnp.float32) * scale
        t_pos = q0 + jnp.arange(BLOCK_Q, dtype=jnp.int32)[:, None]
        s_pos = jnp.arange(kv_len, dtype=jnp.int32)[None, :]
        mask = s_pos < t_pos
        log_keep = jnp.where(mask, jax.nn.log_sigmoid(-z), 0.0)
        suffix = lax.cumsum(log_keep, axis=3, reverse=True) - log_keep
        wts = jnp.where(mask, jnp.exp(jax.nn.log_sigmoid(z) + suffix), 0.0)
        outs.append(jnp.einsum('bhqk,bhkd->bhqd', wts.astype(vb.dtype), vb))
    return jnp.concatenate(outs, axis=2)

def _linear_combine(c1, c2):
    a1, b1 = c1
    a2, b2 = c2
    return a1 * a2, a2 * b1 + b2

def rg_lru_branch(xr, xg, conv_w, conv_b, wa, ba, wx, bx, lam):
    f32 = jnp.float32
    bsz, seq, _ = xr.shape
    xr = causal_depthwise_conv(xr, conv_w, conv_b)
    xblk = xr.reshape(bsz, seq, LRU_BLOCKS, LRU_BLOCK)
    gate_r = jnp.einsum('bsnc,ncd->bsnd', xblk, wa).reshape(bsz, seq, D_LRU) + ba
    gate_i = jnp.einsum('bsnc,ncd->bsnd', xblk, wx).reshape(bsz, seq, D_LRU) + bx
    log_a = LRU_C * jax.nn.sigmoid(gate_r.astype(f32)) * jax.nn.log_sigmoid(lam.astype(f32))
    a = jnp.exp(log_a)
    u = jnp.sqrt(-jnp.expm1(2.0 * log_a)) * (jax.nn.sigmoid(gate_i.astype(f32)) * xr.astype(f32))
    _, h = lax.associative_scan(_linear_combine, (a, u), axis=1)
    return (h * jax.nn.gelu(xg.astype(f32))).astype(xr.dtype)

def conformer_conv(xc, dw_w, dw_b, ln_g, ln_b, pw_w, pw_b):
    val, gate = jnp.split(xc, 2, axis=-1)
    u = val * jax.nn.sigmoid(gate)
    u = causal_depthwise_conv(u, dw_w, dw_b)
    u = jax.nn.silu(layer_norm(u, ln_g, ln_b)).astype(xc.dtype)
    return jnp.einsum('bsc,ce->bse', u, pw_w) + pw_b

def hierarchical_moe(h, w_coarse, w_fine, w_gate, w_up, w_down):
    n_tok, d = h.shape
    f32 = jnp.float32
    logits_c = jnp.einsum('nd,dg->ng', h, w_coarse, preferred_element_type=f32)
    probs_c = jax.nn.softmax(logits_c, axis=-1)
    grp = jnp.argmax(logits_c, axis=-1).astype(jnp.int32)
    w_grp = jnp.take_along_axis(probs_c, grp[:, None], axis=-1)
    logits_f = jnp.einsum('nd,de->ne', h, w_fine, preferred_element_type=f32)
    logits_f = logits_f.reshape(n_tok, N_GROUPS, EXPERTS_PER_GROUP)
    logits_f = jnp.take_along_axis(logits_f, grp[:, None, None], axis=1)[:, 0]
    top_val, top_idx = lax.top_k(logits_f, TOP_K_FINE)
    gate = (jax.nn.softmax(top_val, axis=-1) * w_grp).astype(h.dtype)
    expert = grp[:, None] * EXPERTS_PER_GROUP + top_idx.astype(jnp.int32)

    n_asg = n_tok * TOP_K_FINE
    flat_e = expert.reshape(n_asg)
    flat_tok = jnp.repeat(jnp.arange(n_tok, dtype=jnp.int32), TOP_K_FINE)
    flat_gate = gate.reshape(n_asg)
    order = jnp.argsort(flat_e)
    sorted_e = flat_e[order]
    counts = jnp.bincount(flat_e, length=N_EXPERTS).astype(jnp.int32)
    padded = (counts + MOE_BLOCK - 1) // MOE_BLOCK * MOE_BLOCK
    starts = jnp.cumsum(counts) - counts
    padded_ends = jnp.cumsum(padded)
    padded_starts = padded_ends - padded
    dest = padded_starts[sorted_e] + jnp.arange(n_asg, dtype=jnp.int32) - starts[sorted_e]
    n_blocks = -(-n_asg // MOE_BLOCK) + N_EXPERTS
    n_slots = n_blocks * MOE_BLOCK
    slot_tok = jnp.full((n_slots,), n_tok, jnp.int32).at[dest].set(flat_tok[order])
    slot_gate = jnp.zeros((n_slots,), h.dtype).at[dest].set(flat_gate[order])
    block_start = jnp.arange(n_blocks, dtype=jnp.int32) * MOE_BLOCK
    block_e = jnp.minimum(jnp.searchsorted(padded_ends, block_start, side='right'),
                          N_EXPERTS - 1).astype(jnp.int32)
    h_pad = jnp.concatenate([h, jnp.zeros((1, d), h.dtype)], axis=0)
    xb = h_pad[slot_tok].reshape(n_blocks, MOE_BLOCK, d)

    def run_block(args):
        xe, e = args
        return (jax.nn.silu(xe @ w_gate[e]) * (xe @ w_up[e])) @ w_down[e]

    yb = lax.map(run_block, (xb, block_e)).reshape(n_slots, d)
    y = jnp.zeros((n_tok + 1, d), yb.dtype).at[slot_tok].add(yb * slot_gate[:, None])
    return y[:n_tok]

def first_inputs(seed: int = 0) -> dict:
    key = jax.random.key(seed)
    ks = jax.random.split(key, 28)
    f32 = jnp.float32
    L = DEPTH

    def nrm(k, shape, scale):
        return jax.random.normal(k, shape, f32) * scale

    def gain(k, shape):
        return 1.0 + 0.05 * jax.random.normal(k, shape, f32)

    a_c = jax.random.uniform(ks[11], (L, D_LRU), f32, 0.9, 0.999)
    a0 = a_c ** (1.0 / LRU_C)
    lam = jnp.log(a0) - jnp.log1p(-a0)

    return {
        'x': jax.random.normal(ks[0], (BATCH, SEQ, D_MODEL), f32),
        'norm1_g': gain(ks[1], (L, D_MODEL)),
        'w_in': nrm(ks[2], (L, D_MODEL, D_IN), D_MODEL ** -0.5),
        'q_norm_g': gain(ks[3], (L, SB_HEAD_DIM)),
        'k_norm_g': gain(ks[4], (L, SB_HEAD_DIM)),
        'lru_conv_w': nrm(ks[5], (L, LRU_CONV_WIDTH, D_LRU), LRU_CONV_WIDTH ** -0.5),
        'lru_conv_b': nrm(ks[6], (L, D_LRU), 0.02),
        'lru_wa': nrm(ks[7], (L, LRU_BLOCKS, LRU_BLOCK, LRU_BLOCK), LRU_BLOCK ** -0.5),
        'lru_ba': nrm(ks[8], (L, D_LRU), 0.02),
        'lru_wx': nrm(ks[9], (L, LRU_BLOCKS, LRU_BLOCK, LRU_BLOCK), LRU_BLOCK ** -0.5),
        'lru_bx': nrm(ks[10], (L, D_LRU), 0.02),
        'lru_lambda': lam,
        'conf_dw_w': nrm(ks[12], (L, CONF_CONV_WIDTH, D_CONF), CONF_CONV_WIDTH ** -0.5),
        'conf_dw_b': nrm(ks[13], (L, D_CONF), 0.02),
        'conf_ln_g': gain(ks[14], (L, D_CONF)),
        'conf_ln_b': nrm(ks[15], (L, D_CONF), 0.02),
        'conf_pw_w': nrm(ks[16], (L, D_CONF, D_CONF), D_CONF ** -0.5),
        'conf_pw_b': nrm(ks[17], (L, D_CONF), 0.02),
        'out_norm_g': gain(ks[18], (L, D_MIX)),
        'w_out': nrm(ks[19], (L, D_MIX, D_MODEL), D_MIX ** -0.5),
        'norm2_g': gain(ks[20], (L, D_MODEL)),
        'router_coarse': nrm(ks[21], (L, D_MODEL, N_GROUPS), D_MODEL ** -0.5),
        'router_fine': nrm(ks[22], (L, D_MODEL, N_EXPERTS), D_MODEL ** -0.5),
        'exp_w_gate': nrm(ks[23], (L, N_EXPERTS, D_MODEL, D_EXPERT), D_MODEL ** -0.5),
        'exp_w_up': nrm(ks[24], (L, N_EXPERTS, D_MODEL, D_EXPERT), D_MODEL ** -0.5),
        'exp_w_down': nrm(ks[25], (L, N_EXPERTS, D_EXPERT, D_MODEL), D_EXPERT ** -0.5),
    }

def first_block(x, norm1_g, w_in, q_norm_g, k_norm_g, lru_conv_w, lru_conv_b, lru_wa, lru_ba,
              lru_wx, lru_bx, lru_lambda, conf_dw_w, conf_dw_b, conf_ln_g, conf_ln_b,
              conf_pw_w, conf_pw_b, out_norm_g, w_out, norm2_g, router_coarse, router_fine,
              exp_w_gate, exp_w_up, exp_w_down):
    bsz, seq, d = x.shape
    splits = [D_SB, 2 * D_SB, 3 * D_SB, 3 * D_SB + D_LRU, 3 * D_SB + 2 * D_LRU]
    for l in range(DEPTH):
        h = rms_norm(x, norm1_g[l])
        proj = jnp.einsum('bsd,de->bse', h, w_in[l])
        q, k, v, xr, xg, xc = jnp.split(proj, splits, axis=-1)
        q = rms_norm(q.reshape(bsz, seq, SB_HEADS, SB_HEAD_DIM), q_norm_g[l]).transpose(0, 2, 1, 3)
        k = rms_norm(k.reshape(bsz, seq, SB_HEADS, SB_HEAD_DIM), k_norm_g[l]).transpose(0, 2, 1, 3)
        v = v.reshape(bsz, seq, SB_HEADS, SB_HEAD_DIM).transpose(0, 2, 1, 3)
        y_a = stick_breaking_attention(q, k, v).transpose(0, 2, 1, 3).reshape(bsz, seq, D_SB)
        y_b = rg_lru_branch(xr, xg, lru_conv_w[l], lru_conv_b[l], lru_wa[l], lru_ba[l],
                            lru_wx[l], lru_bx[l], lru_lambda[l])
        y_c = conformer_conv(xc, conf_dw_w[l], conf_dw_b[l], conf_ln_g[l], conf_ln_b[l],
                             conf_pw_w[l], conf_pw_b[l])
        g_out = out_norm_g[l]
        y = jnp.concatenate([
            rms_norm(y_a, g_out[:D_SB]),
            rms_norm(y_b, g_out[D_SB:D_SB + D_LRU]),
            rms_norm(y_c, g_out[D_SB + D_LRU:]),
        ], axis=-1)
        x = x + jnp.einsum('bse,ed->bsd', y, w_out[l])
        h2 = rms_norm(x, norm2_g[l]).reshape(bsz * seq, d)
        x = x + hierarchical_moe(h2, router_coarse[l], router_fine[l], exp_w_gate[l],
                                 exp_w_up[l], exp_w_down[l]).reshape(bsz, seq, d)
    return x


DEPTH_2 = 2

GRID_W = 64
CTX_LEN = 256

DEEPNORM_ALPHA = (2 * DEPTH_2) ** 0.25
DEEPNORM_BETA = (8 * DEPTH_2) ** -0.25
LN_EPS = 1e-6

N_EVEN = (DEPTH_2 + 1) // 2
N_ODD = DEPTH_2 // 2

GLA_HEADS = 4
GLA_DK = 64
GLA_DV = 128
GLA_QK_W = GLA_HEADS * GLA_DK
GLA_V_W = GLA_HEADS * GLA_DV
GLA_GATE_RANK = 16
GLA_TAU = 16.0
GLA_CHUNK = 64

MLA_HEADS = 8
MLA_NOPE = 64
MLA_ROPE = 32
MLA_V = 64
MLA_Q_RANK = 256
MLA_KV_RANK = 128
MLA_V_W = MLA_HEADS * MLA_V
MLA_SCALE = (MLA_NOPE + MLA_ROPE) ** -0.5
ROPE_BASE = 10000.0
Q_BLOCK = 128

FNET_GROUPS = 4
FNET_GROUP_CH = 128
FNET_W = FNET_GROUPS * FNET_GROUP_CH

SGU_GROUPS = 4
SGU_GROUP_CH = 128
SGU_W = SGU_GROUPS * SGU_GROUP_CH
SGU_CHUNK = 128

EVEN_IN_SIZES = (GLA_QK_W, GLA_QK_W, GLA_V_W, 2 * GLA_GATE_RANK, GLA_V_W,
                 MLA_Q_RANK, MLA_KV_RANK, MLA_ROPE, MLA_V_W)
ODD_IN_SIZES = (FNET_W, FNET_W, SGU_W, SGU_W, SGU_W)
EVEN_OUT_IN = GLA_V_W + MLA_V_W
ODD_OUT_IN = FNET_W + SGU_W


def split_cols(z, sizes):
    idx = np.cumsum(sizes)[:-1].tolist()
    return jnp.split(z, idx, axis=-1)

def layer_norm_2(x, g=None, b=None):
    xf = x.astype(jnp.float32)
    xc = xf - jnp.mean(xf, -1, keepdims=True)
    y = xc * lax.rsqrt(jnp.mean(xc * xc, -1, keepdims=True) + LN_EPS)
    if g is not None:
        y = y * g.astype(jnp.float32) + b.astype(jnp.float32)
    return y.astype(x.dtype)

def rms_norm_2(x, g):
    xf = x.astype(jnp.float32)
    y = xf * lax.rsqrt(jnp.mean(xf * xf, -1, keepdims=True) + LN_EPS)
    return (y * g.astype(jnp.float32)).astype(x.dtype)

def ada_mod(cond, w, b):
    m = jnp.dot(jax.nn.silu(cond), w) + b
    return jnp.split(m, 3, axis=-1)

def modulate(x, shift, scale):
    return layer_norm_2(x) * (1 + scale[..., None, :]) + shift[..., None, :]

def axial_rope_angles(n):
    rows = n // GRID_W
    row = jnp.repeat(jnp.arange(rows, dtype=jnp.float32), GRID_W)
    col = (jnp.arange(n) % GRID_W).astype(jnp.float32)
    n_freq = MLA_ROPE // 4
    inv = ROPE_BASE ** (-jnp.arange(n_freq, dtype=jnp.float32) / n_freq)
    ang = jnp.concatenate([row[:, None] * inv, col[:, None] * inv], -1)
    return jnp.cos(ang), jnp.sin(ang)

def apply_rope(x, cos, sin):
    xf = x.astype(jnp.float32)
    x1, x2 = jnp.split(xf, 2, axis=-1)
    return jnp.concatenate([x1 * cos - x2 * sin, x1 * sin + x2 * cos], -1).astype(x.dtype)

def gla_q(q):
    B, n, _ = q.shape
    return q.astype(jnp.float32).reshape(B, n, GLA_HEADS, GLA_DK) * GLA_DK ** -0.5

def gla_kvg(k, v, lr, w2, b):
    B, n, _ = k.shape
    heads = lambda a, d: a.astype(jnp.float32).reshape(B, n, GLA_HEADS, d)
    lr_dirs = jnp.split(lr.astype(jnp.float32), 2, axis=-1)
    g = tuple(
        heads(jax.nn.log_sigmoid(jnp.einsum('bnr,re->bne', lr_dirs[d], w2[d].astype(jnp.float32))
                                 + b[d].astype(jnp.float32)) / GLA_TAU, GLA_DK)
        for d in range(2))
    return heads(k, GLA_DK), heads(v, GLA_DV), g

def gla_chunk_scan(q, k, v, g, s0):
    B, n, H, _ = q.shape
    nc = n // GLA_CHUNK
    chunk = lambda a: a.reshape(B, nc, GLA_CHUNK, H, a.shape[-1])
    q, k, v, g = chunk(q), chunk(k), chunk(v), chunk(g)
    b = jnp.cumsum(g, axis=2)
    b_mid = b[:, :, GLA_CHUNK // 2 - 1:GLA_CHUNK // 2]
    b_end = b[:, :, -1:]
    att = jnp.einsum('bcthk,bcshk->bchts', q * jnp.exp(b - b_mid), k * jnp.exp(b_mid - b))
    tri = jnp.tril(jnp.ones((GLA_CHUNK, GLA_CHUNK), dtype=bool))
    o = jnp.einsum('bchts,bcshv->bcthv', jnp.where(tri, att, 0.0), v)
    ds = jnp.einsum('bcshk,bcshv->bchkv', k * jnp.exp(b_end - b), v)
    decay = jnp.exp(b_end[:, :, 0])

    def step(s, inp):
        d, dsc = inp
        return d[..., None] * s + dsc, s

    s_last, s_start = lax.scan(step, s0, (jnp.moveaxis(decay, 1, 0), jnp.moveaxis(ds, 1, 0)))
    o = o + jnp.einsum('bcthk,cbhkv->bcthv', q * jnp.exp(b), s_start)
    return o.reshape(B, n, H, v.shape[-1]), s_last

def gla_final_state(k, v, g):
    bc = jnp.cumsum(g, axis=1)
    return jnp.einsum('bshk,bshv->bhkv', k * jnp.exp(bc[:, -1:] - bc), v)

def gla_bidir(q_l, k_l, v_l, g_l, k_c, v_c, g_c, q_c):
    B, _, H, _ = k_c.shape
    ident = lambda a: a
    rev = lambda a: a[:, ::-1]
    o_l, o_c = 0.0, 0.0
    for d, order in ((0, ident), (1, rev)):
        if q_c is None:
            s_c = gla_final_state(order(k_c), order(v_c), order(g_c[d]))
        else:
            s0 = jnp.zeros((B, H, GLA_DK, GLA_DV), jnp.float32)
            oc, s_c = gla_chunk_scan(order(q_c), order(k_c), order(v_c), order(g_c[d]), s0)
            o_c = o_c + order(oc)
        ol, _ = gla_chunk_scan(order(q_l), order(k_l), order(v_l), order(g_l[d]), s_c)
        o_l = o_l + order(ol)
    return o_l, (o_c if q_c is not None else None)

def mla_q(cq, q_norm_g, w_uq, rope):
    B, n, _ = cq.shape
    q = jnp.einsum('bnr,re->bne', rms_norm_2(cq, q_norm_g), w_uq).reshape(B, n, MLA_HEADS, MLA_NOPE + MLA_ROPE)
    q_nope, q_rope = q[..., :MLA_NOPE], q[..., MLA_NOPE:]
    if rope is not None:
        q_rope = apply_rope(q_rope, rope[0][:, None, :], rope[1][:, None, :])
    return q_nope, q_rope

def mla_kv(ckv, kr, kv_norm_g, w_ukv, rope):
    B, n, _ = ckv.shape
    kv = jnp.einsum('bnr,re->bne', rms_norm_2(ckv, kv_norm_g), w_ukv).reshape(B, n, MLA_HEADS, MLA_NOPE + MLA_V)
    if rope is not None:
        kr = apply_rope(kr, rope[0], rope[1])
    return kv[..., :MLA_NOPE], kr, kv[..., MLA_NOPE:]

def mla_attend(q_nope, q_rope, k_nope, k_rope, v):
    s = (jnp.einsum('bqhd,bkhd->bhqk', q_nope, k_nope, preferred_element_type=jnp.float32)
         + jnp.einsum('bqhr,bkr->bhqk', q_rope, k_rope, preferred_element_type=jnp.float32)) * MLA_SCALE
    p = jax.nn.softmax(s, axis=-1).astype(v.dtype)
    return jnp.einsum('bhqk,bkhd->bqhd', p, v)

def mla_latent_blocks(q_nope, q_rope, k_nope, k_rope, v):
    B, n = q_nope.shape[:2]
    nb = n // Q_BLOCK
    blocks = lambda a: jnp.moveaxis(a.reshape(B, nb, Q_BLOCK, *a.shape[2:]), 1, 0)
    o = lax.map(lambda qs: mla_attend(qs[0], qs[1], k_nope, k_rope, v), (blocks(q_nope), blocks(q_rope)))
    return jnp.moveaxis(o, 0, 1).reshape(B, n, MLA_V_W)

def even_mixer(h_lat, h_ctx, need_ctx_out, rope, w_in, gla_w2, gla_b, gla_norm_g,
               q_norm_g, w_uq, kv_norm_g, w_ukv, w_out):
    B, n, _ = h_lat.shape
    L = h_ctx.shape[1]
    proj = lambda h: split_cols(jnp.einsum('bnd,de->bne', h, w_in), EVEN_IN_SIZES)
    gq_l, gk_l, gv_l, glr_l, gg_l, cq_l, ckv_l, kr_l, mg_l = proj(h_lat)
    gq_c, gk_c, gv_c, glr_c, gg_c, cq_c, ckv_c, kr_c, mg_c = proj(h_ctx)

    k_l, v_l, g_l = gla_kvg(gk_l, gv_l, glr_l, gla_w2, gla_b)
    k_c, v_c, g_c = gla_kvg(gk_c, gv_c, glr_c, gla_w2, gla_b)
    o_gl, o_gc = gla_bidir(gla_q(gq_l), k_l, v_l, g_l, k_c, v_c, g_c,
                           gla_q(gq_c) if need_ctx_out else None)
    y_gla = rms_norm_2(o_gl, gla_norm_g).reshape(B, n, GLA_V_W).astype(h_lat.dtype) * jax.nn.silu(gg_l)

    kn_c, krot_c, vm_c = mla_kv(ckv_c, kr_c, kv_norm_g, w_ukv, None)
    kn_l, krot_l, vm_l = mla_kv(ckv_l, kr_l, kv_norm_g, w_ukv, rope)
    qn_l, qr_l = mla_q(cq_l, q_norm_g, w_uq, rope)
    o_ml = mla_latent_blocks(qn_l, qr_l,
                             jnp.concatenate([kn_c, kn_l], 1),
                             jnp.concatenate([krot_c, krot_l], 1),
                             jnp.concatenate([vm_c, vm_l], 1))
    y_mla = o_ml * jax.nn.silu(mg_l)
    y_lat = jnp.einsum('bne,ed->bnd', jnp.concatenate([y_gla, y_mla], -1), w_out)

    y_ctx = None
    if need_ctx_out:
        yg_c = rms_norm_2(o_gc, gla_norm_g).reshape(B, L, GLA_V_W).astype(h_ctx.dtype) * jax.nn.silu(gg_c)
        qn_c, qr_c = mla_q(cq_c, q_norm_g, w_uq, None)
        ym_c = mla_attend(qn_c, qr_c, kn_c, krot_c, vm_c).reshape(B, L, MLA_V_W) * jax.nn.silu(mg_c)
        y_ctx = jnp.einsum('bne,ed->bnd', jnp.concatenate([yg_c, ym_c], -1), w_out)
    return y_lat, y_ctx

def odd_mixer(h, w_in, sgu_w, sgu_b, w_out):
    B, n, _ = h.shape
    f, f_gate, u, v, s_gate = split_cols(jnp.einsum('bnd,de->bne', h, w_in), ODD_IN_SIZES)
    fg = f.astype(jnp.float32).reshape(B, n, FNET_GROUPS, FNET_GROUP_CH)
    fr = jnp.fft.fft2(fg, axes=(1, 3), norm='ortho').real.reshape(B, n, FNET_W).astype(h.dtype)
    y_f = fr * jax.nn.silu(f_gate)
    u = jax.nn.gelu(u, approximate=False)
    vg = layer_norm_2(jax.nn.gelu(v, approximate=False).reshape(B, n // SGU_CHUNK, SGU_CHUNK, SGU_GROUPS, SGU_GROUP_CH))
    sv = jnp.einsum('gts,bcsgd->bctgd', sgu_w, vg) + sgu_b.T[:, :, None]
    y_s = u * sv.reshape(B, n, SGU_W) * jax.nn.silu(s_gate)
    return jnp.einsum('bne,ed->bnd', jnp.concatenate([y_f, y_s], -1), w_out)

def second_inputs(seed: int = 0) -> dict:
    key = jax.random.key(seed)
    ks = iter(jax.random.split(key, 24))
    nrm = lambda shape, scale: jax.random.normal(next(ks), shape, jnp.float32) * scale
    D = D_MODEL
    return {
        "x": nrm((BATCH, SEQ, D), 1.0),
        "c": nrm((BATCH, D), 1.0),
        "ctx": nrm((BATCH, CTX_LEN, D), 1.0),
        "c_ctx": nrm((D,), 1.0),
        "ada_w": nrm((DEPTH_2, D, 3 * D), D ** -0.5),
        "ada_b": nrm((DEPTH_2, 3 * D), 0.02),
        "post_ln_g": 1.0 + nrm((DEPTH_2, D), 0.02),
        "post_ln_b": nrm((DEPTH_2, D), 0.02),
        "even_w_in": nrm((N_EVEN, D, sum(EVEN_IN_SIZES)), D ** -0.5),
        "gla_w2": nrm((N_EVEN, 2, GLA_GATE_RANK, GLA_QK_W), GLA_GATE_RANK ** -0.5),
        "gla_b": nrm((N_EVEN, 2, GLA_QK_W), 0.1),
        "gla_norm_g": 1.0 + nrm((N_EVEN, GLA_DV), 0.02),
        "mla_q_norm_g": 1.0 + nrm((N_EVEN, MLA_Q_RANK), 0.02),
        "mla_w_uq": nrm((N_EVEN, MLA_Q_RANK, MLA_HEADS * (MLA_NOPE + MLA_ROPE)), MLA_Q_RANK ** -0.5),
        "mla_kv_norm_g": 1.0 + nrm((N_EVEN, MLA_KV_RANK), 0.02),
        "mla_w_ukv": nrm((N_EVEN, MLA_KV_RANK, MLA_HEADS * (MLA_NOPE + MLA_V)), MLA_KV_RANK ** -0.5),
        "even_w_out": nrm((N_EVEN, EVEN_OUT_IN, D), EVEN_OUT_IN ** -0.5 * DEEPNORM_BETA),
        "odd_w_in": nrm((N_ODD, D, sum(ODD_IN_SIZES)), D ** -0.5),
        "sgu_w": nrm((N_ODD, SGU_GROUPS, SGU_CHUNK, SGU_CHUNK), SGU_CHUNK ** -0.5),
        "sgu_b": 1.0 + nrm((N_ODD, SGU_GROUPS, SGU_CHUNK), 0.1),
        "odd_w_out": nrm((N_ODD, ODD_OUT_IN, D), ODD_OUT_IN ** -0.5 * DEEPNORM_BETA),
    }

def second_block(x, c, ctx, c_ctx, ada_w, ada_b, post_ln_g, post_ln_b, even_w_in, gla_w2, gla_b, gla_norm_g,
              mla_q_norm_g, mla_w_uq, mla_kv_norm_g, mla_w_ukv, even_w_out, odd_w_in, sgu_w, sgu_b, odd_w_out):
    rope = axial_rope_angles(x.shape[1])
    for l in range(DEPTH_2):
        need_ctx_out = any(j % 2 == 0 for j in range(l + 1, DEPTH_2))
        i = l // 2
        shift, scale, gate = ada_mod(c, ada_w[l], ada_b[l])
        h_lat = modulate(x, shift, scale)
        if l % 2 == 0 or need_ctx_out:
            shift_c, scale_c, gate_c = ada_mod(c_ctx, ada_w[l], ada_b[l])
            h_ctx = modulate(ctx, shift_c, scale_c)
        if l % 2 == 0:
            y_lat, y_ctx = even_mixer(h_lat, h_ctx, need_ctx_out, rope, even_w_in[i], gla_w2[i], gla_b[i],
                                      gla_norm_g[i], mla_q_norm_g[i], mla_w_uq[i], mla_kv_norm_g[i],
                                      mla_w_ukv[i], even_w_out[i])
        else:
            y_lat = odd_mixer(h_lat, odd_w_in[i], sgu_w[i], sgu_b[i], odd_w_out[i])
            y_ctx = odd_mixer(h_ctx, odd_w_in[i], sgu_w[i], sgu_b[i], odd_w_out[i]) if need_ctx_out else None
        x = layer_norm_2(DEEPNORM_ALPHA * x + gate[:, None, :] * y_lat, post_ln_g[l], post_ln_b[l])
        if need_ctx_out:
            ctx = layer_norm_2(DEEPNORM_ALPHA * ctx + gate_c[None, :] * y_ctx, post_ln_g[l], post_ln_b[l])
    return x


def setup_inputs(seed=0):
    out = dict(first_inputs(seed))
    for name, value in second_inputs(seed + 1).items():
        if name != "x":
            out[name + "_2"] = value
    return out


def reference(
    x, norm1_g, w_in, q_norm_g, k_norm_g, lru_conv_w, lru_conv_b, lru_wa, lru_ba, lru_wx,
    lru_bx, lru_lambda, conf_dw_w, conf_dw_b, conf_ln_g, conf_ln_b, conf_pw_w, conf_pw_b,
    out_norm_g, w_out, norm2_g, router_coarse, router_fine, exp_w_gate, exp_w_up, exp_w_down,
    c_2, ctx_2, c_ctx_2, ada_w_2, ada_b_2, post_ln_g_2, post_ln_b_2, even_w_in_2, gla_w2_2,
    gla_b_2, gla_norm_g_2, mla_q_norm_g_2, mla_w_uq_2, mla_kv_norm_g_2, mla_w_ukv_2,
    even_w_out_2, odd_w_in_2, sgu_w_2, sgu_b_2, odd_w_out_2,
):
    x = first_block(
        x, norm1_g, w_in, q_norm_g, k_norm_g, lru_conv_w, lru_conv_b, lru_wa, lru_ba, lru_wx,
        lru_bx, lru_lambda, conf_dw_w, conf_dw_b, conf_ln_g, conf_ln_b, conf_pw_w, conf_pw_b,
        out_norm_g, w_out, norm2_g, router_coarse, router_fine, exp_w_gate, exp_w_up,
        exp_w_down,
    )
    return second_block(
        x, c_2, ctx_2, c_ctx_2, ada_w_2, ada_b_2, post_ln_g_2, post_ln_b_2, even_w_in_2,
        gla_w2_2, gla_b_2, gla_norm_g_2, mla_q_norm_g_2, mla_w_uq_2, mla_kv_norm_g_2,
        mla_w_ukv_2, even_w_out_2, odd_w_in_2, sgu_w_2, sgu_b_2, odd_w_out_2,
    )


_drawn_inputs = setup_inputs


def setup_inputs(seed=0):
    import zlib

    import numpy as np

    out = dict(_drawn_inputs(seed))
    spreads = {}
    factors = {'k_norm_g': 2.785,
     'lru_ba': 8.0,
     'lru_bx': 6.201,
     'conf_ln_b': 4.255,
     'conf_pw_b': 2.903,
     'ctx_2': 8.0,
     'c_ctx_2': 4.153,
     'ada_b_2': 5.148,
     'gla_b_2': 8.0,
     'gla_norm_g_2': 8.0,
     'mla_q_norm_g_2': 8.0,
     'mla_w_uq_2': 6.905,
     'mla_kv_norm_g_2': 8.0,
     'sgu_b_2': 4.841}
    for name, (base, spread) in spreads.items():
        noise = np.random.default_rng([zlib.crc32(name.encode()), seed]).standard_normal(out[name].shape)
        drawn = base * np.exp(spread * noise) if base else spread * noise
        out[name] = jnp.asarray(drawn.astype(out[name].dtype))
    for name, factor in factors.items():
        out[name] = (out[name] * factor).astype(out[name].dtype)
    return out
```

```python
from contextlib import ExitStack

import concourse.bass as bass
from concourse import mybir

F32 = mybir.dt.float32
I32 = mybir.dt.int32
U32 = mybir.dt.uint32
ALU = mybir.AluOpType
ACT = mybir.ActivationFunctionType
AX = mybir.AxisListType.X
ADD, SUB, MUL, MAX, MIN, POW = ALU.add, ALU.subtract, ALU.mult, ALU.max, ALU.min, ALU.pow
EPS = 1e-6


class Mark:

    def __init__(self, sem):
        self.sem, self.needed, self.value = sem, False, 0


class Landed:

    def __init__(self, sem, value):
        self.sem, self.value = sem, value


def marks(waits):
    if isinstance(waits, (list, tuple)):
        return [m for w in waits for m in marks(w)]
    return [] if waits is None else [waits]


class Lane:

    def __init__(self, nc, name, sem, sem_if):
        self.nc, self.name, self.sems, self.inside = nc, name, (sem, sem_if), False
        self.items = []

    def __call__(self, fn, *waits):
        mark = Mark(self.sems[self.inside])
        flat = marks(waits)
        for w in flat:
            if isinstance(w, Mark):
                w.needed = True
        self.items.append((fn, flat, mark))
        return mark

    def count(self):
        n = {}
        for _, _, mark in self.items:
            if mark.needed:
                n[id(mark.sem)] = mark.value = n.get(id(mark.sem), 0) + 1

    def when(self, flag, *waits):
        self(("when", flag), *waits)
        self.inside = True

    def always(self):
        self(("always", None))
        self.inside = False

    def emit(self, eng):
        seen = {}
        for fn, waits, mark in self.items:
            if isinstance(fn, tuple) and fn[0] == "always":
                branch.__exit__(None, None, None)
                seen = before
                continue
            for w in waits:
                if seen.get(id(w.sem), 0) < w.value:
                    seen[id(w.sem)] = w.value
                    eng.wait_ge(w.sem, w.value)
            if isinstance(fn, tuple):
                branch = eng.If(eng.value_load(fn[1], min_val=0, max_val=15) > 0)
                branch.__enter__()
                before = dict(seen)
                continue
            ins = fn(eng)
            if mark.needed:
                ins.then_inc(mark.sem, 1)


class Load:

    def __init__(self, sem):
        self.sem, self.n = sem, 0

    def __call__(self, lane, out, in_, *waits, **kw):
        self.n += 16
        lane(lambda e: e.dma_start(out, in_, **kw).then_inc(self.sem, 16), *waits)
        return Landed(self.sem, self.n)


class Banks:

    def __init__(self, banks, order):
        self.banks, self.order, self.at, self.free = banks, order, 0, {}

    def take(self):
        b = self.order[self.at % len(self.order)]
        self.at += 1
        return b, self.banks[b], self.free.get(b)

T = 1024
NT = 8
D = 1024
CAP = 128
NEXP = 32
NOV = 15
NBLK = NEXP + NOV
K4 = 256


def constants():
    import numpy as np
    p = np.arange(128)
    s, t = p[:, None], p[None, :]
    same = (s // 64) == (t // 64)
    parts = {
        "ident": s == t, "ones": s + t >= 0, "bd64": same, "ntri": -1.0 * (s >= t), "nones": -1.0 * (s + t >= 0),
        "sltu": s < t, "glaf": same & (s <= t), "glar": same & (s >= t),
    }
    ang = np.arange(128) * 2.0 * np.pi / 128
    c2 = np.arange(128)[:, None] * np.arange(128)[None, :] % 128
    parts["perm"] = (s // 32 == t // 32) & (s % 32 == (t + 16) % 32)
    parts["iota"] = t + 0.0 * s
    parts["tok"] = s + 128.0 * np.arange(8)[None, :]
    parts["eidx"] = 128.0 * t[:, :32] + 0.0 * s
    parts["dftc"] = np.concatenate([np.cos(ang)[c2], np.sin(ang)[c2]], 1)
    inv = np.float32(10000.0) ** (-np.arange(8, dtype=np.float32) / 8)
    n = np.arange(T)
    a = np.concatenate([(n // 64).astype(np.float32)[:, None] * inv, (n % 64).astype(np.float32)[:, None] * inv], 1)
    a = a.astype(np.float32)
    cos, sin = np.cos(a).T, np.sin(a).T
    rope_c = np.tile(np.concatenate([cos, cos]), (4, 1))
    rope_s = np.tile(np.concatenate([-sin, sin]), (4, 1))
    flat = []
    for v in parts.values():
        flat.append(v.astype(np.float32))
    angn = np.arange(T) * 2.0 * np.pi / T
    kn = np.arange(T)[:, None] * np.arange(T)[None, :] % T
    sc = 1.0 / np.sqrt(T * 128.0)
    cn = np.stack([np.cos(angn)[kn] * sc, -np.sin(angn)[kn] * sc])
    return {
        "k_small": np.ascontiguousarray(np.concatenate(flat, 1)),
        "k_rope": np.stack([rope_c, rope_s]).astype(np.float32),
        "k_dft": cn.astype(np.float32),
    }


def build(nc, A, out):
    constants_at = {}
    at = 0
    for name, n in (("ident", 128), ("ones", 128), ("bd64", 128), ("ntri", 128), ("nones", 128),
                    ("sltu", 128), ("glaf", 128), ("glar", 128), ("perm", 128), ("iota", 128), ("tok", 8), ("eidx", 32),
                    ("dftc", 256)):
        constants_at[name] = (at, n)
        at += n
    NC = at
    ctx = ExitStack()
    with ctx:
        MEM = ctx.enter_context(nc.sbuf_tensor("mem", [128, 401 * K4 // 2], F32))
        CS = ctx.enter_context(nc.sbuf_tensor("cst", [128, NC - 256], F32))
        SM = ctx.enter_context(nc.sbuf_tensor("small", [128, 540], F32))
        PSM = ctx.enter_context(nc.psum_tensor("psm", [128, 8, 512], F32))
        banks = [PSM[:, i, :] for i in range(8)]
        nsem = [0]

        def sem(name=None):
            nsem[0] += 1
            return ctx.enter_context(nc.semaphore(name or f"s{nsem[0]}"))

        SY = Lane(nc, "sync", sem("sy"), sem("syi"))
        PE = Lane(nc, "tensor", sem("pe"), sem("pei"))
        AC = Lane(nc, "scalar", sem("ac"), sem("aci"))
        VE = Lane(nc, "vector", sem("ve"), sem("vei"))
        GP = Lane(nc, "gpsimd", sem("gp"), sem("gpi"))
        lanes = [SY, PE, AC, VE, GP]
        stores = []

        def mem(kb, shape, dt=F32, p=128):
            n = 1
            for s in shape:
                n *= s
            o = round(kb * K4)
            ap = MEM[0:p, o:o + n]
            if len(shape) == 2:
                ap = ap.rearrange("p (a b) -> p a b", a=shape[0])
            if len(shape) == 3:
                ap = ap.rearrange("p (a b c) -> p a b c", a=shape[0], b=shape[1])
            return ap

        def cst(name):
            o, n = constants_at[name]
            return CS[:, o:o + n]

        small_at = [0]

        def small(n, dt=F32):
            o = small_at[0]
            small_at[0] += n
            assert small_at[0] <= 540, small_at
            return SM[:, o:o + n]

        def mm(o, l, r, start, stop, *w):
            return PE(lambda e: e.matmul(o, l, r, start=start, stop=stop, skip_group_check=True), *w)

        def tr(o, i, idn, *w):
            return PE(lambda e: e.transpose(o, i, idn), *w)

        def act(o, i, f, *w, **k):
            return AC(lambda e: e.activation(o, i, f, **k), *w)

        def tt(o, a, b, op, *w, lane=None):
            return (lane or VE)(lambda e: e.tensor_tensor(o, a, b, op), *w)

        def ts(o, a, s1, s2, op0, op1, *w, lane=None):
            if op1 is None:
                return (lane or VE)(lambda e: e.tensor_scalar(o, a, s1, None, op0), *w)
            return (lane or VE)(lambda e: e.tensor_scalar(o, a, s1, s2, op0, op1), *w)

        def stt(o, a, s, b, op0, op1, *w):
            return VE(lambda e: e.scalar_tensor_tensor(o, a, s, b, op0, op1), *w)

        def cp(lane, o, i, *w):
            if lane is AC:
                return act(o, i, ACT.Copy, *w)
            return lane(lambda e: e.tensor_copy(o, i), *w)

        def dma(lane, o, i, *w, load=None, **k):
            return (load or Load(sem()))(lane, o, i, *w, **k)

        epsc = small(1)
        t_eps = VE(lambda e: e.memset(epsc, EPS))

        def rsq(o, ss, n, *w):
            a = act(o, ss, ACT.Ln, *w, t_eps, scale=1.0 / n, bias=epsc[0:o.shape[0], 0:1])
            return act(o, o, ACT.Exp, a, scale=-0.5)

        X = mem(0, [NT, D])
        HT = mem(32, [8, T])
        W0, W1, W2 = 64, 80, 96

        l_c = dma(SY, CS[:, :], A["k_small"][:, 0:NC - 256])
        xs = A["x"][0].rearrange("(t p) d -> p t d", p=128)
        l_x = [dma(SY, X[:, i, :], xs[:, i, :]) for i in range(NT)]

        colL = Load(sem())

        def column(src, n, *w):
            o = small(n)
            return o, dma(GP, o, src, *w, load=colL)

        g1, t_ = column(A["norm1_g"][0].rearrange("(p c) -> p c", c=8), 8)
        gq = small(1)
        gk = small(1)
        for g, nm in ((gq, "q_norm_g"), (gk, "k_norm_g")):
            for h in range(2):
                t_ = dma(GP, g[64 * h:64 * h + 64, :], A[nm][0].rearrange("(p c) -> p c", c=1), load=colL)
        rows = mem(150, [256])
        t_ = dma(GP, rows[0:31, :], A["conf_dw_w"][0], load=colL)
        r = 31
        for nm in ("conf_dw_b", "conf_ln_g", "conf_ln_b", "conf_pw_b"):
            t_ = dma(GP, rows[r:r + 1, :], A[nm], load=colL)
            r += 1
        t_ = dma(GP, rows[35:39, :], A["lru_conv_w"][0], load=colL)
        r = 39
        for nm in ("lru_conv_b", "lru_ba", "lru_bx", "lru_lambda"):
            t_ = dma(GP, rows[r:r + 1, :], A[nm], load=colL)
            r += 1
        t_ = dma(GP, rows[43:47, :], A["out_norm_g"][0].rearrange("(m n) -> m n", m=4), load=colL)
        ct = small(94)
        ctv = ct.rearrange("p (j r) -> p j r", j=2)
        g2, t_ = column(A["norm2_g"][0].rearrange("(p c) -> p c", c=8), 8)
        l_col = t_

        ring = {}

        class Slot:
            def __init__(self, kb):
                self.kb, self.load, self.used = kb, Load(sem()), []

        slots = {}

        def fetch(kb, dst, src, *w, lane=None, n=1):
            if kb not in slots:
                slots[kb] = Slot(kb)
            s = slots[kb]
            m = dma(lane or SY, dst, src, list(s.used), *w, load=s.load)
            return m

        w_in = A["w_in"][0].rearrange("(p c) n -> p c n", c=8)
        PB = Banks(banks, [0, 1, 2, 3, 4, 5, 6, 7])

        def row_stats(t, src, w, eps_n, tag, center):
            pass

        st6 = mem(160, [NT, 2, 6])

        def normed(src, i, dst, rs, nb, w, use):
            return None

        def transposed(srcs, dst_of, evac):
            return None

        def stats(src, n, bn, mv, w):
            a = VE(lambda e: e.bn_stats(bn[:, 0:6], src[:, 0:512]), w)
            b = VE(lambda e: e.bn_stats(bn[:, 6:12], src[:, 512:1024]))
            return VE(lambda e: e.bn_aggr(mv, bn[:, 0:12]), a, b)

        bnb = small(12)
        mv = small(16)
        mvv = mv.rearrange("p (t k) -> p t k", k=2)
        rs8 = small(8)
        nb8 = small(8)
        sq8 = small(8)

        def token_stats(n, get, waits, rms):
            last = None
            for i in range(n):
                last = stats(get(i), 1024, bnb, mvv[:, i, :], [waits[i], last])
            if rms:
                a = tt(sq8[:, 0:n], mvv[:, 0:n, 0], mvv[:, 0:n, 0], MUL, last)
                b = tt(sq8[:, 0:n], sq8[:, 0:n], mvv[:, 0:n, 1], ADD, a)
                c = rsq(rs8[:, 0:n], sq8[:, 0:n], 1, b)
                return c
            c = rsq(rs8[:, 0:n], mvv[:, 0:n, 1], 1, last)
            return stt(nb8[:, 0:n], mvv[:, 0:n, 0], -1.0, rs8[:, 0:n], MUL, MUL, c)

        def channel_major(n, get, tstat, center, tmpkb, dst, scale, shift, w, tok0=0, on_norm=None):
            done = []
            free = [None, None]
            for q in range((n + 3) // 4):
                m = min(4, n - 4 * q)
                tmp = [mem(tmpkb + 4 * j, [D]) for j in range(4)]
                norm = []
                for j in range(m):
                    i = 4 * q + j
                    if center:
                        f = ACT.Identity
                        k = dict(scale=rs8[:, i:i + 1], bias=nb8[:, i:i + 1])
                    else:
                        f, k = ACT.Copy, dict(scale=rs8[:, i:i + 1])
                    if j % 2:
                        if center:
                            norm.append(ts(tmp[j], get(i), rs8[:, i:i + 1], nb8[:, i:i + 1], MUL, ADD, tstat, free[0]))
                        else:
                            norm.append(ts(tmp[j], get(i), rs8[:, i:i + 1], None, MUL, None, tstat, free[0]))
                    else:
                        norm.append(act(tmp[j], get(i), f, tstat, free[0], **k))
                    kept = on_norm(i, tmp[j], norm[-1]) if on_norm else None
                last = None
                for c in range(8):
                    b, ps, fr = PB.take()
                    for j in range(m):
                        last = tr(ps[:, 128 * j:128 * j + 128], tmp[j][:, c::8], cst("ident"), norm[j], fr, w)
                    o = dst[:, c, tok0 + 512 * q:tok0 + 512 * q + 128 * m]
                    src = ps[:, 0:128 * m]
                    if c % 2:
                        if shift is None:
                            d = ts(o, src, scale[:, c:c + 1], None, MUL, None, last)
                        else:
                            d = ts(o, src, scale[:, c:c + 1], shift[:, c:c + 1], MUL, ADD, last)
                    else:
                        kw = dict(scale=scale[:, c:c + 1])
                        if shift is not None:
                            kw["bias"] = shift[:, c:c + 1]
                        d = act(o, src, ACT.Identity if shift is not None else ACT.Copy, last, **kw)
                    PB.free[b] = d
                    done.append(d)
                free[0] = [last, kept]
            return done

        for j in range(2):
            last = tr(banks[7][:, 47 * j:47 * j + 47], rows[0:47, 128 * j:128 * j + 128],
                      cst("ident")[0:47, 0:47], l_c, l_col)
        l_ct = cp(VE, ct, banks[7][:, 0:94], last)
        PB.free[7] = l_ct

        def tap(j, r):
            return ctv[:, j, r:r + 1]

        CDB, CLG, CLB, CPB, LCW, LCB, LBA, LBX, LAM, ONG = 31, 32, 33, 34, 35, 39, 40, 41, 42, 43
        tx = token_stats(NT, lambda i: X[:, i, :], l_x, True)
        hT = channel_major(NT, lambda i: X[:, i, :], tx, False, 112, HT, g1, None, [l_c, l_col, l_ct])

        QK = mem(112, [8, T])
        V = mem(144, [NT, 512])
        XRP = mem(160, [2, 1027])
        XG = mem(168.25, [2, 1024])
        UP = mem(176.25, [2, 1054])
        TB = 184.5

        CSQ = [small(1), small(1)]
        c1 = ts(CSQ[0], gq, 0.125, None, MUL, None, l_col)
        c2 = ts(CSQ[1], gk, 1.0, None, MUL, None, l_col)
        z1 = GP(lambda e: e.memset(XRP[:, :, 0:3], 0.0))
        z2 = GP(lambda e: e.memset(UP[:, :, 0:30], 0.0))

        gw = mem(TB + 12, [4, 128])
        zg = GP(lambda e: e.memset(gw, 0.0))
        gwl = Load(sem())
        for gi, nm in enumerate(("lru_wa", "lru_wx")):
            for n in range(4):
                q = 64 * (n % 2)
                l_gw = dma(GP, gw[q:q + 64, 2 * gi + n // 2, q:q + 64], A[nm][0][n], zg, load=gwl)

        def w_load(kb, src, *w, cols=512):
            dst = mem(kb, [8, 512])[:, :, 0:cols]
            s = slots.setdefault(kb, Slot(kb))
            m = dma(SY, dst, src, list(s.used), *w, load=s.load)
            s.used = []
            return dst, m

        def proj_cm(w, lw, col, src, half, hw, m=128, n=512, tok=None):
            b, ps, fr = PB.take()
            t0 = 512 * half if tok is None else tok
            for c in range(8):
                last = mm(ps[0:m, 0:n], w[:, c, col:col + m], src[:, c, t0:t0 + n], c == 0, c == 7, fr, lw, hw)
            return b, ps, last

        w_ld = {}
        order = [(3, W0), (4, W1), (0, W2), (1, W0), (2, W1)]
        for ch, kb in order[:2]:
            w_ld[ch] = w_load(kb, w_in[:, :, 512 * ch:512 * ch + 512])
        sigb = [mem(TB, [512]), mem(TB + 2, [512])]
        ybp = []
        lru_in, xg_in, up_in = [], [], []
        w, lw = w_ld[3]
        for j in range(4):
            for half in range(2):
                b, ps, last = proj_cm(w, lw, 128 * j, HT, half, hT)
                t0 = 512 * half
                if j < 2:
                    d = cp(VE, XRP[:, j, 3 + t0:3 + t0 + 512], ps[:, :], last)
                    lru_in.append(d)
                else:
                    d = act(XG[:, j - 2, t0:t0 + 512], ps[:, :], ACT.Gelu_apprx_tanh, last)
                    xg_in.append(d)
                PB.free[b] = d
        slots[W0].used = [last]
        w_ld[0] = w_load(W0, w_in[:, :, 0:512])
        w, lw = w_ld[4]
        sfree = [None, None]
        k = 0
        for j in range(2):
            for half in range(2):
                t0 = 512 * half
                bg, psg, lg = proj_cm(w, lw, 256 + 128 * j, HT, half, hT)
                sg = act(sigb[k % 2], psg[:, :], ACT.Sigmoid, lg, sfree[k % 2])
                PB.free[bg] = sg
                bv, psv, lv = proj_cm(w, lw, 128 * j, HT, half, hT)
                d = tt(UP[:, j, 30 + t0:30 + t0 + 512], psv[:, :], sigb[k % 2], MUL, lv, sg)
                PB.free[bv] = sfree[k % 2] = d
                up_in.append(d)
                k += 1
        slots[W1].used = [lv]
        w_ld[1] = w_load(W1, w_in[:, :, 512:1024])
        XR0 = mem(160, [1024])
        YB = XG
        YC = mem(176.25, [2, 1024])
        br = {}

        def lru():
            la8, la8n, lt1, lt2 = small(2), small(2), small(2), small(2)
            lamc = ctv[:, :, LAM]
            a = act(lt1, lamc, ACT.Abs, l_ct)
            a = act(lt1, lt1, ACT.Exp, a, scale=-1.0)
            a = act(lt1, lt1, ACT.Ln, a, bias=1.0)
            b = ts(lt2, lamc, -1.0, 0.0, MUL, MAX, l_ct)
            a = tt(lt1, lt1, lt2, ADD, a, b)
            t_lan = ts(la8n, lt1, 8.0, None, MUL, None, a)
            t_la = ts(la8, lt1, -8.0, None, MUL, None, a)
            LX = [mem(W2, [1024]), mem(W2 + 4, [1024])]
            LA, LI, LTM = mem(W2 + 8, [1024]), mem(W2 + 12, [1024]), mem(TB + 14, [512])
            xconv = []
            for j in range(2):
                d = ts(LX[j], XRP[:, j, 3:1027], tap(j, LCW + 3), tap(j, LCB), MUL, ADD, lru_in, z1)
                for i in range(3):
                    d = stt(LX[j], XRP[:, j, i:i + 1024], tap(j, LCW + i), LX[j], MUL, ADD, d)
                xconv.append(d)
                yield
            lrf = gf = None
            done = []
            for j in range(2):
                LT = XRP[:, j, 0:1024]
                ends = []
                for half in range(2):
                    s0 = slice(512 * half, 512 * half + 512)
                    b1, ps1, f1 = PB.take()
                    m1 = mm(ps1[:, :], gw[:, j, :], LX[j][:, s0], True, True, l_gw, xconv[j], f1)
                    r = act(LA[:, s0], ps1[:, :], ACT.Sigmoid, m1, lrf, bias=tap(j, LBA))
                    PB.free[b1] = r
                    b2, ps2, f2 = PB.take()
                    m2 = mm(ps2[:, :], gw[:, 2 + j, :], LX[j][:, s0], True, True, f2)
                    g = act(LI[:, s0], ps2[:, :], ACT.Sigmoid, m2, lrf, bias=tap(j, LBX))
                    PB.free[b2] = g
                    ends += [r, g]
                t1 = act(LT, LA, ACT.Tanh, ends, t_lan, xconv, scale=la8n[:, j:j + 1])
                t2 = act(LA, LA, ACT.Exp, t1, t_la, scale=la8[:, j:j + 1])
                yield
                for half in range(2):
                    s0 = slice(512 * half, 512 * half + 512)
                    d = ts(LTM, LT[:, s0], 1.0, None, ADD, None, t1, gf)
                    d = VE(lambda e: e.reciprocal(LTM, LTM), d)
                    gf = d = stt(LT[:, s0], LT[:, s0], 2.0, LTM, MUL, MUL, d)
                    yield
                d = act(LT, LT, ACT.Sqrt, d)
                yield
                d = tt(LT, LT, LI, MUL, d)
                d = tt(LT, LT, LX[j], MUL, d)
                yield
                d = VE(lambda e, LT=LT: e.tensor_tensor_scan(LI, LA, LT, 0.0, MUL, ADD), d, t2)
                lrf = tt(YB[:, j, :], LI, XG[:, j, :], MUL, d, xg_in)
                done.append(lrf)
                yield
            br["yb"] = done

        def conformer():
            CA, CQ, CR = mem(W2, [2, 1024]), mem(W2 + 8, [2, 512]), mem(W2 + 12, [512])
            pw = mem(W2 + 14, [2, 256])
            l_pw = dma(GP, pw, A["conf_pw_w"][0].rearrange("(j p) e -> p j e", p=128), br["yb"])
            cc = []
            for j in range(2):
                o = CA[:, j, :]
                d = ts(o, UP[:, j, 30:1054], tap(j, 30), tap(j, CDB), MUL, ADD, up_in, z2, br["yb"])
                for i in range(30):
                    d = stt(o, UP[:, j, i:i + 1024], tap(j, i), o, MUL, ADD, d)
                    if i % 5 == 4:
                        yield
                cc.append(d)
            cf = None
            done = []
            for half in range(2):
                s0 = slice(512 * half, 512 * half + 512)
                b1, ps1, f1 = PB.take()
                mm(ps1[:, :], cst("ones"), CA[:, 0, s0], True, False, cc, f1)
                m1 = mm(ps1[:, :], cst("ones"), CA[:, 1, s0], False, True)
                xc = [stt(CA[:, j, s0], ps1[:, :], -1.0 / 256, CA[:, j, s0], MUL, ADD, m1) for j in range(2)]
                PB.free[b1] = xc[-1]
                sq = [act(CQ[:, j, :], CA[:, j, s0], ACT.Square, xc[j], cf) for j in range(2)]
                yield
                b2, ps2, f2 = PB.take()
                mm(ps2[:, :], cst("ones"), CQ[:, 0, :], True, False, sq[0], f2)
                m2 = mm(ps2[:, :], cst("ones"), CQ[:, 1, :], False, True, sq[1])
                r = rsq(CR, ps2[:, :], 256, m2, cf)
                PB.free[b2] = r
                yield
                sl = []
                for j in range(2):
                    d = tt(CA[:, j, s0], CA[:, j, s0], CR, MUL, r)
                    sl.append(act(CA[:, j, s0], CA[:, j, s0], ACT.Silu, d, scale=tap(j, CLG), bias=tap(j, CLB)))
                cf = [d, m2]
                yield
                for j in range(2):
                    b3, ps3, f3 = PB.take()
                    mm(ps3[:, :], pw[:, 0, 128 * j:128 * j + 128], CA[:, 0, s0], True, False, sl, l_pw, f3)
                    m3 = mm(ps3[:, :], pw[:, 1, 128 * j:128 * j + 128], CA[:, 1, s0], False, True)
                    d = act(YC[:, j, s0], ps3[:, :], ACT.Identity, m3, cc, bias=tap(j, CPB))
                    PB.free[b3] = d
                    done.append(d)
                yield
            br["yc"] = done
            br["end"] = m3

        def both():
            yield from lru()
            yield from conformer()

        branches = both()

        def branch_step(n=1):
            for _ in range(n):
                next(branches, None)

        sqb = [mem(TB + 4, [512]), mem(TB + 6, [512])]
        rb = [mem(TB + 8, [512]), mem(TB + 10, [512])]
        qk_done = {}
        sqf, rf = [None, None], [None, None]
        pend = None
        k = 0

        def qk_tail(p):
            e, half, b, ps, sq, k = p
            b2, ps2, fr2 = PB.take()
            m2 = mm(ps2[:, :], cst("bd64"), sqb[k % 2], True, True, sq, fr2)
            sqf[k % 2] = m2
            r = rsq(rb[k % 2], ps2[:, :], 64, m2, rf[k % 2])
            PB.free[b2] = r
            d = stt(QK[:, e, 512 * half:512 * half + 512], ps[:, :], CSQ[e // 4][:, 0:1], rb[k % 2], MUL, MUL, r, c1, c2)
            rf[k % 2] = d
            PB.free[b] = d
            qk_done[(e, half)] = d

        for ch in (0, 1):
            w, lw = w_ld[ch]
            for j in range(4):
                for half in range(2):
                    e = 4 * ch + j
                    b, ps, last = proj_cm(w, lw, 128 * j, HT, half, hT)
                    sq = act(sqb[k % 2], ps[:, :], ACT.Square, last, sqf[k % 2])
                    if pend:
                        qk_tail(pend)
                    branch_step(2)
                    pend = (e, half, b, ps, sq, k)
                    k += 1
            slots[(W0, W1)[ch]].used = [last]
            if ch == 0:
                w_ld[2] = w_load(W0, w_in[:, :, 1024:1536])
        qk_tail(pend)
        w, lw = w_ld[2]
        v_done = []
        for i in range(NT):
            b, ps, fr = PB.take()
            for c in range(8):
                last = mm(ps[:, :], HT[:, c, 128 * i:128 * i + 128], w[:, c, :], c == 0, c == 7, fr, lw, hT)
            d = cp(AC, V[:, i, :], ps[:, :], last)
            PB.free[b] = d
            v_done.append(d)
            branch_step(2)
        slots[W0].used = [last]
        branch_step(100)
        yb_done, yc_done = br["yb"], br["yc"]
        ht_free = last
        YT = HT
        PT1 = [mem(TB + 2 * i, [512]) for i in range(2)]
        PSP = [mem(TB + 4 + 2 * i, [512]) for i in range(3)]
        PW_ = [mem(TB + 10 + 2 * i, [512]) for i in range(3)]
        PRS = [mem(160 + 2 * i, [512]) for i in range(4)]
        items = [(hp, qc, kb, h) for hp in range(4) for qc in range(2) for kb in range(4 * qc + 3, -1, -1)
                 for h in (2 * hp, 2 * hp + 1)]
        att_w = [br["end"], yb_done, yc_done, list(qk_done.values())]
        AZ = Banks(banks, [0, 1, 2, 3, 4, 5])
        AZ.free = dict(PB.free)
        z_, sp_, w_, lane_r = {}, {}, {}, {}
        t1f, spf, wf = [att_w] * 2, [att_w] * 3, [att_w] * 3
        rsum = {}
        ya_done = []
        ofree = [PB.free.get(6), PB.free.get(7)]
        rf_ = [att_w] * 4

        def ext(i):
            hp, qc, kb, h = items[i]
            lo = max(0, kb - 4 * qc) * 128
            return hp, qc, kb, h, lo

        def stage_z(i):
            hp, qc, kb, h, lo = ext(i)
            b, ps, fr = AZ.take()
            q0 = 64 * (h % 2)
            m = mm(ps[:, lo:512], QK[q0:q0 + 64, 4 + hp, 128 * kb:128 * kb + 128],
                   QK[q0:q0 + 64, hp, 512 * qc + lo:512 * qc + 512], True, True, fr, att_w if i < 6 else None)
            z_[i] = (b, ps, m)

        def stage_sp(i):
            hp, qc, kb, h, lo = ext(i)
            b, ps, m = z_[i]
            k = i % 2
            t1 = act(PT1[k][:, lo:], ps[:, lo:512], ACT.Abs, m, t1f[k])
            t2 = act(PT1[k][:, lo:], PT1[k][:, lo:], ACT.Exp, t1, scale=-1.0)
            t3 = act(PT1[k][:, lo:], PT1[k][:, lo:], ACT.Ln, t2, bias=1.0)
            j = i % 3
            d = stt(PSP[j][:, lo:], ps[:, lo:512], 0.0, PT1[k][:, lo:], MAX, ADD, t3, spf[j])
            t1f[k] = d
            if kb >= 4 * qc:
                v = PSP[j][:, lo:lo + 128]
                d = GP(lambda e: e.affine_select(out=v, in_=v, compare_op=ALU.is_gt, fill=0.0, base=0,
                                                 pattern=[[1, 128]], channel_multiplier=-1), d)
            sp_[i] = d

        def stage_c(i):
            hp, qc, kb, h, lo = ext(i)
            b, ps, m = z_[i]
            k = i % 3
            top = 4 * qc + 3
            m = mm(ps[:, lo:512], cst("ntri"), PSP[k][:, lo:], False, kb == top, sp_[i])
            rk = 2 * (qc % 2) + h % 2
            R = PRS[rk]
            if kb < top:
                prev = max(0, kb + 1 - 4 * qc) * 128
                m = mm(ps[:, prev:512], cst("nones"), R[:, prev:], False, True, rsum[rk])
            if kb > 0:
                if kb == top:
                    if lo > 0:
                        GP(lambda e: e.memset(R[:, 0:lo], 0.0), rf_[rk])
                    g = cp(GP, R[:, lo:], PSP[k][:, lo:], sp_[i], rf_[rk], m)
                    rsum[rk] = g
                else:
                    g = tt(R[:, lo:], R[:, lo:], PSP[k][:, lo:], ADD, m, sp_[i], rsum[rk], lane=GP)
                    rsum[rk] = g
                spf[k] = [m, g]
            else:
                rf_[rk] = m
                spf[k] = m
            w = act(PW_[k][:, lo:], ps[:, lo:512], ACT.Exp, m, wf[k])
            AZ.free[b] = w
            if kb >= 4 * qc:
                v = PW_[k][:, lo:lo + 128]
                w = GP(lambda e: e.affine_select(out=v, in_=v, compare_op=ALU.is_gt, fill=0.0, base=0,
                                                 pattern=[[1, 128]], channel_multiplier=-1), w)
            w_[i] = w

        def stage_pv(i):
            hp, qc, kb, h, lo = ext(i)
            k = i % 3
            ob = banks[6 + qc % 2]
            q0 = 64 * (h % 2)
            top = 4 * qc + 3
            m = mm(ob[q0:q0 + 64, lo:512], V[:, kb, 64 * h:64 * h + 64], PW_[k][:, lo:], kb == top, kb == 0,
                   w_[i], v_done, ofree[qc % 2] if kb == top else None)
            wf[k] = m
            if kb == 0:
                d = cp(VE, YT[q0:q0 + 64, hp, 512 * qc:512 * qc + 512], ob[q0:q0 + 64, :], m, ht_free)
                ofree[qc % 2] = [ofree[qc % 2], d] if h % 2 else d
                ya_done.append(d)

        zrow = mem(W2 + 12, [512])
        tz0 = GP(lambda e: e.memset(zrow, 0.0), att_w)
        ysl = nc.dram_tensor("ysl", [NBLK * 128, D], F32).ap()
        yzl = Load(sem())
        for b in range(NEXP, NBLK):
            t_yz = dma(SY, ysl[128 * b:128 * b + 128, :].rearrange("p (q n) -> p q n", q=2),
                       zrow.unsqueeze(1).broadcast_to([128, 2, 512]), tz0, load=yzl)
        LAG1, LAG2 = 3, 5
        AC(lambda e: e.preload_act_table_set("natural_log_exp_and_others"))
        n = len(items)
        for s in range(n + LAG2):
            if s < n:
                stage_z(s)
                stage_sp(s)
            if 0 <= s - LAG1 + 1 < n:
                stage_c(s - LAG1 + 1)
            if 0 <= s - LAG2 + 1 < n:
                stage_pv(s - LAG2 + 1)
        for b in range(6):
            PB.free[b] = AZ.free.get(b)
        PB.free[6], PB.free[7] = ofree

        w_o = A["w_out"][0].rearrange("(j p) n -> p j n", p=128)
        WO = mem(W0, [8, 1024])
        l_wo = []
        for q in range(2):
            s = slots[(W0, W1)[q]]
            l_wo.append(dma(SY, WO[:, 4 * q:4 * q + 4, :], w_o[:, 4 * q:4 * q + 4, :], s.used, load=s.load))
            s.used = []
        att_end = ya_done[-1]

        def yt(j):
            return YT[:, j, :] if j < 4 else YB[:, j - 4, :] if j < 6 else YC[:, j - 6, :]

        NSQ = [mem(112 + 2 * i, [512]) for i in range(4)]
        NR = [mem(120, [512]), mem(122, [512])]
        nf, nrf = [None] * 4, [None] * 2
        yn = []
        k = 0
        for half in range(2):
            s0 = slice(512 * half, 512 * half + 512)
            for (j0, j1, dn) in ((4, 6, yb_done), (6, 8, yc_done), (0, 4, ya_done)):
                b, ps, fr = PB.take()
                for j in range(j0, j1):
                    q = act(NSQ[k % 4], yt(j)[:, s0], ACT.Square, dn, att_end, nf[k % 4])
                    last = mm(ps[:, :], cst("ones"), NSQ[k % 4], j == j0, j == j1 - 1, q, fr)
                    nf[k % 4] = last
                    k += 1
                r = rsq(NR[half], ps[:, :], 128 * (j1 - j0), last, nrf[half])
                PB.free[b] = r
                for j in range(j0, j1):
                    d = stt(yt(j)[:, s0], yt(j)[:, s0], ctv[:, j % 2, ONG + j // 2:ONG + j // 2 + 1], NR[half], MUL, MUL, r)
                nrf[half] = d
                yn.append(d)
        x1 = []
        for i in range(NT):
            for q in range(2):
                b, ps, fr = PB.take()
                for j in range(8):
                    last = mm(ps[:, :], yt(j)[:, 128 * i:128 * i + 128], WO[:, j, 512 * q:512 * q + 512],
                              j == 0, j == 7, fr, l_wo, yn[0:3] if i < 4 else yn[3:6])
                d = tt(X[:, i, 512 * q:512 * q + 512], ps[:, :], X[:, i, 512 * q:512 * q + 512], ADD, last, hT)
                PB.free[b] = d
            x1.append(d)
        slots[W0].used = slots[W1].used = [last]
        yt_free = last

        ada_d = nc.dram_tensor("ada_d", [2, 2, 3072], F32).ap()
        cnd = small(16)
        SCND = small(16)
        cl = Load(sem())
        dma(GP, cnd[:, 0:8], A["c_2"][0].rearrange("(p c) -> p c", c=8), load=cl)
        t_cl = dma(GP, cnd[:, 8:16], A["c_ctx_2"].rearrange("(p c) -> p c", c=8), load=cl)
        t_scnd = act(SCND, cnd, ACT.Silu, t_cl)
        sc2 = SCND.rearrange("p (m c) -> p c m", m=2)
        ARW = [mem(192, [512], p=2), mem(194, [512], p=2)]
        ABI = [mem(196, [512], p=2), mem(198, [512], p=2)]
        aw_l = [Load(sem()), Load(sem())]
        ab_l = [Load(sem()), Load(sem())]
        as_l = [Load(sem()), Load(sem())]
        asf, abf = [att_end, att_end], [att_end, att_end]
        t_ada = [None, None]
        ada_w = {}
        ADA_AT = [(W0, W1), (112, 128)]

        def ada_load(n):
            l, ch, k = n // 6, n % 6, n % 2
            kb = ADA_AT[l][k]
            dst, m = w_load(kb, A["ada_w_2"][l].rearrange("(p c) n -> p c n", c=8)[:, :, 512 * ch:512 * ch + 512])
            bi = dma(SY, ABI[k], A["ada_b_2"][l:l + 1, 512 * ch:512 * ch + 512].broadcast_to([2, 512]), abf[k], load=ab_l[k])
            ada_w[n] = (dst, m, bi)

        def ada_chunk(n):
            l, ch, k = n // 6, n % 6, n % 2
            dst, m, bi = ada_w[n]
            b, ps, fr = PB.take()
            for c in range(8):
                last = mm(ps[0:2, :], sc2[:, c, :], dst[:, c, :], c == 0, c == 7, fr, t_scnd, m)
            slots[ADA_AT[l][k]].used = [last]
            d = tt(ARW[k], ps[0:2, :], ABI[k], ADD, last, bi, asf[k])
            PB.free[b] = d
            abf[k] = d
            t_ada[k] = asf[k] = dma(SY, ada_d[l, :, 512 * ch:512 * ch + 512], ARW[k], d, load=as_l[k])


        def ada_chunks(n0, n1):
            for n in range(n0, n1):
                if n % 6 == 0:
                    ada_load(n)
                    ada_load(n + 1)
                ada_chunk(n)
                if n % 6 < 4:
                    ada_load(n + 2)

        h2d = nc.dram_tensor("h2d", [T + 1, D], F32).ap()
        std = nc.dram_tensor("std", [NBLK * 128, 1], I32).ap()
        H2T = mem(128, [8, T])
        WR = mem(33, [8, 36])
        zr = mem(56, [1024], p=1)
        l_wr = Load(sem())
        dma(SY, WR[:, :, 0:4], A["router_coarse"][0].rearrange("(p c) g -> p c g", c=8), yt_free, load=l_wr)
        t_wr = dma(SY, WR[:, :, 4:36], A["router_fine"][0].rearrange("(p c) g -> p c g", c=8), load=l_wr)
        d = VE(lambda e: e.memset(zr, 0.0), yt_free)
        h2_st = Load(sem())
        t_h2 = [dma(AC, h2d[T:T + 1, :], zr, d, load=h2_st)]
        tx = token_stats(NT, lambda i: X[:, i, :], x1, True)

        def keep_row(i, tmp, norm):
            t_h2.append(dma(AC, h2d[128 * i:128 * i + 128, :], tmp, norm, load=h2_st))
            return t_h2[-1]

        h2T = channel_major(NT, lambda i: X[:, i, :], [tx, yn[-1], att_end], False, 112, H2T, g2, None, [], on_norm=keep_row)
        b, ps, fr = PB.take()
        for i in range(NT):
            for c in range(8):
                last = mm(ps[:, 36 * i:36 * i + 36], H2T[:, c, 128 * i:128 * i + 128], WR[:, c, :], c == 0, c == 7,
                          fr, t_wr, h2T)
        lg_end = last
        ada_chunks(0, 4)
        rt_at = [34.5]

        def tmp(*shape):
            n = 1
            for s in shape:
                n *= s
            ap = mem(rt_at[0], list(shape))
            rt_at[0] += n / 256
            return ap

        L = tmp(8, 36)
        d = cp(VE, L, ps[:, 0:288].rearrange("p (a b) -> p a b", a=8), last)
        PB.free[b] = d
        LC, LF = L[:, :, 0:4], L[:, :, 4:36]
        i4 = cst("iota")[:, 0:4].unsqueeze(1).broadcast_to([128, 8, 4])
        i32_ = cst("iota")[:, 0:32].unsqueeze(1).broadcast_to([128, 8, 32])

        def bc(v, n):
            return v.unsqueeze(2).broadcast_to([128, 8, n])

        def red(o, i, op, *w):
            return VE(lambda e: e.tensor_reduce(o, i, AX, op), *w)

        def onehot(o, i, v, n, iota, *w):
            idx = tmp(8)
            a = tt(o, i, bc(v, n), ALU.is_equal, *w)
            a = ts(o, o, -64.0, 64.0, MUL, ADD, a)
            a = tt(o, o, iota, ADD, a)
            a = red(idx, o, MIN, a)
            return tt(o, iota, bc(idx, n), ALU.is_equal, a)

        mc, ec, oc, sc, wg_ = tmp(8), tmp(8, 4), tmp(8, 4), tmp(8), tmp(8)
        a = red(mc, LC, MAX, d)
        b_ = tt(ec, LC, bc(mc, 4), SUB, a)
        b_ = act(ec, ec, ACT.Exp, b_)
        b_ = red(sc, ec, ADD, b_)
        t_wg = VE(lambda e: e.reciprocal(wg_, sc), b_)
        a = onehot(oc, LC, mc, 4, i4, a)
        mask, pen, LM = tmp(8, 32), tmp(8, 32), tmp(8, 32)
        a = cp(VE, mask.rearrange("p a (g e) -> p a g e", g=4), oc.unsqueeze(3).broadcast_to([128, 8, 4, 8]), a)
        a1 = ts(pen, mask, -1.0, 1e30, ADD, MUL, a)
        a = tt(LM, LF, mask, MUL, a)
        a = tt(LM, LM, pen, ADD, a, a1)
        m1, m2, o1, o2 = tmp(8), tmp(8), tmp(8, 32), tmp(8, 32)
        d1 = red(m1, LM, MAX, a)
        a = onehot(o1, LM, m1, 32, i32_, d1)
        a1 = ts(pen, o1, -1e30, None, MUL, None, a)
        a1 = tt(LM, LM, pen, ADD, a1)
        d2 = red(m2, LM, MAX, a1)
        a2 = onehot(o2, LM, m2, 32, i32_, d2)
        G1 = small(8)
        G2 = small(8)
        e2, s2 = tmp(8), tmp(8)
        a3 = tt(e2, m2, m1, SUB, d2)
        a3 = act(e2, e2, ACT.Exp, a3)
        a3 = ts(s2, e2, 1.0, None, ADD, None, a3)
        a3 = VE(lambda e: e.reciprocal(s2, s2), a3)
        a3 = tt(G1, s2, wg_, MUL, a3, t_wg)
        t_g = tt(G2, G1, e2, MUL, a3)
        OO = tmp(8, 32)
        PR = tmp(8, 32)
        a = tt(OO, o1, o2, ADD, a2)
        z_a = VE(lambda e: e.memset(PR[:, 0, :], 0.0), a)
        pr = z_a
        for i in range(1, 8):
            pr = tt(PR[:, i, :], PR[:, i - 1, :], OO[:, i - 1, :], ADD, pr)
        TOT = tmp(32)
        pr2 = tt(TOT, PR[:, 7, :], OO[:, 7, :], ADD, pr)
        b, ps, fr = PB.take()
        mm(ps[:, 0:256], cst("sltu"), OO.rearrange("p a b -> p (a b)"), True, False, a, fr)
        last = mm(ps[:, 0:256], cst("ones"), PR.rearrange("p a b -> p (a b)"), False, True, pr)
        b2, ps2, fr2 = PB.take()
        last2 = mm(ps2[:, 0:32], cst("ones"), TOT, True, True, pr2, fr2)
        NV, NVI, TMPV = tmp(32), tmp(32), tmp(32)
        CN = tmp(32)
        d = cp(VE, CN, ps2[:, 0:32], last2)
        PB.free[b2] = d
        a = ts(NV, CN, float(CAP), None, ALU.is_gt, None, d)
        for k in range(2, 8):
            a = stt(NV, CN, float(CAP * k), NV, ALU.is_gt, ADD, a)
        ON = tmp(32)
        o_ = VE(lambda e: e.memset(ON, 1.0))
        a = VE(lambda e: e.tensor_tensor_scan(NVI, ON, NV, 0.0, MUL, ADD), a, o_)
        BO = tmp(32)
        c = tt(BO, NVI, NV, SUB, a)
        c = ts(BO, BO, 31.0, 128.0, ADD, MUL, c)
        c = tt(BO, BO, cst("eidx"), SUB, c)
        PO = tmp(8, 32)
        OV = tmp(8, 32)
        d = cp(VE, PO, ps[:, 0:256].rearrange("p (a b) -> p a b", a=8), last)
        PB.free[b] = d
        e_ = ts(OV, PO, float(CAP), None, ALU.is_ge, None, d)
        e_ = tt(OV, OV, BO.unsqueeze(1).broadcast_to([128, 8, 32]), MUL, e_, c)
        e_ = tt(PO, PO, OV, ADD, e_)
        e_ = tt(PO, PO, cst("eidx").unsqueeze(1).broadcast_to([128, 8, 32]), ADD, e_)
        PS_ = tmp(8, 2)
        for k, o in enumerate((o1, o2)):
            a = tt(OV, PO, o, MUL, e_)
            e_ = red(PS_[:, :, k], OV, ADD, a)
        POSI = small(16).bitcast(I32).rearrange("p (a b) -> p a b", a=8)
        t_pos = cp(VE, POSI, PS_, e_)
        TOKI = small(8).bitcast(I32)
        t_tok = cp(VE, TOKI, cst("tok"), l_c)
        EB = tmp(15, 32)
        EF = tmp(16)
        io15 = cst("iota")[:, 0:15].unsqueeze(2).broadcast_to([128, 15, 32])
        a = tt(EB, NVI.unsqueeze(1).broadcast_to([128, 15, 32]), io15, ALU.is_le, c)
        a = red(EF[:, 0:15], EB, ADD, a)
        a = ts(EF[:, 0:15], EF[:, 0:15], 31.0, None, MIN, None, a)
        b_ = cp(VE, EF[:, 15:16], NVI[:, 31:32], c)
        EI = small(16).bitcast(I32)
        t_ei = cp(VE, EI, EF, a, b_)
        INI = mem(60, [128], p=NBLK).bitcast(I32)
        d = VE(lambda e: e.memset(INI, T), yt_free)
        stdL = Load(sem())
        t_ini = dma(GP, std[:, :].rearrange("(b s) o -> b (s o)", s=128), INI, d, load=stdL)
        stdS = Load(sem())

        def indirect(load, lane, *w, **kw):
            load.n += 16
            lane(lambda e: e.indirect_dma_start(**kw).then_inc(load.sem, 16), *w)
            return Landed(load.sem, load.n)

        for i in range(NT):
            for k in range(2):
                t_sc = indirect(stdS, GP, t_ini, t_pos, t_tok, out=std[:, :],
                                out_offset=bass.IndirectOffsetOnAxis(ap=POSI[:, i, k:k + 1].bitcast(U32), axis=0),
                                in_=TOKI[:, i:i + 1], in_offset=None)
        ada_chunks(4, 6)
        STI = mem(60.5, [128], p=NBLK).bitcast(I32)
        STF = mem(61, [128], p=NBLK)
        t_st = dma(GP, STI, std[:, :].rearrange("(b s) o -> b (s o)", s=128), t_sc, h2T)
        d = cp(VE, STF, STI, t_st)
        b, ps, fr = PB.take()
        last = tr(ps[:, 0:NBLK], STF, cst("ident")[0:NBLK, 0:NBLK], d, fr)
        TAB = small(NBLK).bitcast(I32)
        t_tab = cp(VE, TAB, ps[:, 0:NBLK], last)
        PB.free[b] = t_tab
        routed = [t_tab, t_ei, t_g, t_pos]

        RING = [96, 64, 80, 112, 128, 144, 160, 176]
        for kb in RING:
            slots.setdefault(kb, Slot(kb))
        slots[96].used = [yn[-1], att_end, t_yz, yt_free]
        slots[112].used = [h2T[-1], h2T[-2], h2T[-3], t_h2[-1], lg_end]
        slots[128].used = slots[144].used = h2T + [lg_end]
        slots[160].used = slots[176].used = [yt_free]
        wi = [0]

        def expert_w(e):
            out_ = []
            for nm, c, n in (("exp_w_gate", 8, 512), ("exp_w_up", 8, 512), ("exp_w_down", 4, 1024)):
                kb = RING[wi[0] % len(RING)]
                wi[0] += 1
                s = slots[kb]
                dst = mem(kb, [c, n])
                ld = dma(SY, dst, A[nm][0, e].rearrange("(p c) n -> p c n", c=c), s.used, load=s.load)
                s.used = []
                out_.append((dst, ld, s))
            return out_

        XGB = [mem(32, [1024]), mem(36, [1024])]
        XTB = [mem(40, [8, 128]), mem(44, [8, 128])]
        SGB = [mem(48, [512]), mem(50, [512])]
        HDB = [mem(52, [512]), mem(54, [512])]
        HTB = [mem(56, [4, 128]), mem(58, [4, 128])]
        YB = [mem(60, [1024]), mem(192, [1024])]

        class Experts:

            def __init__(self, start):
                self.xg, self.xt = [start] * 2, [start] * 2
                self.sg, self.hd, self.ht, self.y = [start] * 2, [start] * 2, [start] * 2, [start] * 2
                self.bank = {b: [PB.free.get(b), start] for b in range(8)}
                self.gl = [Load(sem()), Load(sem())]
                self.yl = [Load(sem()), Load(sem())]

            def gather(self, n, blk):
                k = n % 2
                return indirect(self.gl[k], GP, self.xg[k], t_tab, t_h2[-1], out=XGB[k], out_offset=None, in_=h2d,
                                in_offset=bass.IndirectOffsetOnAxis(ap=TAB[:, blk:blk + 1].bitcast(U32), axis=0))

            def turn(self, n, t_g):
                k = n % 2
                done = []
                for q in range(2):
                    ps = banks[q]
                    for c in range(4):
                        last = tr(ps[:, 128 * c:128 * c + 128], XGB[k][:, 4 * q + c::8], cst("ident"), t_g, self.bank[q])
                    g = g2[:, 4 * q:4 * q + 4].unsqueeze(2).broadcast_to([128, 4, 128])
                    d = tt(XTB[k][:, 4 * q:4 * q + 4, :], ps[:, :].rearrange("p (a b) -> p a b", a=4), g, MUL,
                           last, self.xt[k])
                    self.bank[q] = d
                    done.append(d)
                self.xg[k] = last
                return done

            def up(self, n, xt, w):
                k = n % 2
                for v in range(2):
                    dst, ld, s = w[v]
                    for c in range(8):
                        last = mm(banks[2 + v][:, :], XTB[k][:, c, :], dst[:, c, :], c == 0, c == 7, xt, ld, self.bank[2 + v])
                    s.used = [last]
                    if v == 0:
                        sg = act(SGB[k], banks[2][:, :], ACT.Silu, last, self.sg[k])
                        self.bank[2] = sg
                self.xt[k] = last
                hd = tt(HDB[k], banks[3][:, :], SGB[k], MUL, last, sg, self.hd[k])
                self.bank[3] = self.sg[k] = hd
                return hd

            def down(self, n, hd, w, blk):
                k = n % 2
                for j in range(4):
                    last = tr(banks[4][:, 128 * j:128 * j + 128], HDB[k][:, j::4], cst("ident"), hd, self.bank[4])
                self.hd[k] = last
                ht = cp(AC, HTB[k], banks[4][:, :].rearrange("p (a b) -> p a b", a=4), last, self.ht[k])
                self.bank[4] = ht
                dst, ld, s = w[2]
                ev = []
                for q in range(2):
                    for j in range(4):
                        last = mm(banks[5 + q][:, :], HTB[k][:, j, :], dst[:, j, 512 * q:512 * q + 512], j == 0, j == 3,
                                  ht, ld, self.bank[5 + q])
                    e = cp((VE, AC)[q], YB[k][:, 512 * q:512 * q + 512], banks[5 + q][:, :], last, self.y[k])
                    self.bank[5 + q] = e
                    ev.append(e)
                s.used = [last]
                self.ht[k] = last
                self.y[k] = dma(AC, ysl[128 * blk:128 * blk + 128, :], YB[k], ev, load=self.yl[k])
                return self.y[k]

        X1 = Experts([yt_free, routed, t_wg, t_ada])
        ws = [expert_w(0), expert_w(1)]
        gs = [X1.gather(0, 0), X1.gather(1, 1)]
        xt = X1.turn(0, gs[0])
        for e in range(NEXP):
            hd = X1.up(e, xt, ws[e])
            if e + 1 < NEXP:
                xt = X1.turn(e + 1, gs[e + 1])
            if e + 2 < NEXP:
                gs.append(X1.gather(e + 2, e + 2))
            y_ = X1.down(e, hd, ws[e], e)
            if e + 2 < NEXP:
                ws.append(expert_w(e + 2))
        y_end = [X1.y[0], X1.y[1]]
        pe_end = PE(lambda e: e.nop(), X1.ht)

        for l in lanes:
            l.when(EI[0:1, 15:16], t_ei, pe_end, y_end, t_yz)
        X2 = Experts(None)
        X2.bank = {b: None for b in range(8)}
        owl = [Load(sem()) for _ in range(3)]
        last_use = None
        for blk in range(NOV):
            w = []

            class Used:
                used = []

            reg = {}

            def expert_of(e, blk=blk, reg=reg):
                reg["e"] = e.value_load(EI[0:1, blk:blk + 1], min_val=0, max_val=31)
                return e.nop()

            SY(expert_of, last_use)
            for v, (nm, c, n, kb) in enumerate((("exp_w_gate", 8, 512, 96), ("exp_w_up", 8, 512, 64), ("exp_w_down", 4, 1024, 80))):
                dst = mem(kb, [c, n])
                owl[v].n += 16
                SY(lambda e, reg=reg, v=v, nm=nm, c=c, dst=dst: e.dma_start(
                    dst, A[nm][0, bass.ds(reg["e"], 1)].rearrange("a (p c) n -> p (a c) n", c=c)).then_inc(owl[v].sem, 16),
                   last_use)
                w.append((dst, Landed(owl[v].sem, owl[v].n), Used()))
            g_ = X2.gather(blk, NEXP + blk)
            xt = X2.turn(blk, g_)
            hd = X2.up(blk, xt, w)
            y_ = X2.down(blk, hd, w, NEXP + blk)
            last_use = X2.ht[blk % 2]
            if blk >= 1:
                AC(lambda e: e.nop(), X2.y[(blk - 1) % 2])
        for l in (SY, PE, AC, VE, GP):
            l(lambda e: e.nop(), X2.y[0], X2.y[1], last_use)
        for l in lanes:
            l.always()
        ex = [l(lambda e: e.nop()) for l in lanes]
        for l in lanes:
            l(lambda e: e.nop(), ex)
        for b in range(8):
            PB.free[b] = X1.bank[b]
        for s in slots.values():
            s.used = list(s.used) + ex

        asf, abf = [ex, ex], [ex, ex]
        CB = [mem(32 + 4 * i, [1024]) for i in range(8)]
        cbl = [Load(sem()) for _ in range(8)]
        cbf = [None] * 8
        x2 = []
        k = 0
        for i in range(NT):
            d = x1[i]
            for q, G in enumerate((G1, G2)):
                ld = indirect(cbl[k % 8], GP, cbf[k % 8], ex, y_end, t_yz, t_pos, out=CB[k % 8], out_offset=None, in_=ysl,
                              in_offset=bass.IndirectOffsetOnAxis(ap=POSI[:, i, q:q + 1].bitcast(U32), axis=0))
                d = stt(X[:, i, :], CB[k % 8], G[:, i:i + 1], X[:, i, :], MUL, ADD, ld, d, t_g)
                cbf[k % 8] = d
                k += 1
            x2.append(d)
        for kb in ADA_AT[1]:
            slots[kb].used = [ex, slots[kb].used]
        ada_chunks(6, 12)

        cp2 = Load(sem())
        m = small_at[0]
        gbc, gnc, qnc, kvc = small(4), small(1), small(2), small(1)
        for o, v, n in ((gbc, A["gla_b_2"][0].rearrange("k (j p) -> p (k j)", p=128), 4),
                        (gnc, A["gla_norm_g_2"][0].rearrange("(p j) -> p j", j=1), 1),
                        (qnc, A["mla_q_norm_g_2"][0].rearrange("(j p) -> p j", p=128), 2),
                        (kvc, A["mla_kv_norm_g_2"][0].rearrange("(p j) -> p j", j=1), 1)):
            t_cp2 = dma(SY, o, v, load=cp2, allow_slow_non_contiguous=True)
        SH, SCL = {}, {}
        adl = Load(sem())
        for key, l, r in (("l0", 0, 0), ("c0", 0, 1), ("l1", 1, 0)):
            SH[key], SCL[key] = small(8), small(8)
            t_ad = dma(SY, SH[key], ada_d[l, r, 0:1024].rearrange("(p c) -> p c", c=8), t_ada, load=adl)
            t_ad = dma(SY, SCL[key], ada_d[l, r, 1024:2048].rearrange("(p c) -> p c", c=8), load=adl)
        for key in SH:
            t_scl = ts(SCL[key], SCL[key], 1.0, None, ADD, None, t_ad)

        HC = mem(64, [8, 256])
        GQ, GK, GV = mem(104, [2, 1024]), mem(112, [2, 1280]), mem(122, [10, 512])
        LK, GG = mem(142, [1280]), mem(147, [4, 1024])
        CQ, CKV, MG = mem(163, [2, 1024]), mem(171, [1280]), mem(176, [8, 512])
        LRW = mem(192, [8, 32])
        SA, SB = 72, 88
        for kb in (SA, SB):
            slots[kb] = Slot(kb)
            slots[kb].used = list(slots[96].used)
        w_e = A["even_w_in_2"][0].rearrange("(p c) n -> p c n", c=8)

        def w_chunk(kb, src, cols):
            dst = mem(kb, [8, cols])
            s = slots[kb]
            m = dma(SY, dst, src, s.used, load=s.load)
            s.used = []
            return dst, m

        l_lr = dma(SY, LRW, w_e[:, :, 1024:1056], slots[96].used, t_ada)
        wq_ = w_chunk(SA, w_e[:, :, 0:512], 512)
        wv_ = w_chunk(SB, w_e[:, :, 512:1024], 512)
        HL = mem(32, [8, T])
        CT_ = [mem(193 + 0, [1024]), mem(196.5, [1024])]
        CXR = mem(104, [2, 1024])
        l_cx = dma(SY, CXR, A["ctx_2"][0].rearrange("(t p) d -> p t d", p=128), ex)
        tc_ = token_stats(2, lambda i: CXR[:, i, :], [[l_cx, x2[-1]], None], False)
        hC = channel_major(2, lambda i: CXR[:, i, :], tc_, True, 147, HC, SCL["c0"], SH["c0"], [t_scl, ex])
        tx = token_stats(NT, lambda i: X[:, i, :], [[x, hC] for x in x2], False)
        hL = channel_major(NT, lambda i: X[:, i, :], [tx, hC], True, 147, HL, SCL["l0"], SH["l0"], [t_scl])
        hLC = [hL, hC]
        CH = [(HC, 0, 0, 256), (HL, 0, 256, 512), (HL, 512, 768, 512)]

        def cm_lc(w, lw, col, m, evac, ctx_too=True):
            for src, t0, o, n in CH if ctx_too else CH[1:]:
                b, ps, last = proj_cm(w, lw, col, src, 0, hLC, m=m, n=n, tok=t0)
                PB.free[b] = evac(ps[0:m, 0:n], o, n, last)
            return last

        w, lw = wq_
        gq_d, gk_d, gv_d, lk_d, gg_d, cq_d, ckv_d, mg_d = [], [], [], [], [], [], [], []
        alt = [0]

        def put(dst, lst, scale=None, func=None):
            def f(ps, o, n, last):
                if func is not None:
                    d = act(dst(o, n), ps, func, last)
                elif scale is not None:
                    d = ts(dst(o, n), ps, scale, None, MUL, None, last)
                else:
                    alt[0] ^= 1
                    d = cp((VE, AC)[alt[0]], dst(o, n), ps, last)
                lst.append(d)
                return d
            return f

        for j in range(2):
            cm_lc(w, lw, 128 * j, 128, put(lambda o, n, j=j: GQ[:, j, o - 256:o - 256 + n], gq_d, scale=0.125), False)
            last = cm_lc(w, lw, 256 + 128 * j, 128, put(lambda o, n, j=j: GK[:, j, o:o + n], gk_d))
        slots[SA].used = [last]
        wg_c = w_chunk(SA, w_e[:, :, 1056:1568], 512)
        w, lw = wv_
        for i in range(10):
            src, t0 = (HC, 128 * i) if i < 2 else (HL, 128 * (i - 2))
            b, ps, fr = PB.take()
            for c in range(8):
                last = mm(ps[:, :], src[:, c, t0:t0 + 128], w[:, c, :], c == 0, c == 7, fr, lw)
            d = cp((VE, AC)[i % 2], GV[:, i, :], ps[:, :], last)
            PB.free[b] = d
            gv_d.append(d)
        slots[SB].used = [last]
        wc_c = w_chunk(SB, w_e[:, :, 1568:1984], 416)
        for k in range(2):
            cm_lc(LRW, l_lr, 16 * k, 16, put(lambda o, n, k=k: LK[32 * k:32 * k + 16, o:o + n], lk_d))
        w, lw = wg_c
        for j in range(4):
            last = cm_lc(w, lw, 128 * j, 128, put(lambda o, n, j=j: GG[:, j, o - 256:o - 256 + n], gg_d, func=ACT.Silu), False)
        slots[SA].used = [last]
        wm_c = w_chunk(SA, w_e[:, :, 1984:2496], 512)
        w, lw = wc_c
        for j in range(2):
            cm_lc(w, lw, 128 * j, 128, put(lambda o, n, j=j: CQ[:, j, o - 256:o - 256 + n], cq_d), False)
        cm_lc(w, lw, 256, 128, put(lambda o, n: CKV[:, o:o + n], ckv_d))
        last = cm_lc(w, lw, 384, 32, put(lambda o, n: LK[64:96, o:o + n], lk_d))
        slots[SB].used = [last]
        w, lw = wm_c
        for i in range(8):
            b, ps, fr = PB.take()
            for c in range(8):
                last = mm(ps[:, :], HL[:, c, 128 * i:128 * i + 128], w[:, c, :], c == 0, c == 7, fr, lw)
            d = act(MG[:, i, :], ps[:, :], ACT.Silu, last)
            PB.free[b] = d
            mg_d.append(d)
        slots[SA].used = [last]
        pr_end = last

        YG = mem(32, [4, 1024])
        GB, QM, KM, QE, KD = mem(48, [1280]), mem(53, [1024]), mem(57, [1024]), mem(64, [1024]), mem(72, [1280])
        KDT, SS = mem(77, [10, 128]), mem(82, [16, 128])
        E1, E2 = mem(90, [1280]), mem(95, [1024])
        RM = mem(99, [1024])
        W2G = mem(193, [256])
        l_w2g = [dma(SY, W2G[32 * k:32 * k + 16, :], A["gla_w2_2"][0, k], ex, pr_end) for k in range(2)]
        ATT = [[mem(61, [512]), mem(68, [512])], [mem(70, [512]), mem(194, [512])]]
        DC = small(16)
        tz = []
        for k in range(2):
            for q in range(2):
                tz.append(VE(lambda e, k=k, q=q: e.memset(ATT[k][q], 0.0), pr_end))
        d = VE(lambda e: e.memset(RM, 1.0), pr_end)
        d = VE(lambda e: e.memset(RM[:, ::64], 0.0), d)
        tz.append(d)
        PG = Banks(banks, [0, 1, 2, 3])
        PG.free = dict(PB.free)
        gla_all = [gq_d, gk_d, gv_d, lk_d, gg_d, pr_end, tz]
        o_free = [PB.free.get(4 + i) for i in range(4)]
        prev_pe = None
        prev_all = [pr_end]
        attf = [[None, None], [None, None]]
        yg_d = []
        AC(lambda e: e.preload_act_table_set("natural_log_exp_and_others"))
        for tau in range(2):
            for k in range(2):
                g_d = []
                for o, n in ((0, 256), (256, 512), (768, 512)):
                    b, ps, fr = PG.take()
                    m1 = mm(ps[:, 0:n], W2G[32 * k:32 * k + 16, 128 * tau:128 * tau + 128], LK[32 * k:32 * k + 16, o:o + n],
                            True, True, fr, l_w2g, lk_d)
                    bias = gbc[:, 2 * k + tau:2 * k + tau + 1]
                    a0 = act(E1[:, o:o + n], ps[:, 0:n], ACT.Abs, m1, prev_all, t_cp2, bias=bias)
                    a = act(E1[:, o:o + n], E1[:, o:o + n], ACT.Exp, a0, scale=-1.0)
                    a = act(E1[:, o:o + n], E1[:, o:o + n], ACT.Ln, a, bias=1.0)
                    d = ts(KD[:, o:o + n], ps[:, 0:n], bias, 0.0, ADD, MIN, m1, a0, prev_all, t_cp2)
                    PG.free[b] = [d, a]
                    d = tt(KD[:, o:o + n], KD[:, o:o + n], E1[:, o:o + n], SUB, d, a)
                    g_d.append(d)
                o1_ = VE(lambda e: e.memset(E2[:, 0:256], 1.0), prev_all)
                if k == 0:
                    d = VE(lambda e: e.tensor_tensor_scan(GB[:, 0:256], E2[:, 0:256], KD[:, 0:256], 0.0, MUL, ADD), g_d, o1_, prev_all)
                    d2 = VE(lambda e: e.tensor_tensor_scan(GB[:, 256:1280], RM, KD[:, 256:1280], 0.0, MUL, ADD), tz, g_d, prev_all)
                else:
                    d = VE(lambda e: e.tensor_tensor_scan(GB[:, 0:256][:, ::-1], E2[:, 0:256], KD[:, 0:256][:, ::-1], 0.0, MUL, ADD), g_d, o1_, prev_all)
                    d2 = VE(lambda e: e.tensor_tensor_scan(GB[:, 256:1280][:, ::-1], RM, KD[:, 256:1280][:, ::-1], 0.0, MUL, ADD), tz, g_d)
                BL = GB[:, 256:1280].rearrange("p (c s) -> p c s", c=16)
                mid, end = (31, 63) if k == 0 else (32, 0)
                e1v = E1[:, 256:1280].rearrange("p (c s) -> p c s", c=16)
                bmid = BL[:, :, mid:mid + 1].broadcast_to([128, 16, 64])
                bend = BL[:, :, end:end + 1].broadcast_to([128, 16, 64])
                GKl, GQl = GK[:, tau, 256:1280], GQ[:, tau, :]
                a = tt(e1v, BL, bmid, SUB, d2)
                q1 = act(QM, E1[:, 256:1280], ACT.Exp, a, prev_all, scale=1.0 / 16)
                q1 = tt(QM, QM, GQl, MUL, q1, gq_d)
                k1 = act(KM, E1[:, 256:1280], ACT.Exp, a, prev_all, scale=-1.0 / 16)
                k1 = tt(KM, KM, GKl, MUL, k1, gk_d)
                q2 = act(QE, GB[:, 256:1280], ACT.Exp, d2, prev_all, scale=1.0 / 16)
                q2 = tt(QE, QE, GQl, MUL, q2, gq_d)
                a = tt(KD[:, 256:1280].rearrange("p (c s) -> p c s", c=16), bend, BL, SUB, d2, d)
                ce = 255 if k == 0 else 0
                a2 = tt(KD[:, 0:256], GB[:, ce:ce + 1].broadcast_to([128, 256]), GB[:, 0:256], SUB, d)
                a = act(KD, KD, ACT.Exp, a, a2, scale=1.0 / 16)
                k2 = tt(KD, KD, GK[:, tau, :], MUL, a, gk_d)
                dc = act(DC, BL[:, :, end], ACT.Exp, d2, prev_all, scale=1.0 / 16)
                kdt = []
                for q in range(3):
                    m_ = 4 if q < 2 else 2
                    b, ps, fr = PG.take()
                    for j in range(m_):
                        i = 4 * q + j
                        last = tr(ps[:, 128 * j:128 * j + 128], KD[:, 128 * i:128 * i + 128], cst("ident"), k2, fr)
                    d = cp(AC, KDT[:, 4 * q:4 * q + m_, :], ps[:, 0:128 * m_].rearrange("p (a b) -> p a b", a=m_), last, prev_all)
                    PG.free[b] = d
                    kdt.append(d)
                b, ps, fr = PG.take()
                for hh in range(2):
                    hv = slice(128 * (2 * tau + hh), 128 * (2 * tau + hh) + 128)
                    for i in range(2):
                        last = mm(ps[64 * hh:64 * hh + 64, 0:128], KDT[:, i, 64 * hh:64 * hh + 64], GV[:, i, hv], i == 0, i == 1,
                                  kdt, fr, gv_d)
                order = list(range(16)) if k == 0 else list(range(15, -1, -1))
                s_d = cp(VE, SS[:, order[0], :], ps[:, 0:128], last, prev_all)
                PG.free[b] = s_d
                s_at = {order[0]: s_d}
                for q in range(2):
                    grp = order[8 * q:8 * q + 8]
                    bk = {}
                    for par in range(2):
                        b, ps, fr = PG.take()
                        bk[par] = (b, ps)
                        for n_, c in enumerate([c for c in grp if c % 2 == par]):
                            p0, i = 64 * par, 2 + c // 2
                            for hh in range(2):
                                hv = slice(128 * (2 * tau + hh), 128 * (2 * tau + hh) + 128)
                                last = mm(ps[64 * hh:64 * hh + 64, 128 * n_:128 * n_ + 128],
                                          KDT[p0:p0 + 64, i, 64 * hh:64 * hh + 64], GV[p0:p0 + 64, i, hv], True, True, kdt, fr)
                    for n_, c in enumerate(grp):
                        nx = order.index(c) + 1
                        if nx < 16:
                            c0 = 128 * (n_ // 2)
                            s_d = stt(SS[:, order[nx], :], SS[:, c, :], DC[:, c:c + 1], bk[c % 2][1][:, c0:c0 + 128], MUL, ADD,
                                      last, s_d, dc)
                            s_at[order[nx]] = s_d
                    PG.free[bk[0][0]] = PG.free[bk[1][0]] = s_d
                msk = cst("glaf" if k == 0 else "glar").unsqueeze(1).broadcast_to([128, 4, 128]).bitcast(I32)
                for g_ in range(4):
                    b, ps, fr = PG.take()
                    for n_ in range(4):
                        i, hh = 4 * (g_ // 2) + n_, g_ % 2
                        last = mm(ps[:, 128 * n_:128 * n_ + 128], KM[64 * hh:64 * hh + 64, 128 * i:128 * i + 128],
                                  QM[64 * hh:64 * hh + 64, 128 * i:128 * i + 128], True, True, q1, k1, fr)
                    at_ = ATT[k][g_ % 2]
                    d = VE(lambda e, at_=at_, ps=ps, msk=msk: e.copy_predicated(
                        at_.rearrange("p (a b) -> p a b", a=4), msk, ps[:, :].rearrange("p (a b) -> p a b", a=4)),
                        last, attf[k][g_ % 2], tz)
                    PG.free[b] = d
                    for n_ in range(4):
                        i, hh = 4 * (g_ // 2) + n_, g_ % 2
                        h = 2 * tau + hh
                        ob = banks[4 + 2 * hh + i // 4]
                        c0 = 128 * (i % 4)
                        mm(ob[:, c0:c0 + 128], GV[:, 2 + i, 128 * h:128 * h + 128], at_[:, 128 * n_:128 * n_ + 128], k == 0 and n_ == 0, False,
                           d, o_free if k == 0 else None)
                        for c in (2 * i, 2 * i + 1):
                            last = mm(ob[:, c0 + 64 * (c % 2):c0 + 64 * (c % 2) + 64], SS[64 * hh:64 * hh + 64, c, :],
                                      QE[64 * hh:64 * hh + 64, 64 * c:64 * c + 64], False, k == 1, s_at[c], q2)
                    attf[k][g_ % 2] = last
                prev_all = [last]
            fr4 = []
            for hh in range(2):
                h = 2 * tau + hh
                for half in range(2):
                    s0 = slice(512 * half, 512 * half + 512)
                    ob = banks[4 + 2 * hh + half]
                    sq = act(E2[:, 0:512], ob[:, :], ACT.Square, last, prev_all)
                    b, ps, fr = PG.take()
                    m1 = mm(ps[:, :], cst("ones"), E2[:, 0:512], True, True, sq, fr)
                    r = rsq(E1[:, 0:512], ps[:, :], 128, m1, prev_all)
                    PG.free[b] = r
                    d = stt(YG[:, h, s0], ob[:, :], gnc[:, 0:1], E1[:, 0:512], MUL, MUL, r, t_cp2)
                    fr4.append(d)
                    d = tt(YG[:, h, s0], YG[:, h, s0], GG[:, h, s0], MUL, d, gg_d)
                    yg_d.append(d)
                    prev_all = [d, m1]
            o_free = fr4
        for b in range(4):
            PB.free[b] = PG.free.get(b)
            PB.free[4 + b] = fr4
        gla_end = [yg_d[-1], m1]

        QT, KT, MV = mem(48, [8, 1024], p=96), mem(80, [8, 1280], p=96), mem(122, [10, 512])
        WQN, WQR, WKN, WKVV = mem(147, [2, 512]), mem(151, [2, 256]), mem(153, [512]), mem(155, [512])
        ROP = mem(192, [2, 1024])
        MSQ = [mem(157, [512]), mem(159, [512])]
        MR = mem(161, [512])
        uq = A["mla_w_uq_2"][0].rearrange("(j p) (h x) -> p j h x", p=128, h=8)
        ukv = A["mla_w_ukv_2"][0].rearrange("p (h x) -> p h x", h=8)
        wml = Load(sem())
        for j in range(2):
            dma(SY, WQN[:, j, :].rearrange("p (h x) -> p h x", h=8), uq[:, j, :, 0:64], gla_end, load=wml)
            dma(SY, WQR[:, j, :].rearrange("p (h x) -> p h x", h=8), uq[:, j, :, 64:96], load=wml)
        dma(SY, WKN.rearrange("p (h x) -> p h x", h=8), ukv[:, :, 0:64], load=wml)
        l_uq = l_kv = dma(SY, WKVV.rearrange("p (h x) -> p h x", h=8), ukv[:, :, 64:128], load=wml)
        l_rp = dma(SY, ROP, A["k_rope"].rearrange("a p n -> p a n"), gla_end)
        mrf = gla_end
        msf = [gla_end, gla_end]
        cqn, kvn = [], []
        k = 0
        for src, gain, nj, chunks, dn, lst in ((CKV.unsqueeze(1), kvc, 1, ((0, 256), (256, 512), (768, 512)), ckv_d, kvn),
                                               (CQ, qnc, 2, ((0, 512), (512, 512)), cq_d, cqn)):
            for o, n in chunks:
                b, ps, fr = PB.take()
                for j in range(nj):
                    q = act(MSQ[k % 2][:, 0:n], src[:, j, o:o + n], ACT.Square, dn, msf[k % 2])
                    last = mm(ps[:, 0:n], cst("ones"), MSQ[k % 2][:, 0:n], j == 0, j == nj - 1, q, fr)
                    msf[k % 2] = last
                    k += 1
                r = rsq(MR[:, 0:n], ps[:, 0:n], 128 * nj, last, mrf)
                PB.free[b] = r
                for j in range(nj):
                    d = stt(src[:, j, o:o + n], src[:, j, o:o + n], gain[:, j:j + 1], MR[:, 0:n], MUL, MUL, r, t_cp2)
                mrf = d
                lst.append(d)
        qt_d, kt_d, mv_d = [], [], []
        RQ = [mem(157, [512]), mem(159, [512])]
        RT1 = mem(161, [512])
        RT2 = mem(142 + 5 - 5, [512])
        rqf = [mrf, mrf]
        rtf = mrf
        kr0 = cp(AC, KT[64:96, 0, 0:256], LK[64:96, 0:256], lk_d, gla_end)
        krl = [kr0]
        for half in range(2):
            s0 = slice(512 * half, 512 * half + 512)
            lk = LK[64:96, 256 + 512 * half:768 + 512 * half]
            b, ps, fr = PB.take()
            m1 = mm(ps[64:96, :], cst("perm")[64:96, 64:96], lk, True, True, fr, lk_d, gla_end)
            d = tt(RT1[64:96, :], ps[64:96, :], ROP[64:96, 1, s0], MUL, m1, l_rp, rtf)
            PB.free[b] = d
            ko = KT[64:96, 0, 256 + 512 * half:768 + 512 * half]
            a = tt(ko, lk, ROP[64:96, 0, s0], MUL, l_rp, gla_end)
            d = tt(ko, ko, RT1[64:96, :], ADD, d, a)
            rtf = d
            krl.append(d)
        for h in range(1, 8):
            kt_d.append(cp(GP, KT[64:96, h, :], KT[64:96, 0, :], krl))
        kt_d += krl
        for hp in range(4):
            for o, n in ((0, 256), (256, 512), (768, 512)):
                b, ps, fr = PB.take()
                last = mm(ps[:, 0:n], WKN[:, 128 * hp:128 * hp + 128], CKV[:, o:o + n], True, True, fr, l_kv, kvn)
                d1 = cp(VE, KT[0:64, 2 * hp, o:o + n], ps[0:64, 0:n], last, gla_end)
                d2 = cp(AC, KT[0:64, 2 * hp + 1, o:o + n], ps[64:128, 0:n], last, gla_end)
                PB.free[b] = [d1, d2]
                kt_d += [d1, d2]
        for hp in range(4):
            for half in range(2):
                s0 = slice(512 * half, 512 * half + 512)
                b, ps, fr = PB.take()
                for j in range(2):
                    last = mm(ps[:, :], WQN[:, j, 128 * hp:128 * hp + 128], CQ[:, j, s0], j == 0, j == 1, fr, l_uq, cqn)
                d1 = cp(VE, QT[0:64, 2 * hp, s0], ps[0:64, :], last, gla_end)
                d2 = cp(AC, QT[0:64, 2 * hp + 1, s0], ps[64:128, :], last, gla_end)
                PB.free[b] = [d1, d2]
                qt_d += [d1, d2]
        k = 0
        for g_ in range(2):
            for half in range(2):
                s0 = slice(512 * half, 512 * half + 512)
                b, ps, fr = PB.take()
                for j in range(2):
                    last = mm(ps[:, :], WQR[:, j, 128 * g_:128 * g_ + 128], CQ[:, j, s0], j == 0, j == 1, fr, l_uq, cqn)
                r = cp(AC, RQ[k % 2], ps[:, :], last, rqf[k % 2])
                b2, ps2, fr2 = PB.take()
                m2 = mm(ps2[:, :], cst("perm"), RQ[k % 2], True, True, r, fr2)
                d = tt(RT1, ps2[:, :], ROP[:, 1, s0], MUL, m2, rtf)
                PB.free[b2] = d
                a = tt(RQ[k % 2], RQ[k % 2], ROP[:, 0, s0], MUL, m2)
                PB.free[b] = r
                a = tt(RQ[k % 2], RQ[k % 2], RT1, ADD, a, d)
                rtf = a
                for q in range(4):
                    c_ = cp(AC if q % 2 else VE, QT[64:96, 4 * g_ + q, s0], RQ[k % 2][32 * q:32 * q + 32, :], a, gla_end)
                    qt_d.append(c_)
                rqf[k % 2] = qt_d[-2:]
                k += 1
        for i in range(10):
            b, ps, fr = PB.take()
            last = mm(ps[:, :], CKV[:, 128 * i:128 * i + 128], WKVV, True, True, fr, l_kv, kvn)
            d = cp((VE, AC)[i % 2], MV[:, i, :], ps[:, :], last, gla_end)
            PB.free[b] = d
            mv_d.append(d)
        up_end = [last, rtf]

        YM = mem(147, [4, 1024])
        PP = [mem(163, [1280]), mem(168, [1280])]
        PT = [mem(192, [10, 128]), mem(142, [10, 128])]
        OT = [mem(173, [512]), mem(197, [512])]
        NM, RS2, RI = small(8), [small(8), small(8)], small(8)
        SCALE = 96.0 ** -0.5
        ready = [qt_d, kt_d, mv_d, up_end]
        start = [PB.free.get(b) for b in range(8)]
        sfree = [start, start]
        tfree = [start]
        ppf, ptf = [up_end, up_end], [up_end, up_end]
        otf = [up_end, up_end]
        ym_d = []
        its = [(qt, h) for qt in range(8) for h in range(8)]
        st = {}

        def score_part(s, q):
            qt, h = its[s]
            o, n = ((0, 512), (512, 512), (1024, 256))[q]
            return mm(PSM[:, 3 * (s % 2) + q, 0:n], QT[:, h, 128 * qt:128 * qt + 128], KT[:, h, o:o + n], True, True,
                      sfree[s % 2], ready)

        def soften(s, last):
            qt, h = its[s]
            k = s % 2
            ps = PSM[:, 3 * k:3 * k + 3, :].rearrange("p a b -> p (a b)")[:, 0:1280]
            d = VE(lambda e: e.tensor_reduce(NM[:, h:h + 1], ps, AX, MAX), last, st.get(("e", s - 8)))
            d = ts(NM[:, h:h + 1], NM[:, h:h + 1], -SCALE, None, MUL, None, d)
            e_ = AC(lambda e: e.activation(PP[k], ps, ACT.Exp, bias=NM[:, h:h + 1], scale=SCALE,
                                           accum_out=RS2[qt % 2][:, h:h + 1]), d, ppf[k], st.get(("o", qt - 2)))
            sfree[k] = e_
            st[("e", s)] = e_

        tb = banks[6]

        def turn_part(s, q):
            k = s % 2
            m_ = 4 if q < 2 else 2
            for j in range(m_):
                i = 4 * q + j
                last = tr(tb[:, 128 * j:128 * j + 128], PP[k][:, 128 * i:128 * i + 128], cst("ident"), st[("e", s)], tfree[0])
            d = cp((VE, AC, VE)[q], PT[k][:, 4 * q:4 * q + m_, :], tb[:, 0:128 * m_].rearrange("p (a b) -> p a b", a=m_), last, ptf[k])
            tfree[0] = d
            ppf[k] = last
            return d

        def mix(s, pt):
            qt, h = its[s]
            k = s % 2
            for i in range(10):
                last = mm(banks[7][:, 64 * h:64 * h + 64], PT[k][:, i, :], MV[:, i, 64 * h:64 * h + 64], i == 0, i == 9,
                          pt[i // 4], of[0] if h == 0 else None)
            ptf[k] = last
            if h == 7:
                kk = qt % 2
                r = VE(lambda e: e.reciprocal(RI, RS2[kk]), st[("e", s)])
                d = tt(OT[kk].rearrange("p (a b) -> p a b", a=8), banks[7][:, :].rearrange("p (a b) -> p a b", a=8),
                       RI.unsqueeze(2).broadcast_to([128, 8, 64]), MUL, last, r, otf[kk])
                of[0] = d
                st[("o", qt)] = r
                return tt(OT[kk], OT[kk], MG[:, qt, :], MUL, d, mg_d)

        def turn_out(qt, d):
            kk = qt % 2
            for j in range(4):
                last = tr(tb[:, 128 * j:128 * j + 128], OT[kk][:, 128 * j:128 * j + 128], cst("ident"), d, tfree[0])
            otf[kk] = last
            d = cp(AC, YM[:, :, 128 * qt:128 * qt + 128], tb[:, :].rearrange("p (a b) -> p a b", a=4), last, up_end)
            tfree[0] = d
            ym_d.append(d)

        of = [start]
        late = None
        for s in range(66):
            pt = []
            for q in range(3):
                if s >= 2:
                    pt.append(turn_part(s - 2, q))
                if s < 64:
                    last = score_part(s, q)
            if s < 64:
                soften(s, last)
            if late:
                turn_out(*late)
                late = None
            if s >= 2:
                d = mix(s - 2, pt)
                if its[s - 2][1] == 7:
                    late = (its[s - 2][0], d)
        turn_out(*late)
        for b in range(8):
            PB.free[b] = [sfree, tfree, of]
        ml_end = [ym_d[-1], ptf]

        GROW, PLG, PLB = mem(120 - 8, [1024]), mem(116, [1024]), mem(122, [1024])

        def post(layer, W, lw, tile_of, yd, G_, P1_, P2_, w0, tmps):
            l1 = dma(SY, G_, ada_d[layer, 0:1, 2048:3072].broadcast_to([128, 1024]), w0)
            l2 = dma(SY, P1_, A["post_ln_g_2"][layer:layer + 1, :].broadcast_to([128, 1024]), w0)
            l3 = dma(SY, P2_, A["post_ln_b_2"][layer:layer + 1, :].broadcast_to([128, 1024]), w0)
            done = []
            alpha = float(4 ** 0.25)
            fr_t = [w0, w0]
            bnf = None
            for i in range(NT):
                xi = X[:, i, :]
                ds_ = []
                for q in range(2):
                    b, ps, fr = PB.take()
                    for j in range(8):
                        last = mm(ps[:, :], tile_of(j)[:, 128 * i:128 * i + 128], W[:, j, 512 * q:512 * q + 512], j == 0, j == 7,
                                  fr, lw, yd)
                    s_ = slice(512 * q, 512 * q + 512)
                    d = tt(tmps[q], ps[:, :], G_[:, s_], MUL, last, l1, fr_t[q])
                    PB.free[b] = d
                    d = stt(xi[:, s_], xi[:, s_], alpha, tmps[q], MUL, ADD, d)
                    fr_t[q] = d
                    ds_.append(d)
                mvi = mvv[:, i, :]
                d = stats(xi, 1024, bnb, mvi, [ds_, bnf])
                bnf = d
                r = rsq(rs8[:, i:i + 1], mvi[:, 1:2], 1, d)
                n_ = stt(nb8[:, i:i + 1], mvi[:, 0:1], -1.0, rs8[:, i:i + 1], MUL, MUL, r)
                a = act(xi, xi, ACT.Identity, n_, scale=rs8[:, i:i + 1], bias=nb8[:, i:i + 1])
                a = tt(xi, xi, P1_, MUL, a, l2, lane=GP)
                a = tt(xi, xi, P2_, ADD, a, l3, lane=GP)
                done.append(a)
            return done, last

        WO2 = mem(48, [8, 1024])
        w2v = A["even_w_out_2"][0].rearrange("(j p) n -> p j n", p=128)
        l_wo2 = [dma(SY, WO2[:, 4 * q:4 * q + 4, :], w2v[:, 4 * q:4 * q + 4, :], ml_end) for q in range(2)]
        x3, po_end = post(0, WO2, l_wo2, lambda j: YG[:, j, :] if j < 4 else YM[:, j - 4, :], [ym_d, yg_d], GROW, PLG, PLB, ml_end,
                          [mem(126, [512]), mem(128, [512])])

        OS = [64, 80, 96]
        for kb in OS:
            slots[kb] = Slot(kb)
            slots[kb].used = [po_end, x3]
        HO = mem(32, [8, T])
        FT, FGT, UT, VT = mem(112, [4, 1024]), mem(128, [4, 1024]), mem(144, [4, 1024]), mem(160, [8, 512])
        w_d = A["odd_w_in_2"][0].rearrange("(p c) n -> p c n", c=8)
        wf_, wu_ = [w_chunk(OS[i], w_d[:, :, 512 * c:512 * c + 512], 512) for i, c in enumerate((0, 2))]
        wsg_ = w_chunk(OS[2], w_d[:, :, 2048:2560], 512)
        DFC, SGB, SGW, SGT = mem(192, [256]), mem(193, [512]), mem(195, [4, 128]), mem(197, [4, 128])
        l_dfc = dma(SY, DFC, A["k_small"][:, NC - 256:NC], po_end, x3)
        l_sgb = dma(SY, SGB, A["sgu_b_2"].rearrange("a g t -> a (g t)").broadcast_to([128, 512]), po_end, x3)
        l_sgw = dma(SY, SGW, A["sgu_w_2"][0].rearrange("g t s -> t g s"), po_end, x3)
        tx = token_stats(NT, lambda i: X[:, i, :], x3, False)
        hO = channel_major(NT, lambda i: X[:, i, :], [tx, po_end], True, 176, HO, SCL["l1"], SH["l1"], [po_end])
        b, ps, fr = PB.take()
        for g_ in range(4):
            last = tr(ps[:, 128 * g_:128 * g_ + 128], SGW[:, g_, :], cst("ident"), l_sgw, fr)
        t_sgt = cp(AC, SGT, ps[:, :].rearrange("p (a b) -> p a b", a=4), last, po_end)
        PB.free[b] = t_sgt
        ft_d, fg_d, u_d, v_d = [], [], [], []
        w, lw = wf_
        for j in range(4):
            for half in range(2):
                b, ps, last = proj_cm(w, lw, 128 * j, HO, half, hO)
                d = cp((VE, AC)[half], FT[:, j, 512 * half:512 * half + 512], ps[:, :], last)
                PB.free[b] = d
                ft_d.append(d)
        slots[OS[0]].used = [last]
        wv_ = w_chunk(OS[0], w_d[:, :, 1536:2048], 512)
        w, lw = wu_
        for j in range(4):
            for half in range(2):
                b, ps, last = proj_cm(w, lw, 128 * j, HO, half, hO)
                d = act(UT[:, j, 512 * half:512 * half + 512], ps[:, :], ACT.Gelu, last)
                PB.free[b] = d
                u_d.append(d)
        slots[OS[1]].used = [last]
        wfg_ = w_chunk(OS[1], w_d[:, :, 512:1024], 512)
        VST = mem(184, [32, 6])
        VMV = mem(185, [32, 2])
        VR, VN = mem(185.5, [32]), mem(185.75, [32])
        w, lw = wv_
        vs = None
        for i in range(8):
            b, ps, fr = PB.take()
            for c in range(8):
                last = mm(ps[:, :], HO[:, c, 128 * i:128 * i + 128], w[:, c, :], c == 0, c == 7, fr, lw, hO)
            d = act(VT[:, i, :], ps[:, :], ACT.Gelu, last)
            PB.free[b] = d
            for g_ in range(4):
                n_ = 4 * i + g_
                a = VE(lambda e, n_=n_, i=i, g_=g_: e.bn_stats(VST[:, n_, :], VT[:, i, 128 * g_:128 * g_ + 128]), d, hO)
                vs = VE(lambda e, n_=n_: e.bn_aggr(VMV[:, n_, :], VST[:, n_, :]), a)
        slots[OS[0]].used = [last]
        dft = A["k_dft"]

        def dft_load(kb, part, half):
            dst = mem(kb, [8, 512])
            s = slots[kb]
            m = dma(SY, dst, dft[part].rearrange("(t p) k -> p t k", p=128)[:, :, 512 * half:512 * half + 512], s.used, load=s.load)
            s.used = []
            return dst, m

        dl = {(0, 0): dft_load(OS[0], 0, 0)}
        r = rsq(VR, VMV[:, :, 1], 1, vs)
        nb_ = stt(VN, VMV[:, :, 0], -1.0, VR, MUL, MUL, r)
        for i in range(8):
            for g_ in range(4):
                n_ = 4 * i + g_
                v = VT[:, i, 128 * g_:128 * g_ + 128]
                v_d.append(ts(v, v, VR[:, n_:n_ + 1], VN[:, n_:n_ + 1], MUL, ADD, nb_))
        SGX = [mem(176, [512]), mem(178, [512])]
        sgf = [hO, hO]
        w, lw = wsg_
        us_d = []
        k = 0
        for j in range(4):
            for half in range(2):
                s0 = slice(512 * half, 512 * half + 512)
                b, ps, last = proj_cm(w, lw, 128 * j, HO, half, hO)
                d = act(SGX[k % 2], ps[:, :], ACT.Silu, last, sgf[k % 2])
                PB.free[b] = d
                d = tt(UT[:, j, s0], UT[:, j, s0], SGX[k % 2], MUL, d, u_d)
                sgf[k % 2] = d
                us_d.append(d)
                k += 1
        slots[OS[2]].used = [last]
        dl[(1, 0)] = dft_load(OS[2], 1, 0)
        w, lw = wfg_
        for j in range(4):
            for half in range(2):
                b, ps, last = proj_cm(w, lw, 128 * j, HO, half, hO)
                d = act(FGT[:, j, 512 * half:512 * half + 512], ps[:, :], ACT.Silu, last)
                PB.free[b] = d
                fg_d.append(d)
        slots[OS[1]].used = [last]
        dl[(0, 1)] = dft_load(OS[1], 0, 1)
        ho_end = last
        ys_d = []
        k = 0
        for g_ in range(4):
            for half in range(2):
                s0 = slice(512 * half, 512 * half + 512)
                b, ps, fr = PB.take()
                for q in range(4):
                    i = 4 * half + q
                    last = mm(ps[:, 128 * q:128 * q + 128], VT[:, i, 128 * g_:128 * g_ + 128], SGT[:, g_, :], True, True,
                              v_d, t_sgt, fr)
                bb = SGB[:, 128 * g_:128 * g_ + 128].unsqueeze(1).broadcast_to([128, 4, 128])
                d = tt(SGX[k % 2].rearrange("p (a b) -> p a b", a=4), ps[:, :].rearrange("p (a b) -> p a b", a=4), bb, ADD,
                       last, l_sgb, sgf[k % 2])
                PB.free[b] = d
                d = tt(UT[:, g_, s0], UT[:, g_, s0], SGX[k % 2], MUL, d, us_d)
                sgf[k % 2] = d
                ys_d.append(d)
                k += 1
        AB = mem(32, [8, 1024])
        ab_d = []
        for i in range(8):
            for gg_ in range(2):
                b, ps, fr = PB.take()
                for q in range(2):
                    g_ = 2 * gg_ + q
                    last = mm(ps[:, 256 * q:256 * q + 256], FT[:, g_, 128 * i:128 * i + 128], DFC, True, True, ft_d, l_dfc, fr)
                d = cp((VE, AC)[gg_], AB[:, i, 512 * gg_:512 * gg_ + 512], ps[:, :], last, ho_end)
                PB.free[b] = d
                ab_d.append(d)
        ab_end = last
        yf_d = []
        for half in range(2):
            s0 = slice(512 * half, 512 * half + 512)
            if half == 1:
                slots[OS[2]].used = [f_last]
                slots[OS[0]].used = [f_last]
                dl[(1, 1)] = dft_load(OS[2], 1, 1)
            for g_ in range(4):
                b, ps, fr = PB.take()
                for part in range(2):
                    dst, m = dl[(part, half)]
                    for i in range(8):
                        last = mm(ps[:, :], AB[:, i, 256 * g_ + 128 * part:256 * g_ + 128 * part + 128], dst[:, i, :],
                                  part == 0 and i == 0, part == 1 and i == 7, ab_d, m, fr)
                d = tt(FT[:, g_, s0], ps[:, :], FGT[:, g_, s0], MUL, last, fg_d, ab_end)
                PB.free[b] = d
                yf_d.append(d)
            f_last = last
        WO3 = mem(64, [8, 1024])
        w3v = A["odd_w_out_2"][0].rearrange("(j p) n -> p j n", p=128)
        l_wo3 = [dma(SY, WO3[:, 4 * q:4 * q + 4, :], w3v[:, 4 * q:4 * q + 4, :], f_last, ys_d) for q in range(2)]
        x4, pe4 = post(1, WO3, l_wo3, lambda j: FT[:, j, :] if j < 4 else UT[:, j - 4, :], [yf_d, ys_d],
                       mem(128, [1024]), mem(132, [1024]), mem(136, [1024]), [yf_d, ys_d, f_last], [mem(176, [512]), mem(178, [512])])
        od = out[0].rearrange("(t p) d -> p t d", p=128)

        for i in range(NT):
            stores.append(dma(SY, od[:, i, :], X[:, i, :], x4[i]))
        stores += [y_end, t_yz, t_ada, t_h2[-1], t_ini, t_sc]
        for s in stores:
            SY(lambda e: e.nop(), s)
        for l in lanes:
            l.count()
        block = ctx.enter_context(nc.Block())
        block.sync(SY.emit)
        block.tensor(PE.emit)
        block.scalar(AC.emit)
        block.vector(VE.emit)
        block.gpsimd(GP.emit)


_OUT = ((1, 1024, 1024), "float32")


def kernel(**inputs):
    import numpy as _np
    import concourse.bacc as _bacc
    from concourse import mybir as _mybir
    from concourse.bass_utils import run_bass_kernel_spmd as _run

    nc = _bacc.Bacc("TRN2", target_bir_lowering=False, num_devices=1)
    arrays, aps = {}, {}
    for name, a in {**inputs, **constants()}.items():
        a = _np.ascontiguousarray(a)
        arrays[f"in_{name}_dram"] = a
        aps[name] = nc.dram_tensor(f"in_{name}_dram", a.shape, _mybir.dt.from_np(a.dtype), kind="ExternalInput").ap()
    out = nc.dram_tensor("out_0_dram", _OUT[0], _mybir.dt.from_np(_np.dtype(_OUT[1])), kind="ExternalOutput").ap()
    build(nc, aps, out)
    r = _run(nc, [arrays], core_ids=[0])
    return r.results[0]["out_0_dram"]
```

```python
from contextlib import ExitStack

import concourse.bass as bass
from concourse import mybir

F32 = mybir.dt.float32
F32R = mybir.dt.float32r
I32 = mybir.dt.int32
U32 = mybir.dt.uint32
ALU = mybir.AluOpType
ACT = mybir.ActivationFunctionType
AX = mybir.AxisListType.X
ADD, SUB, MUL, MAX, MIN, POW = ALU.add, ALU.subtract, ALU.mult, ALU.max, ALU.min, ALU.pow
EPS = 1e-6


class Mark:

    def __init__(self, sem):
        self.sem, self.needed, self.value = sem, False, 0


class Landed:

    def __init__(self, sem, value):
        self.sem, self.value = sem, value


def marks(waits):
    if isinstance(waits, (list, tuple)):
        return [m for w in waits for m in marks(w)]
    return [] if waits is None else [waits]


class Lane:

    def __init__(self, nc, name, sem, sem_if):
        self.nc, self.name, self.sems, self.inside = nc, name, (sem, sem_if), False
        self.items = []

    def __call__(self, fn, *waits):
        mark = Mark(self.sems[self.inside])
        flat = marks(waits)
        for w in flat:
            if isinstance(w, Mark):
                w.needed = True
        self.items.append((fn, flat, mark))
        return mark

    def count(self):
        n = {}
        for _, _, mark in self.items:
            if mark.needed:
                n[id(mark.sem)] = mark.value = n.get(id(mark.sem), 0) + 1

    def when(self, flag, *waits):
        self(("when", flag), *waits)
        self.inside = True

    def always(self):
        self(("always", None))
        self.inside = False

    def emit(self, eng):
        seen = {}
        for fn, waits, mark in self.items:
            if isinstance(fn, tuple) and fn[0] == "always":
                branch.__exit__(None, None, None)
                seen = before
                continue
            for w in waits:
                if seen.get(id(w.sem), 0) < w.value:
                    seen[id(w.sem)] = w.value
                    eng.wait_ge(w.sem, w.value)
            if isinstance(fn, tuple):
                branch = eng.If(eng.value_load(fn[1], min_val=0, max_val=15) > 0)
                branch.__enter__()
                before = dict(seen)
                continue
            ins = fn(eng)
            if mark.needed:
                ins.then_inc(mark.sem, 1)


class Load:

    def __init__(self, sem):
        self.sem, self.n = sem, 0

    def __call__(self, lane, out, in_, *waits, **kw):
        self.n += 16
        lane(lambda e: e.dma_start(out, in_, **kw).then_inc(self.sem, 16), *waits)
        return Landed(self.sem, self.n)


class Banks:

    def __init__(self, banks, order):
        self.banks, self.order, self.at, self.free = banks, order, 0, {}

    def take(self):
        b = self.order[self.at % len(self.order)]
        self.at += 1
        return b, self.banks[b], self.free.get(b)

T = 1024
NT = 8
D = 1024
CAP = 128
NEXP = 32
NOV = 15
NBLK = NEXP + NOV
K4 = 256


def constants():
    import numpy as np
    p = np.arange(128)
    s, t = p[:, None], p[None, :]
    same = (s // 64) == (t // 64)
    parts = {
        "ident": s == t, "ones": s + t >= 0, "bd64": same, "ntri": -1.0 * (s >= t), "nones": -1.0 * (s + t >= 0),
        "sltu": s < t, "glaf": same & (s <= t), "glar": same & (s >= t),
    }
    ang = np.arange(128) * 2.0 * np.pi / 128
    c2 = np.arange(128)[:, None] * np.arange(128)[None, :] % 128
    parts["perm"] = (s // 32 == t // 32) & (s % 32 == (t + 16) % 32)
    parts["iota"] = t + 0.0 * s
    parts["tok"] = s + 128.0 * np.arange(8)[None, :]
    parts["eidx"] = 128.0 * t[:, :32] + 0.0 * s
    parts["dftc"] = np.concatenate([np.cos(ang)[c2], np.sin(ang)[c2]], 1)
    inv = np.float32(10000.0) ** (-np.arange(8, dtype=np.float32) / 8)
    n = np.arange(T)
    a = np.concatenate([(n // 64).astype(np.float32)[:, None] * inv, (n % 64).astype(np.float32)[:, None] * inv], 1)
    a = a.astype(np.float32)
    cos, sin = np.cos(a).T, np.sin(a).T
    rope_c = np.tile(np.concatenate([cos, cos]), (4, 1))
    rope_s = np.tile(np.concatenate([-sin, sin]), (4, 1))
    flat = []
    for v in parts.values():
        flat.append(v.astype(np.float32))
    angn = np.arange(T) * 2.0 * np.pi / T
    kn = np.arange(T)[:, None] * np.arange(T)[None, :] % T
    sc = 1.0 / np.sqrt(T * 128.0)
    cn = np.stack([np.cos(angn)[kn] * sc, -np.sin(angn)[kn] * sc])
    return {
        "k_small": np.ascontiguousarray(np.concatenate(flat, 1)),
        "k_rope": np.stack([rope_c, rope_s]).astype(np.float32),
        "k_dft": cn.astype(np.float32),
    }


def build(nc, A, out):
    constants_at = {}
    at = 0
    for name, n in (("ident", 128), ("ones", 128), ("bd64", 128), ("ntri", 128), ("nones", 128),
                    ("sltu", 128), ("glaf", 128), ("glar", 128), ("perm", 128), ("iota", 128), ("tok", 8), ("eidx", 32),
                    ("dftc", 256)):
        constants_at[name] = (at, n)
        at += n
    NC = at
    ctx = ExitStack()
    with ctx:
        MEM = ctx.enter_context(nc.sbuf_tensor("mem", [128, 401 * K4 // 2], F32))
        mem_at = nc.sbuf_base - 401 * K4 * 2
        CS = ctx.enter_context(nc.sbuf_tensor("cst", [128, NC - 256], F32))
        SM = ctx.enter_context(nc.sbuf_tensor("small", [128, 540], F32))
        PSM = ctx.enter_context(nc.psum_tensor("psm", [128, 8, 512], F32))
        banks = [PSM[:, i, :] for i in range(8)]
        nsem = [0]

        def sem(name=None):
            nsem[0] += 1
            return ctx.enter_context(nc.semaphore(name or f"s{nsem[0]}"))

        SY = Lane(nc, "sync", sem("sy"), sem("syi"))
        PE = Lane(nc, "tensor", sem("pe"), sem("pei"))
        AC = Lane(nc, "scalar", sem("ac"), sem("aci"))
        VE = Lane(nc, "vector", sem("ve"), sem("vei"))
        GP = Lane(nc, "gpsimd", sem("gp"), sem("gpi"))
        lanes = [SY, PE, AC, VE, GP]
        stores = []

        def mem(kb, shape, dt=F32, p=128):
            n = 1
            for s in shape:
                n *= s
            o = round(kb * K4)
            ap = MEM[0:p, o:o + n]
            if len(shape) == 2:
                ap = ap.rearrange("p (a b) -> p a b", a=shape[0])
            if len(shape) == 3:
                ap = ap.rearrange("p (a b c) -> p a b c", a=shape[0], b=shape[1])
            return ap

        nr = [0]

        def rounded(kb, n):
            nr[0] += 1
            return nc.alloc_sbuf_tensor_at(f"r{nr[0]}", [128, n], F32R, offset=mem_at + round(kb * 1024))[:, :]

        def cst(name):
            o, n = constants_at[name]
            return CS[:, o:o + n]

        small_at = [0]

        def small(n, dt=F32):
            o = small_at[0]
            small_at[0] += n
            assert small_at[0] <= 540, small_at
            return SM[:, o:o + n]

        def mm(o, l, r, start, stop, *w):
            return PE(lambda e: e.matmul(o, l, r, start=start, stop=stop, skip_group_check=True), *w)

        def tr(o, i, idn, *w):
            return PE(lambda e: e.transpose(o, i, idn), *w)

        def act(o, i, f, *w, **k):
            return AC(lambda e: e.activation(o, i, f, **k), *w)

        def tt(o, a, b, op, *w, lane=None):
            return (lane or VE)(lambda e: e.tensor_tensor(o, a, b, op), *w)

        def ts(o, a, s1, s2, op0, op1, *w, lane=None):
            if op1 is None:
                return (lane or VE)(lambda e: e.tensor_scalar(o, a, s1, None, op0), *w)
            return (lane or VE)(lambda e: e.tensor_scalar(o, a, s1, s2, op0, op1), *w)

        def stt(o, a, s, b, op0, op1, *w):
            return VE(lambda e: e.scalar_tensor_tensor(o, a, s, b, op0, op1), *w)

        def cp(lane, o, i, *w):
            if lane is AC:
                return act(o, i, ACT.Copy, *w)
            return lane(lambda e: e.tensor_copy(o, i), *w)

        def dma(lane, o, i, *w, load=None, **k):
            return (load or Load(sem()))(lane, o, i, *w, **k)

        epsc = small(1)
        t_eps = VE(lambda e: e.memset(epsc, EPS))

        def rsq(o, ss, n, *w):
            a = act(o, ss, ACT.Ln, *w, t_eps, scale=1.0 / n, bias=epsc[0:o.shape[0], 0:1])
            return act(o, o, ACT.Exp, a, scale=-0.5)

        X = mem(0, [NT, D])
        HT = mem(32, [8, T])
        W0, W1, W2 = 64, 80, 96

        l_c = dma(SY, CS[:, :], A["k_small"][:, 0:NC - 256])
        xs = A["x"][0].rearrange("(t p) d -> p t d", p=128)
        xL = [Load(sem()) for _ in range(NT)]
        l_x = [xL[i](SY, X[:, i, :], xs[:, i, :]) for i in range(NT)]

        colL = Load(sem())

        def column(src, n, *w):
            o = small(n)
            return o, dma(GP, o, src, *w, load=colL)

        g1, t_ = column(A["norm1_g"][0].rearrange("(p c) -> p c", c=8), 8)
        gq = small(1)
        gk = small(1)
        for g, nm in ((gq, "q_norm_g"), (gk, "k_norm_g")):
            for h in range(2):
                t_ = dma(GP, g[64 * h:64 * h + 64, :], A[nm][0].rearrange("(p c) -> p c", c=1), load=colL)
        rows = mem(150, [256])
        t_ = dma(GP, rows[0:31, :], A["conf_dw_w"][0], load=colL)
        r = 31
        for nm in ("conf_dw_b", "conf_ln_g", "conf_ln_b", "conf_pw_b"):
            t_ = dma(GP, rows[r:r + 1, :], A[nm], load=colL)
            r += 1
        t_ = dma(GP, rows[35:39, :], A["lru_conv_w"][0], load=colL)
        r = 39
        for nm in ("lru_conv_b", "lru_ba", "lru_bx", "lru_lambda"):
            t_ = dma(GP, rows[r:r + 1, :], A[nm], load=colL)
            r += 1
        t_ = dma(GP, rows[43:47, :], A["out_norm_g"][0].rearrange("(m n) -> m n", m=4), load=colL)
        ct = small(94)
        ctv = ct.rearrange("p (j r) -> p j r", j=2)
        g2, t_ = column(A["norm2_g"][0].rearrange("(p c) -> p c", c=8), 8)
        l_col = t_

        class Slot:
            def __init__(self, kb):
                self.kb, self.load, self.used = kb, Load(sem()), []

        slots = {}

        def fetch(kb, dst, src, *w, lane=None, n=1):
            if kb not in slots:
                slots[kb] = Slot(kb)
            s = slots[kb]
            m = dma(lane or SY, dst, src, list(s.used), *w, load=s.load)
            return m

        w_in = A["w_in"][0].rearrange("(p c) n -> p c n", c=8)
        PB = Banks(banks, [0, 1, 2, 3, 4, 5, 6, 7])

        def row_stats(t, src, w, eps_n, tag, center):
            pass

        st6 = mem(160, [NT, 2, 6])

        def normed(src, i, dst, rs, nb, w, use):
            return None

        def transposed(srcs, dst_of, evac):
            return None

        def stats(src, n, bn, mv, w):
            a = VE(lambda e: e.bn_stats(bn[:, 0:6], src[:, 0:512]), w)
            b = VE(lambda e: e.bn_stats(bn[:, 6:12], src[:, 512:1024]))
            return VE(lambda e: e.bn_aggr(mv, bn[:, 0:12]), a, b)

        class Two:

            def __init__(self, hi, lo, m):
                self.hi, self.lo, self.m = hi, lo, m

        def two_rows(kh, kl, n):
            k = n / 256
            return [rounded(kh + k * c, n) for c in range(8)], [rounded(kl + k * c, n) for c in range(8)]

        parts_at = {}

        def parts(kb):
            if kb not in parts_at:
                parts_at[kb] = [rounded(kb + 4 * i, 1024) for i in range(4)]
            return parts_at[kb]

        class Stream:

            def __init__(self, pieces):
                self.pieces, self.raw, self.two, self.at, self.freed = pieces, [], [], 0, 0
                self.fetch()

            def fetch(self):
                n = len(self.raw)
                if n == len(self.pieces) or self.pieces[n][0] in [p[0] for p in self.pieces[self.freed:n]]:
                    return
                kb, srcs, R, n = self.pieces[len(self.raw)]
                s = slots.setdefault(kb, Slot(kb))
                dst = mem(kb + 8, [R, n])
                for src, o, m in srcs:
                    ld = dma(SY, dst[:, :, o:o + m], src, list(s.used), load=s.load)
                s.used = []
                self.raw.append(ld)
                self.fetch()

            def split(self):
                i = len(self.two)
                if i == len(self.raw):
                    return
                kb, _, R, n = self.pieces[i]
                h0, h1, l0, l1 = parts(kb)
                w = R // 2 * n
                hi, lo, m = [], [], []
                for q, (h, l) in enumerate(((h0, l0), (h1, l1))):
                    src = mem(kb + 8, [R * n])[:, w * q:w * q + w]
                    if w == 1024 or q == 0:
                        lv = l[:, 0:w]
                    else:
                        lv = rounded(kb + 8 + w / 256, w)
                    a = act(h[:, 0:w], src, ACT.Copy, self.raw[i])
                    m.append(tt(lv, src, h[:, 0:w].bitcast(F32), SUB, a, self.raw[i]))
                    for r in range(R // 2):
                        hi.append(h[:, r * n:r * n + n])
                        lo.append(lv[:, r * n:r * n + n])
                self.two.append(Two(hi, lo, m))

            def get(self):
                if len(self.two) == self.at:
                    self.split()
                self.at += 1
                return self.two[self.at - 1]

            def done(self, last):
                slots[self.pieces[self.freed][0]].used = [last]
                self.freed += 1
                self.fetch()

        def mm3(o, l, r, c, ls, rs, first, last, *w):
            mm(o, l.hi[c][:, ls], r.hi[c][:, rs], first, False, *w)
            mm(o, l.hi[c][:, ls], r.lo[c][:, rs], False, False)
            return mm(o, l.lo[c][:, ls], r.hi[c][:, rs], False, last)

        def split_major(n, get, tstat, center, dst, scale, shift, w, tok0=0, at=range(112, 144, 4)):
            tmp = [mem(at[i], [D]) for i in range(n)]
            norm = []
            for i in range(n):
                if i % 2:
                    if center:
                        norm.append(ts(tmp[i], get(i), rs8[:, i:i + 1], nb8[:, i:i + 1], MUL, ADD, tstat))
                    else:
                        norm.append(ts(tmp[i], get(i), rs8[:, i:i + 1], None, MUL, None, tstat))
                elif center:
                    norm.append(act(tmp[i], get(i), ACT.Identity, tstat, scale=rs8[:, i:i + 1], bias=nb8[:, i:i + 1]))
                else:
                    norm.append(act(tmp[i], get(i), ACT.Copy, tstat, scale=rs8[:, i:i + 1]))
            for q in range((n + 3) // 4):
                m = min(4, n - 4 * q)
                for c in range(8):
                    b, ps, fr = PB.take()
                    for j in range(m):
                        last = tr(ps[:, 128 * j:128 * j + 128], tmp[4 * q + j][:, c::8], cst("ident"), norm[4 * q + j], fr, w)
                    s_ = slice(tok0 + 512 * q, tok0 + 512 * q + 128 * m)
                    src, h, l = ps[:, 0:128 * m], dst.hi[c][:, s_], dst.lo[c][:, s_]
                    if shift is None:
                        a = act(h, src, ACT.Copy, last, scale=scale[:, c:c + 1])
                        d = stt(l, src, scale[:, c:c + 1], h.bitcast(F32), MUL, SUB, a, norm)
                    else:
                        if c % 2:
                            a = ts(src, src, scale[:, c:c + 1], shift[:, c:c + 1], MUL, ADD, last)
                        else:
                            a = act(src, src, ACT.Identity, last, scale=scale[:, c:c + 1], bias=shift[:, c:c + 1])
                        a = act(h, src, ACT.Copy, a)
                        d = tt(l, src, h.bitcast(F32), SUB, a, norm)
                    PB.free[b] = d
                    dst.m.append(d)
            return dst.m

        bnb = small(12)
        mv = small(16)
        mvv = mv.rearrange("p (t k) -> p t k", k=2)
        rs8 = small(8)
        nb8 = small(8)
        sq8 = small(8)

        def token_stats(n, get, waits, rms):
            last = None
            for i in range(n):
                last = stats(get(i), 1024, bnb, mvv[:, i, :], [waits[i], last])
            if rms:
                a = tt(sq8[:, 0:n], mvv[:, 0:n, 0], mvv[:, 0:n, 0], MUL, last)
                b = tt(sq8[:, 0:n], sq8[:, 0:n], mvv[:, 0:n, 1], ADD, a)
                c = rsq(rs8[:, 0:n], sq8[:, 0:n], 1, b)
                return c
            c = rsq(rs8[:, 0:n], mvv[:, 0:n, 1], 1, last)
            return stt(nb8[:, 0:n], mvv[:, 0:n, 0], -1.0, rs8[:, 0:n], MUL, MUL, c)

        def channel_major(n, get, tstat, center, tmpkb, dst, scale, shift, w, tok0=0, on_norm=None):
            done = []
            free = [None, None]
            for q in range((n + 3) // 4):
                m = min(4, n - 4 * q)
                tmp = [mem(tmpkb + 4 * j, [D]) for j in range(4)]
                norm = []
                for j in range(m):
                    i = 4 * q + j
                    if center:
                        f = ACT.Identity
                        k = dict(scale=rs8[:, i:i + 1], bias=nb8[:, i:i + 1])
                    else:
                        f, k = ACT.Copy, dict(scale=rs8[:, i:i + 1])
                    if j % 2:
                        if center:
                            norm.append(ts(tmp[j], get(i), rs8[:, i:i + 1], nb8[:, i:i + 1], MUL, ADD, tstat, free[0]))
                        else:
                            norm.append(ts(tmp[j], get(i), rs8[:, i:i + 1], None, MUL, None, tstat, free[0]))
                    else:
                        norm.append(act(tmp[j], get(i), f, tstat, free[0], **k))
                    kept = on_norm(i, tmp[j], norm[-1]) if on_norm else None
                last = None
                for c in range(8):
                    b, ps, fr = PB.take()
                    for j in range(m):
                        last = tr(ps[:, 128 * j:128 * j + 128], tmp[j][:, c::8], cst("ident"), norm[j], fr, w)
                    o = dst[:, c, tok0 + 512 * q:tok0 + 512 * q + 128 * m]
                    src = ps[:, 0:128 * m]
                    if c % 2:
                        if shift is None:
                            d = ts(o, src, scale[:, c:c + 1], None, MUL, None, last)
                        else:
                            d = ts(o, src, scale[:, c:c + 1], shift[:, c:c + 1], MUL, ADD, last)
                    else:
                        kw = dict(scale=scale[:, c:c + 1])
                        if shift is not None:
                            kw["bias"] = shift[:, c:c + 1]
                        d = act(o, src, ACT.Identity if shift is not None else ACT.Copy, last, **kw)
                    PB.free[b] = d
                    done.append(d)
                free[0] = [last, kept]
            return done

        for j in range(2):
            last = tr(banks[7][:, 47 * j:47 * j + 47], rows[0:47, 128 * j:128 * j + 128],
                      cst("ident")[0:47, 0:47], l_c, l_col)
        l_ct = cp(VE, ct, banks[7][:, 0:94], last)
        PB.free[7] = l_ct

        def tap(j, r):
            return ctv[:, j, r:r + 1]

        CDB, CLG, CLB, CPB, LCW, LCB, LBA, LBX, LAM, ONG = 31, 32, 33, 34, 35, 39, 40, 41, 42, 43
        tx = token_stats(NT, lambda i: X[:, i, :], l_x, True)
        HT2 = Two(*two_rows(32, 0, T), [])
        hT = split_major(NT, lambda i: X[:, i, :], tx, False, HT2, g1, None, [l_c, l_col, l_ct])

        QK = mem(112, [8, T])
        V = mem(144, [NT, 512])
        XRP = mem(160, [2, 1027])
        XG = mem(168.25, [2, 1024])
        UP = mem(176.25, [2, 1054])
        TB = 184.5

        CSQ = [small(1), small(1)]
        c1 = ts(CSQ[0], gq, 0.125, None, MUL, None, l_col)
        c2 = ts(CSQ[1], gk, 1.0, None, MUL, None, l_col)
        z1 = GP(lambda e: e.memset(XRP[:, :, 0:3], 0.0))
        z2 = GP(lambda e: e.memset(UP[:, :, 0:30], 0.0))

        gw = mem(TB + 12, [4, 128])
        zg = GP(lambda e: e.memset(gw, 0.0))
        gwl = Load(sem())
        for gi, nm in enumerate(("lru_wa", "lru_wx")):
            for n in range(4):
                q = 64 * (n % 2)
                l_gw = dma(GP, gw[q:q + 64, 2 * gi + n // 2, q:q + 64], A[nm][0][n], zg, load=gwl)

        def w_load(kb, src, *w, cols=512):
            dst = mem(kb, [8, 512])[:, :, 0:cols]
            s = slots.setdefault(kb, Slot(kb))
            m = dma(SY, dst, src, list(s.used), *w, load=s.load)
            s.used = []
            return dst, m

        def proj_cm(w, lw, col, src, half, hw, m=128, n=512, tok=None):
            b, ps, fr = PB.take()
            t0 = 512 * half if tok is None else tok
            for c in range(8):
                last = mm(ps[0:m, 0:n], w[:, c, col:col + m], src[:, c, t0:t0 + n], c == 0, c == 7, fr, lw, hw)
            return b, ps, last

        def proj3(w, col, src, half, m=128, n=512, tok=None):
            b, ps, fr = PB.take()
            t0 = 512 * half if tok is None else tok
            for c in range(8):
                last = mm3(ps[0:m, 0:n], w, src, c, slice(col, col + m), slice(t0, t0 + n), c == 0, c == 7, fr, w.m, src.m)
            return b, ps, last

        def piece(kb, src, col, n=256):
            return kb, [(src[:, :, col:col + n], 0, n)], 8, n

        def wide(k0, k1, src, col):
            return [(kb, [(src[:, 4 * q:4 * q + 4, col:col + 512], 0, 512)], 4, 512) for q, kb in enumerate((k0, k1))]

        def joined(a, b):
            return Two(a.hi + b.hi, a.lo + b.lo, a.m + b.m)

        conf_w = [(kb, [(w_in[:, :, 2048 + 128 * j:2176 + 128 * j], 0, 128),
                        (w_in[:, :, 2304 + 128 * j:2432 + 128 * j], 128, 128)], 8, 256) for j, kb in ((0, W0), (1, W1))]
        WS = Stream([piece(W0, w_in, 1536), piece(W1, w_in, 1792)] + conf_w +
                    [piece((W0, W1)[q % 2], w_in, 256 * q) for q in range(4)] + wide(W2, W0, w_in, 1024))
        WS.split()
        sigb = [mem(TB, [512]), mem(TB + 2, [512])]
        lru_in, xg_in, up_in = [], [], []
        for j in range(4):
            if j % 2 == 0:
                w = WS.get()
            for half in range(2):
                b, ps, last = proj3(w, 128 * (j % 2), HT2, half)
                t0 = 512 * half
                if j < 2:
                    d = cp(VE, XRP[:, j, 3 + t0:3 + t0 + 512], ps[:, :], last)
                    lru_in.append(d)
                else:
                    d = act(XG[:, j - 2, t0:t0 + 512], ps[:, :], ACT.Gelu_apprx_tanh, last)
                    xg_in.append(d)
                PB.free[b] = d
            if j % 2 == 0:
                WS.split()
            else:
                WS.done(last)
        sfree = [None, None]
        k = 0
        for j in range(2):
            w = WS.get()
            for half in range(2):
                t0 = 512 * half
                bg, psg, lg = proj3(w, 128, HT2, half)
                sg = act(sigb[k % 2], psg[:, :], ACT.Sigmoid, lg, sfree[k % 2])
                PB.free[bg] = sg
                bv, psv, lv = proj3(w, 0, HT2, half)
                d = tt(UP[:, j, 30 + t0:30 + t0 + 512], psv[:, :], sigb[k % 2], MUL, lv, sg)
                PB.free[bv] = sfree[k % 2] = d
                up_in.append(d)
                k += 1
                if half == 0:
                    WS.split()
            WS.done(lv)
        XR0 = mem(160, [1024])
        YB = XG
        YC = mem(176.25, [2, 1024])
        br = {}

        def lru():
            la8, la8n, lt1, lt2 = small(2), small(2), small(2), small(2)
            lamc = ctv[:, :, LAM]
            a = act(lt1, lamc, ACT.Abs, l_ct)
            a = act(lt1, lt1, ACT.Exp, a, scale=-1.0)
            a = act(lt1, lt1, ACT.Ln, a, bias=1.0)
            b = ts(lt2, lamc, -1.0, 0.0, MUL, MAX, l_ct)
            a = tt(lt1, lt1, lt2, ADD, a, b)
            t_lan = ts(la8n, lt1, 8.0, None, MUL, None, a)
            t_la = ts(la8, lt1, -8.0, None, MUL, None, a)
            LX = [mem(W2, [1024]), mem(W2 + 4, [1024])]
            LA, LI, LTM = mem(W2 + 8, [1024]), mem(W2 + 12, [1024]), mem(TB + 14, [512])
            xconv = []
            for j in range(2):
                d = ts(LX[j], XRP[:, j, 3:1027], tap(j, LCW + 3), tap(j, LCB), MUL, ADD, lru_in, z1)
                for i in range(3):
                    d = stt(LX[j], XRP[:, j, i:i + 1024], tap(j, LCW + i), LX[j], MUL, ADD, d)
                xconv.append(d)
                yield
            lrf = gf = None
            done = []
            for j in range(2):
                LT = XRP[:, j, 0:1024]
                ends = []
                for half in range(2):
                    s0 = slice(512 * half, 512 * half + 512)
                    b1, ps1, f1 = PB.take()
                    m1 = mm(ps1[:, :], gw[:, j, :], LX[j][:, s0], True, True, l_gw, xconv[j], f1)
                    r = act(LA[:, s0], ps1[:, :], ACT.Sigmoid, m1, lrf, bias=tap(j, LBA))
                    PB.free[b1] = r
                    b2, ps2, f2 = PB.take()
                    m2 = mm(ps2[:, :], gw[:, 2 + j, :], LX[j][:, s0], True, True, f2)
                    g = act(LI[:, s0], ps2[:, :], ACT.Sigmoid, m2, lrf, bias=tap(j, LBX))
                    PB.free[b2] = g
                    ends += [r, g]
                t1 = act(LT, LA, ACT.Tanh, ends, t_lan, xconv, scale=la8n[:, j:j + 1])
                t2 = act(LA, LA, ACT.Exp, t1, t_la, scale=la8[:, j:j + 1])
                yield
                for half in range(2):
                    s0 = slice(512 * half, 512 * half + 512)
                    d = ts(LTM, LT[:, s0], 1.0, None, ADD, None, t1, gf)
                    d = VE(lambda e: e.reciprocal(LTM, LTM), d)
                    gf = d = stt(LT[:, s0], LT[:, s0], 2.0, LTM, MUL, MUL, d)
                    yield
                d = act(LT, LT, ACT.Sqrt, d)
                yield
                d = tt(LT, LT, LI, MUL, d)
                d = tt(LT, LT, LX[j], MUL, d)
                yield
                d = VE(lambda e, LT=LT: e.tensor_tensor_scan(LI, LA, LT, 0.0, MUL, ADD), d, t2)
                lrf = tt(YB[:, j, :], LI, XG[:, j, :], MUL, d, xg_in)
                done.append(lrf)
                yield
            br["yb"] = done
            br["lru_end"] = [done[-1], m1, m2]

        def conformer():
            CA, CQ, CR = mem(TB, [2, 1024]), mem(TB + 8, [2, 512]), mem(TB + 12, [512])
            pw = mem(TB + 14, [2, 256])
            o = mem(144, [1024])
            d = ts(o, UP[:, 0, 30:1054], tap(0, 30), tap(0, CDB), MUL, ADD, up_in, z2)
            for i in range(29):
                yield
                d = stt(o, UP[:, 0, i:i + 1024], tap(0, i), o, MUL, ADD, d)
            yield
            cc = [stt(CA[:, 0, :], UP[:, 0, 29:1053], tap(0, 29), o, MUL, ADD, d, br["qk_end"])]
            br["moved"] = cc[0]
            yield
            l_pw = dma(GP, pw, A["conf_pw_w"][0].rearrange("(j p) e -> p j e", p=128), br["qk_end"])
            ends = []
            for half in range(2):
                o = CA[:, 1, 512 * half:512 * half + 512]
                u = UP[:, 1, 512 * half:512 * half + 542]
                d = ts(o, u[:, 30:542], tap(1, 30), tap(1, CDB), MUL, ADD, up_in, z2, br["qk_end"])
                for i in range(30):
                    yield
                    d = stt(o, u[:, i:i + 512], tap(1, i), o, MUL, ADD, d)
                ends.append(d)
            cc.append(ends)
            yield
            cf = None
            done = []
            take = br["banks"].take
            freed = br["banks"].free
            for half in range(2):
                s0 = slice(512 * half, 512 * half + 512)
                b, cb, free = take()
                mm(cb[:, :], cst("ones"), CA[:, 0, s0], True, False, cc, free)
                m1 = mm(cb[:, :], cst("ones"), CA[:, 1, s0], False, True)
                yield
                freed[b] = xc = [stt(CA[:, j, s0], cb[:, :], -1.0 / 256, CA[:, j, s0], MUL, ADD, m1) for j in range(2)]
                yield
                sq = [act(CQ[:, j, :], CA[:, j, s0], ACT.Square, xc[j], cf) for j in range(2)]
                yield
                b, cb, free = take()
                mm(cb[:, :], cst("ones"), CQ[:, 0, :], True, False, sq[0], free)
                m2 = mm(cb[:, :], cst("ones"), CQ[:, 1, :], False, True, sq[1])
                yield
                freed[b] = r = rsq(CR, cb[:, :], 256, m2, cf)
                yield
                sl = []
                for j in range(2):
                    d = tt(CA[:, j, s0], CA[:, j, s0], CR, MUL, r)
                    d = ts(CA[:, j, s0], CA[:, j, s0], tap(j, CLG), tap(j, CLB), MUL, ADD, d)
                    yield
                    a = act(CQ[:, j, :], CA[:, j, s0], ACT.Exp, d, m2, scale=-1.0)
                    yield
                    a = ts(CQ[:, j, :], CQ[:, j, :], 1.0, None, ADD, None, a)
                    a = VE(lambda e, j=j: e.reciprocal(CQ[:, j, :], CQ[:, j, :]), a)
                    sl.append(tt(CA[:, j, s0], CA[:, j, s0], CQ[:, j, :], MUL, a))
                    yield
                for j in range(2):
                    b, cb, free = take()
                    mm(cb[:, :], pw[:, 0, 128 * j:128 * j + 128], CA[:, 0, s0], True, False, sl, l_pw, free)
                    m3 = mm(cb[:, :], pw[:, 1, 128 * j:128 * j + 128], CA[:, 1, s0], False, True)
                    yield
                    freed[b] = d = act(YC[:, j, s0], cb[:, :], ACT.Identity, m3, cc, bias=tap(j, CPB))
                    done.append(d)
                    yield
                cf = [sl, m2]
            br["yc"] = done
            br["end"] = [m3, d]

        def run(steps, n=1):
            for _ in range(n):
                next(steps, None)

        branch = lru()
        conf = conformer()
        sqb = [mem(TB + 4, [512]), mem(TB + 6, [512])]
        rb = [mem(TB + 8, [512]), mem(TB + 10, [512])]
        qk_done = {}
        sqf, rf = [None, None], [None, None]
        pend = None
        k = 0

        def qk_tail(p):
            e, half, b, ps, sq, k = p
            b2, ps2, fr2 = PB.take()
            m2 = mm(ps2[:, :], cst("bd64"), sqb[k % 2], True, True, sq, fr2)
            sqf[k % 2] = m2
            r = rsq(rb[k % 2], ps2[:, :], 64, m2, rf[k % 2])
            PB.free[b2] = r
            d = stt(QK[:, e, 512 * half:512 * half + 512], ps[:, :], CSQ[e // 4][:, 0:1], rb[k % 2], MUL, MUL, r, c1, c2)
            rf[k % 2] = d
            PB.free[b] = d
            qk_done[(e, half)] = d

        for e in range(8):
            if e % 2 == 0:
                w = WS.get()
            for half in range(2):
                b, ps, last = proj3(w, 128 * (e % 2), HT2, half)
                sq = act(sqb[k % 2], ps[:, :], ACT.Square, last, sqf[k % 2])
                if pend:
                    qk_tail(pend)
                run(conf, k < 14)
                run(branch)
                run(conf, k < 14)
                run(branch)
                pend = (e, half, b, ps, sq, k)
                k += 1
            if e % 2 == 0:
                WS.split()
            else:
                if e == 3:
                    run(branch, 100)
                    slots[W2] = Slot(W2)
                    slots[W2].used = [br["yb"], br["lru_end"]]
                WS.done(last)
        qk_tail(pend)
        run(branch, 100)
        br["qk_end"] = [list(qk_done.values()), sqf]
        while "moved" not in br:
            run(conf, 1)
        yb_done = br["yb"]
        a, b = WS.get(), WS.get()
        w = joined(a, b)
        v_done = []
        for i in range(NT):
            b, ps, fr = PB.take()
            for c in range(8):
                last = mm3(ps[:, :], HT2, w, c, slice(128 * i, 128 * i + 128), slice(0, 512), c == 0, c == 7, fr, hT, w.m)
            d = cp(AC, V[:, i, :], ps[:, :], last, br["moved"])
            PB.free[b] = d
            v_done.append(d)
        WS.done(last)
        WS.done(last)
        ht_free = last
        YT = HT
        PT1 = [mem(48 + 2 * i, [512]) for i in range(2)]
        PSP = [mem(52 + 2 * i, [512]) for i in range(3)]
        PW_ = [mem(58 + 2 * i, [512]) for i in range(3)]
        PRS = [mem(160 + 2 * i, [512]) for i in range(4)]
        items = [(hp, qc, kb, h) for hp in range(4) for qc in range(2) for kb in range(4 * qc + 3, -1, -1)
                 for h in (2 * hp, 2 * hp + 1)]
        att_w = [br["lru_end"], yb_done, list(qk_done.values()), ht_free]
        br["banks"] = AZ = Banks(banks, [0, 1, 2, 3, 4, 5])
        AZ.free = dict(PB.free)
        z_, sp_, w_, lane_r = {}, {}, {}, {}
        t1f, spf, wf = [att_w] * 2, [att_w] * 3, [att_w] * 3
        rsum = {}
        ya_done = []
        ofree = [PB.free.get(6), PB.free.get(7)]
        rf_ = [att_w] * 4

        def ext(i):
            hp, qc, kb, h = items[i]
            lo = max(0, kb - 4 * qc) * 128
            return hp, qc, kb, h, lo

        def stage_z(i):
            hp, qc, kb, h, lo = ext(i)
            b, ps, fr = AZ.take()
            q0 = 64 * (h % 2)
            m = mm(ps[:, lo:512], QK[q0:q0 + 64, 4 + hp, 128 * kb:128 * kb + 128],
                   QK[q0:q0 + 64, hp, 512 * qc + lo:512 * qc + 512], True, True, fr, att_w if i < 6 else None)
            z_[i] = (b, ps, m)

        def stage_sp(i):
            hp, qc, kb, h, lo = ext(i)
            b, ps, m = z_[i]
            k = i % 2
            t1 = act(PT1[k][:, lo:], ps[:, lo:512], ACT.Abs, m, t1f[k])
            t2 = act(PT1[k][:, lo:], PT1[k][:, lo:], ACT.Exp, t1, scale=-1.0)
            t3 = act(PT1[k][:, lo:], PT1[k][:, lo:], ACT.Ln, t2, bias=1.0)
            j = i % 3
            d = stt(PSP[j][:, lo:], ps[:, lo:512], 0.0, PT1[k][:, lo:], MAX, ADD, t3, spf[j])
            t1f[k] = d
            if kb >= 4 * qc:
                v = PSP[j][:, lo:lo + 128]
                d = GP(lambda e: e.affine_select(out=v, in_=v, compare_op=ALU.is_gt, fill=0.0, base=0,
                                                 pattern=[[1, 128]], channel_multiplier=-1), d)
            sp_[i] = d

        def stage_c(i):
            hp, qc, kb, h, lo = ext(i)
            b, ps, m = z_[i]
            k = i % 3
            top = 4 * qc + 3
            m = mm(ps[:, lo:512], cst("ntri"), PSP[k][:, lo:], False, kb == top, sp_[i])
            rk = 2 * (qc % 2) + h % 2
            R = PRS[rk]
            if kb < top:
                prev = max(0, kb + 1 - 4 * qc) * 128
                m = mm(ps[:, prev:512], cst("nones"), R[:, prev:], False, True, rsum[rk])
            if kb > 0:
                if kb == top:
                    if lo > 0:
                        GP(lambda e: e.memset(R[:, 0:lo], 0.0), rf_[rk])
                    g = cp(GP, R[:, lo:], PSP[k][:, lo:], sp_[i], rf_[rk], m)
                    rsum[rk] = g
                else:
                    g = tt(R[:, lo:], R[:, lo:], PSP[k][:, lo:], ADD, m, sp_[i], rsum[rk], lane=GP)
                    rsum[rk] = g
                spf[k] = [m, g]
            else:
                rf_[rk] = m
                spf[k] = m
            w = act(PW_[k][:, lo:], ps[:, lo:512], ACT.Exp, m, wf[k])
            AZ.free[b] = w
            if kb >= 4 * qc:
                v = PW_[k][:, lo:lo + 128]
                w = GP(lambda e: e.affine_select(out=v, in_=v, compare_op=ALU.is_gt, fill=0.0, base=0,
                                                 pattern=[[1, 128]], channel_multiplier=-1), w)
            w_[i] = w

        def stage_pv(i):
            hp, qc, kb, h, lo = ext(i)
            k = i % 3
            ob = banks[6 + qc % 2]
            q0 = 64 * (h % 2)
            top = 4 * qc + 3
            m = mm(ob[q0:q0 + 64, lo:512], V[:, kb, 64 * h:64 * h + 64], PW_[k][:, lo:], kb == top, kb == 0,
                   w_[i], v_done, ofree[qc % 2] if kb == top else None)
            wf[k] = m
            if kb == 0:
                d = cp(VE, YT[q0:q0 + 64, hp, 512 * qc:512 * qc + 512], ob[q0:q0 + 64, :], m, ht_free)
                ofree[qc % 2] = [ofree[qc % 2], d] if h % 2 else d
                ya_done.append(d)

        zrow = mem(W2 + 12, [512])
        tz0 = GP(lambda e: e.memset(zrow, 0.0), att_w)
        ysl = nc.dram_tensor("ysl", [NBLK * 128, D], F32).ap()
        yzl = Load(sem())
        for b in range(NEXP, NBLK):
            t_yz = dma(SY, ysl[128 * b:128 * b + 128, :].rearrange("p (q n) -> p q n", q=2),
                       zrow.unsqueeze(1).broadcast_to([128, 2, 512]), tz0, load=yzl)
        l_xr = [xL[i](SY, X[:, i, :], xs[:, i, :], ht_free) for i in range(NT)]
        LAG1, LAG2 = 3, 5
        AC(lambda e: e.preload_act_table_set("natural_log_exp_and_others"))
        n = len(items)
        for s in range(n + LAG2):
            if s < n:
                stage_z(s)
                stage_sp(s)
            run(conf, 1)
            if 0 <= s - LAG1 + 1 < n:
                stage_c(s - LAG1 + 1)
            if 0 <= s - LAG2 + 1 < n:
                stage_pv(s - LAG2 + 1)
            run(conf, 1)
        run(conf, 100)
        yc_done = br["yc"]
        for b in range(6):
            PB.free[b] = AZ.free.get(b)
        PB.free[6], PB.free[7] = ofree

        w_o = A["w_out"][0].rearrange("(j p) n -> p j n", p=128)
        WO = mem(W0, [8, 1024])
        l_wo = []
        for q in range(2):
            s = slots[(W0, W1)[q]]
            l_wo.append(dma(SY, WO[:, 4 * q:4 * q + 4, :], w_o[:, 4 * q:4 * q + 4, :], s.used, load=s.load))
            s.used = []
        att_end = ya_done[-1]

        def yt(j):
            return YT[:, j, :] if j < 4 else YB[:, j - 4, :] if j < 6 else YC[:, j - 6, :]

        NSQ = [mem(112 + 2 * i, [512]) for i in range(4)]
        NR = [mem(120, [512]), mem(122, [512])]
        nf, nrf = [None] * 4, [None] * 2
        yn = []
        k = 0
        for half in range(2):
            s0 = slice(512 * half, 512 * half + 512)
            for (j0, j1, dn) in ((4, 6, yb_done), (6, 8, yc_done), (0, 4, ya_done)):
                b, ps, fr = PB.take()
                for j in range(j0, j1):
                    q = act(NSQ[k % 4], yt(j)[:, s0], ACT.Square, dn, att_end, nf[k % 4])
                    last = mm(ps[:, :], cst("ones"), NSQ[k % 4], j == j0, j == j1 - 1, q, fr)
                    nf[k % 4] = last
                    k += 1
                r = rsq(NR[half], ps[:, :], 128 * (j1 - j0), last, nrf[half])
                PB.free[b] = r
                for j in range(j0, j1):
                    d = stt(yt(j)[:, s0], yt(j)[:, s0], ctv[:, j % 2, ONG + j // 2:ONG + j // 2 + 1], NR[half], MUL, MUL, r)
                nrf[half] = d
                yn.append(d)
        x1 = []
        for i in range(NT):
            for q in range(2):
                b, ps, fr = PB.take()
                for j in range(8):
                    last = mm(ps[:, :], yt(j)[:, 128 * i:128 * i + 128], WO[:, j, 512 * q:512 * q + 512],
                              j == 0, j == 7, fr, l_wo, yn[0:3] if i < 4 else yn[3:6])
                d = tt(X[:, i, 512 * q:512 * q + 512], ps[:, :], X[:, i, 512 * q:512 * q + 512], ADD, last, l_xr)
                PB.free[b] = d
            x1.append(d)
        slots[W0].used = slots[W1].used = [last]
        yt_free = last

        ada_d = nc.dram_tensor("ada_d", [2, 2, 3072], F32).ap()
        cnd = small(16)
        SCND = small(16)
        cl = Load(sem())
        dma(GP, cnd[:, 0:8], A["c_2"][0].rearrange("(p c) -> p c", c=8), load=cl)
        t_cl = dma(GP, cnd[:, 8:16], A["c_ctx_2"].rearrange("(p c) -> p c", c=8), load=cl)
        t_scnd = act(SCND, cnd, ACT.Silu, t_cl)
        sc2 = SCND.rearrange("p (m c) -> p c m", m=2)
        ARW = [mem(192, [512], p=2), mem(194, [512], p=2)]
        ABI = [mem(196, [512], p=2), mem(198, [512], p=2)]
        aw_l = [Load(sem()), Load(sem())]
        ab_l = [Load(sem()), Load(sem())]
        as_l = [Load(sem()), Load(sem())]
        asf, abf = [att_end, att_end], [att_end, att_end]
        t_ada = [None, None]
        ada_w = {}
        ADA_AT = [(W0, W1), (112, 128)]

        def ada_load(n):
            l, ch, k = n // 6, n % 6, n % 2
            kb = ADA_AT[l][k]
            dst, m = w_load(kb, A["ada_w_2"][l].rearrange("(p c) n -> p c n", c=8)[:, :, 512 * ch:512 * ch + 512])
            bi = dma(SY, ABI[k], A["ada_b_2"][l:l + 1, 512 * ch:512 * ch + 512].broadcast_to([2, 512]), abf[k], load=ab_l[k])
            ada_w[n] = (dst, m, bi)

        def ada_chunk(n):
            l, ch, k = n // 6, n % 6, n % 2
            dst, m, bi = ada_w[n]
            b, ps, fr = PB.take()
            for c in range(8):
                last = mm(ps[0:2, :], sc2[:, c, :], dst[:, c, :], c == 0, c == 7, fr, t_scnd, m)
            slots[ADA_AT[l][k]].used = [last]
            d = tt(ARW[k], ps[0:2, :], ABI[k], ADD, last, bi, asf[k])
            PB.free[b] = d
            abf[k] = d
            t_ada[k] = asf[k] = dma(SY, ada_d[l, :, 512 * ch:512 * ch + 512], ARW[k], d, load=as_l[k])


        def ada_chunks(n0, n1):
            for n in range(n0, n1):
                if n % 6 == 0:
                    ada_load(n)
                    ada_load(n + 1)
                ada_chunk(n)
                if n % 6 < 4:
                    ada_load(n + 2)

        h2d = nc.dram_tensor("h2d", [T + 1, D], F32).ap()
        std = nc.dram_tensor("std", [NBLK * 128, 1], I32).ap()
        H2T = mem(128, [8, T])
        WR = mem(33, [8, 36])
        zr = mem(56, [1024], p=1)
        l_wr = Load(sem())
        dma(SY, WR[:, :, 0:4], A["router_coarse"][0].rearrange("(p c) g -> p c g", c=8), yt_free, load=l_wr)
        t_wr = dma(SY, WR[:, :, 4:36], A["router_fine"][0].rearrange("(p c) g -> p c g", c=8), load=l_wr)
        d = VE(lambda e: e.memset(zr, 0.0), yt_free)
        h2_st = Load(sem())
        t_h2 = [dma(AC, h2d[T:T + 1, :], zr, d, load=h2_st)]
        tx = token_stats(NT, lambda i: X[:, i, :], x1, True)

        def keep_row(i, tmp, norm):
            t_h2.append(dma(AC, h2d[128 * i:128 * i + 128, :], tmp, norm, load=h2_st))
            return t_h2[-1]

        h2T = channel_major(NT, lambda i: X[:, i, :], [tx, yn[-1], att_end], False, 112, H2T, g2, None, [], on_norm=keep_row)
        b, ps, fr = PB.take()
        for i in range(NT):
            for c in range(8):
                last = mm(ps[:, 36 * i:36 * i + 36], H2T[:, c, 128 * i:128 * i + 128], WR[:, c, :], c == 0, c == 7,
                          fr, t_wr, h2T)
        lg_end = last
        ada_chunks(0, 4)
        rt_at = [34.5]

        def tmp(*shape):
            n = 1
            for s in shape:
                n *= s
            ap = mem(rt_at[0], list(shape))
            rt_at[0] += n / 256
            return ap

        L = tmp(8, 36)
        d = cp(VE, L, ps[:, 0:288].rearrange("p (a b) -> p a b", a=8), last)
        PB.free[b] = d
        LC, LF = L[:, :, 0:4], L[:, :, 4:36]
        i4 = cst("iota")[:, 0:4].unsqueeze(1).broadcast_to([128, 8, 4])
        i32_ = cst("iota")[:, 0:32].unsqueeze(1).broadcast_to([128, 8, 32])

        def bc(v, n):
            return v.unsqueeze(2).broadcast_to([128, 8, n])

        def red(o, i, op, *w):
            return VE(lambda e: e.tensor_reduce(o, i, AX, op), *w)

        def onehot(o, i, v, n, iota, *w):
            idx = tmp(8)
            a = tt(o, i, bc(v, n), ALU.is_equal, *w)
            a = ts(o, o, -64.0, 64.0, MUL, ADD, a)
            a = tt(o, o, iota, ADD, a)
            a = red(idx, o, MIN, a)
            return tt(o, iota, bc(idx, n), ALU.is_equal, a)

        mc, ec, oc, sc, wg_ = tmp(8), tmp(8, 4), tmp(8, 4), tmp(8), tmp(8)
        a = red(mc, LC, MAX, d)
        b_ = tt(ec, LC, bc(mc, 4), SUB, a)
        b_ = act(ec, ec, ACT.Exp, b_)
        b_ = red(sc, ec, ADD, b_)
        t_wg = VE(lambda e: e.reciprocal(wg_, sc), b_)
        a = onehot(oc, LC, mc, 4, i4, a)
        mask, pen, LM = tmp(8, 32), tmp(8, 32), tmp(8, 32)
        a = cp(VE, mask.rearrange("p a (g e) -> p a g e", g=4), oc.unsqueeze(3).broadcast_to([128, 8, 4, 8]), a)
        a1 = ts(pen, mask, -1.0, 1e30, ADD, MUL, a)
        a = tt(LM, LF, mask, MUL, a)
        a = tt(LM, LM, pen, ADD, a, a1)
        m1, m2, o1, o2 = tmp(8), tmp(8), tmp(8, 32), tmp(8, 32)
        d1 = red(m1, LM, MAX, a)
        a = onehot(o1, LM, m1, 32, i32_, d1)
        a1 = ts(pen, o1, -1e30, None, MUL, None, a)
        a1 = tt(LM, LM, pen, ADD, a1)
        d2 = red(m2, LM, MAX, a1)
        a2 = onehot(o2, LM, m2, 32, i32_, d2)
        G1 = small(8)
        G2 = small(8)
        e2, s2 = tmp(8), tmp(8)
        a3 = tt(e2, m2, m1, SUB, d2)
        a3 = act(e2, e2, ACT.Exp, a3)
        a3 = ts(s2, e2, 1.0, None, ADD, None, a3)
        a3 = VE(lambda e: e.reciprocal(s2, s2), a3)
        a3 = tt(G1, s2, wg_, MUL, a3, t_wg)
        t_g = tt(G2, G1, e2, MUL, a3)
        OO = tmp(8, 32)
        PR = tmp(8, 32)
        a = tt(OO, o1, o2, ADD, a2)
        z_a = VE(lambda e: e.memset(PR[:, 0, :], 0.0), a)
        pr = z_a
        for i in range(1, 8):
            pr = tt(PR[:, i, :], PR[:, i - 1, :], OO[:, i - 1, :], ADD, pr)
        TOT = tmp(32)
        pr2 = tt(TOT, PR[:, 7, :], OO[:, 7, :], ADD, pr)
        b, ps, fr = PB.take()
        mm(ps[:, 0:256], cst("sltu"), OO.rearrange("p a b -> p (a b)"), True, False, a, fr)
        last = mm(ps[:, 0:256], cst("ones"), PR.rearrange("p a b -> p (a b)"), False, True, pr)
        b2, ps2, fr2 = PB.take()
        last2 = mm(ps2[:, 0:32], cst("ones"), TOT, True, True, pr2, fr2)
        NV, NVI, TMPV = tmp(32), tmp(32), tmp(32)
        CN = tmp(32)
        d = cp(VE, CN, ps2[:, 0:32], last2)
        PB.free[b2] = d
        a = ts(NV, CN, float(CAP), None, ALU.is_gt, None, d)
        for k in range(2, 8):
            a = stt(NV, CN, float(CAP * k), NV, ALU.is_gt, ADD, a)
        ON = tmp(32)
        o_ = VE(lambda e: e.memset(ON, 1.0))
        a = VE(lambda e: e.tensor_tensor_scan(NVI, ON, NV, 0.0, MUL, ADD), a, o_)
        BO = tmp(32)
        c = tt(BO, NVI, NV, SUB, a)
        c = ts(BO, BO, 31.0, 128.0, ADD, MUL, c)
        c = tt(BO, BO, cst("eidx"), SUB, c)
        PO = tmp(8, 32)
        OV = tmp(8, 32)
        d = cp(VE, PO, ps[:, 0:256].rearrange("p (a b) -> p a b", a=8), last)
        PB.free[b] = d
        e_ = ts(OV, PO, float(CAP), None, ALU.is_ge, None, d)
        e_ = tt(OV, OV, BO.unsqueeze(1).broadcast_to([128, 8, 32]), MUL, e_, c)
        e_ = tt(PO, PO, OV, ADD, e_)
        e_ = tt(PO, PO, cst("eidx").unsqueeze(1).broadcast_to([128, 8, 32]), ADD, e_)
        PS_ = tmp(8, 2)
        for k, o in enumerate((o1, o2)):
            a = tt(OV, PO, o, MUL, e_)
            e_ = red(PS_[:, :, k], OV, ADD, a)
        POSI = small(16).bitcast(I32).rearrange("p (a b) -> p a b", a=8)
        t_pos = cp(VE, POSI, PS_, e_)
        TOKI = small(8).bitcast(I32)
        t_tok = cp(VE, TOKI, cst("tok"), l_c)
        EB = tmp(15, 32)
        EF = tmp(16)
        io15 = cst("iota")[:, 0:15].unsqueeze(2).broadcast_to([128, 15, 32])
        a = tt(EB, NVI.unsqueeze(1).broadcast_to([128, 15, 32]), io15, ALU.is_le, c)
        a = red(EF[:, 0:15], EB, ADD, a)
        a = ts(EF[:, 0:15], EF[:, 0:15], 31.0, None, MIN, None, a)
        b_ = cp(VE, EF[:, 15:16], NVI[:, 31:32], c)
        EI = small(16).bitcast(I32)
        t_ei = cp(VE, EI, EF, a, b_)
        INI = mem(60, [128], p=NBLK).bitcast(I32)
        d = VE(lambda e: e.memset(INI, T), yt_free)
        stdL = Load(sem())
        t_ini = dma(GP, std[:, :].rearrange("(b s) o -> b (s o)", s=128), INI, d, load=stdL)
        stdS = Load(sem())

        def indirect(load, lane, *w, **kw):
            load.n += 16
            lane(lambda e: e.indirect_dma_start(**kw).then_inc(load.sem, 16), *w)
            return Landed(load.sem, load.n)

        for i in range(NT):
            for k in range(2):
                t_sc = indirect(stdS, GP, t_ini, t_pos, t_tok, out=std[:, :],
                                out_offset=bass.IndirectOffsetOnAxis(ap=POSI[:, i, k:k + 1].bitcast(U32), axis=0),
                                in_=TOKI[:, i:i + 1], in_offset=None)
        ada_chunks(4, 6)
        STI = mem(60.5, [128], p=NBLK).bitcast(I32)
        STF = mem(61, [128], p=NBLK)
        t_st = dma(GP, STI, std[:, :].rearrange("(b s) o -> b (s o)", s=128), t_sc, h2T)
        d = cp(VE, STF, STI, t_st)
        b, ps, fr = PB.take()
        last = tr(ps[:, 0:NBLK], STF, cst("ident")[0:NBLK, 0:NBLK], d, fr)
        TAB = small(NBLK).bitcast(I32)
        t_tab = cp(VE, TAB, ps[:, 0:NBLK], last)
        PB.free[b] = t_tab
        routed = [t_tab, t_ei, t_g, t_pos]

        RING = [96, 64, 80, 112, 128, 144, 160, 176]
        for kb in RING:
            slots.setdefault(kb, Slot(kb))
        slots[96].used = [yn[-1], att_end, t_yz, yt_free]
        slots[112].used = [h2T[-1], h2T[-2], h2T[-3], t_h2[-1], lg_end]
        slots[128].used = slots[144].used = h2T + [lg_end]
        slots[160].used = slots[176].used = [yt_free]
        wi = [0]

        def expert_w(e):
            out_ = []
            for nm, c, n in (("exp_w_gate", 8, 512), ("exp_w_up", 8, 512), ("exp_w_down", 4, 1024)):
                kb = RING[wi[0] % len(RING)]
                wi[0] += 1
                s = slots[kb]
                dst = mem(kb, [c, n])
                ld = dma(SY, dst, A[nm][0, e].rearrange("(p c) n -> p c n", c=c), s.used, load=s.load)
                s.used = []
                out_.append((dst, ld, s))
            return out_

        XGB = [mem(32, [1024]), mem(36, [1024])]
        XTB = [mem(40, [8, 128]), mem(44, [8, 128])]
        SGB = [mem(48, [512]), mem(50, [512])]
        HDB = [mem(52, [512]), mem(54, [512])]
        HTB = [mem(56, [4, 128]), mem(58, [4, 128])]
        YB = [mem(60, [1024]), mem(192, [1024])]

        class Experts:

            def __init__(self, start):
                self.xg, self.xt = [start] * 2, [start] * 2
                self.sg, self.hd, self.ht, self.y = [start] * 2, [start] * 2, [start] * 2, [start] * 2
                self.bank = {b: [PB.free.get(b), start] for b in range(8)}
                self.gl = [Load(sem()), Load(sem())]
                self.yl = [Load(sem()), Load(sem())]

            def gather(self, n, blk):
                k = n % 2
                return indirect(self.gl[k], GP, self.xg[k], t_tab, t_h2[-1], out=XGB[k], out_offset=None, in_=h2d,
                                in_offset=bass.IndirectOffsetOnAxis(ap=TAB[:, blk:blk + 1].bitcast(U32), axis=0))

            def turn(self, n, t_g):
                k = n % 2
                done = []
                for q in range(2):
                    ps = banks[q]
                    for c in range(4):
                        last = tr(ps[:, 128 * c:128 * c + 128], XGB[k][:, 4 * q + c::8], cst("ident"), t_g, self.bank[q])
                    g = g2[:, 4 * q:4 * q + 4].unsqueeze(2).broadcast_to([128, 4, 128])
                    d = tt(XTB[k][:, 4 * q:4 * q + 4, :], ps[:, :].rearrange("p (a b) -> p a b", a=4), g, MUL,
                           last, self.xt[k])
                    self.bank[q] = d
                    done.append(d)
                self.xg[k] = last
                return done

            def up(self, n, xt, w):
                k = n % 2
                for v in range(2):
                    dst, ld, s = w[v]
                    for c in range(8):
                        last = mm(banks[2 + v][:, :], XTB[k][:, c, :], dst[:, c, :], c == 0, c == 7, xt, ld, self.bank[2 + v])
                    s.used = [last]
                    if v == 0:
                        sg = act(SGB[k], banks[2][:, :], ACT.Silu, last, self.sg[k])
                        self.bank[2] = sg
                self.xt[k] = last
                hd = tt(HDB[k], banks[3][:, :], SGB[k], MUL, last, sg, self.hd[k])
                self.bank[3] = self.sg[k] = hd
                return hd

            def down(self, n, hd, w, blk):
                k = n % 2
                for j in range(4):
                    last = tr(banks[4][:, 128 * j:128 * j + 128], HDB[k][:, j::4], cst("ident"), hd, self.bank[4])
                self.hd[k] = last
                ht = cp(AC, HTB[k], banks[4][:, :].rearrange("p (a b) -> p a b", a=4), last, self.ht[k])
                self.bank[4] = ht
                dst, ld, s = w[2]
                ev = []
                for q in range(2):
                    for j in range(4):
                        last = mm(banks[5 + q][:, :], HTB[k][:, j, :], dst[:, j, 512 * q:512 * q + 512], j == 0, j == 3,
                                  ht, ld, self.bank[5 + q])
                    e = cp((VE, AC)[q], YB[k][:, 512 * q:512 * q + 512], banks[5 + q][:, :], last, self.y[k])
                    self.bank[5 + q] = e
                    ev.append(e)
                s.used = [last]
                self.ht[k] = last
                self.y[k] = dma(AC, ysl[128 * blk:128 * blk + 128, :], YB[k], ev, load=self.yl[k])
                return self.y[k]

        X1 = Experts([yt_free, routed, t_wg, t_ada])
        ws = [expert_w(0), expert_w(1)]
        gs = [X1.gather(0, 0), X1.gather(1, 1)]
        xt = X1.turn(0, gs[0])
        for e in range(NEXP):
            hd = X1.up(e, xt, ws[e])
            if e + 1 < NEXP:
                xt = X1.turn(e + 1, gs[e + 1])
            if e + 2 < NEXP:
                gs.append(X1.gather(e + 2, e + 2))
            y_ = X1.down(e, hd, ws[e], e)
            if e + 2 < NEXP:
                ws.append(expert_w(e + 2))
        y_end = [X1.y[0], X1.y[1]]
        pe_end = PE(lambda e: e.nop(), X1.ht)

        for l in lanes:
            l.when(EI[0:1, 15:16], t_ei, pe_end, y_end, t_yz)
        X2 = Experts(None)
        X2.bank = {b: None for b in range(8)}
        owl = [Load(sem()) for _ in range(3)]
        last_use = None
        for blk in range(NOV):
            w = []

            class Used:
                used = []

            reg = {}

            def expert_of(e, blk=blk, reg=reg):
                reg["e"] = e.value_load(EI[0:1, blk:blk + 1], min_val=0, max_val=31)
                return e.nop()

            SY(expert_of, last_use)
            for v, (nm, c, n, kb) in enumerate((("exp_w_gate", 8, 512, 96), ("exp_w_up", 8, 512, 64), ("exp_w_down", 4, 1024, 80))):
                dst = mem(kb, [c, n])
                owl[v].n += 16
                SY(lambda e, reg=reg, v=v, nm=nm, c=c, dst=dst: e.dma_start(
                    dst, A[nm][0, bass.ds(reg["e"], 1)].rearrange("a (p c) n -> p (a c) n", c=c)).then_inc(owl[v].sem, 16),
                   last_use)
                w.append((dst, Landed(owl[v].sem, owl[v].n), Used()))
            g_ = X2.gather(blk, NEXP + blk)
            xt = X2.turn(blk, g_)
            hd = X2.up(blk, xt, w)
            y_ = X2.down(blk, hd, w, NEXP + blk)
            last_use = X2.ht[blk % 2]
            if blk >= 1:
                AC(lambda e: e.nop(), X2.y[(blk - 1) % 2])
        for l in (SY, PE, AC, VE, GP):
            l(lambda e: e.nop(), X2.y[0], X2.y[1], last_use)
        for l in lanes:
            l.always()
        ex = [l(lambda e: e.nop()) for l in lanes]
        for l in lanes:
            l(lambda e: e.nop(), ex)
        for b in range(8):
            PB.free[b] = X1.bank[b]
        for s in slots.values():
            s.used = list(s.used) + ex

        asf, abf = [ex, ex], [ex, ex]
        CB = [mem(32 + 4 * i, [1024]) for i in range(8)]
        cbl = [Load(sem()) for _ in range(8)]
        cbf = [None] * 8
        x2 = []
        x2d = nc.dram_tensor("x2d", [NT, 128, D], F32).ap()
        x2l = Load(sem())
        k = 0
        for i in range(NT):
            d = x1[i]
            for q, G in enumerate((G1, G2)):
                ld = indirect(cbl[k % 8], GP, cbf[k % 8], ex, y_end, t_yz, t_pos, out=CB[k % 8], out_offset=None, in_=ysl,
                              in_offset=bass.IndirectOffsetOnAxis(ap=POSI[:, i, q:q + 1].bitcast(U32), axis=0))
                d = stt(X[:, i, :], CB[k % 8], G[:, i:i + 1], X[:, i, :], MUL, ADD, ld, d, t_g)
                cbf[k % 8] = d
                k += 1
            x2.append(d)
            t_x2 = dma(AC, x2d[i], X[:, i, :], d, load=x2l)
        for kb in ADA_AT[1]:
            slots[kb].used = [ex, slots[kb].used]
        ada_chunks(6, 12)

        cp2 = Load(sem())
        m = small_at[0]
        gbc, gnc, qnc, kvc = small(4), small(1), small(2), small(1)
        for o, v, n in ((gbc, A["gla_b_2"][0].rearrange("k (j p) -> p (k j)", p=128), 4),
                        (gnc, A["gla_norm_g_2"][0].rearrange("(p j) -> p j", j=1), 1),
                        (qnc, A["mla_q_norm_g_2"][0].rearrange("(j p) -> p j", p=128), 2),
                        (kvc, A["mla_kv_norm_g_2"][0].rearrange("(p j) -> p j", j=1), 1)):
            t_cp2 = dma(SY, o, v, load=cp2, allow_slow_non_contiguous=True)
        SH, SCL = {}, {}
        adl = Load(sem())
        for key, l, r in (("l0", 0, 0), ("c0", 0, 1), ("l1", 1, 0)):
            SH[key], SCL[key] = small(8), small(8)
            t_ad = dma(SY, SH[key], ada_d[l, r, 0:1024].rearrange("(p c) -> p c", c=8), t_ada, load=adl)
            t_ad = dma(SY, SCL[key], ada_d[l, r, 1024:2048].rearrange("(p c) -> p c", c=8), load=adl)
        for key in SH:
            t_scl = ts(SCL[key], SCL[key], 1.0, None, ADD, None, t_ad)

        GQ, GK, GV = mem(104, [2, 1024]), mem(112, [2, 1280]), mem(122, [10, 512])
        LK, GG = mem(142, [1280]), mem(147, [4, 1024])
        CQ, CKV, MG = mem(163, [2, 1024]), mem(171, [1280]), mem(176, [8, 512])
        SA, SB = 72, 88
        for kb in (SA, SB):
            slots[kb] = Slot(kb)
            slots[kb].used = list(slots[96].used)
        w_e = A["even_w_in_2"][0].rearrange("(p c) n -> p c n", c=8)
        CXR = mem(72, [2, 1024])
        l_cx = dma(SY, CXR, A["ctx_2"][0].rearrange("(t p) d -> p t d", p=128), ex)
        ada_end = [t_ada, slots[112].used, slots[128].used]
        tc_ = token_stats(2, lambda i: CXR[:, i, :], [[l_cx, x2[-1]], None], False)
        HC = Two(*two_rows(64, 192, 256), [])
        hC = split_major(2, lambda i: CXR[:, i, :], [tc_, ada_end], True, HC, SCL["c0"], SH["c0"], [t_scl, ex], at=(147, 151))
        tc_ = None
        for kb in (SA, 104, 147):
            slots[kb] = Slot(kb)
            slots[kb].used = [hC]
        WS = Stream(wide(104, 147, w_e, 512) + wide(SA, SB, w_e, 1984) +
                    [piece(147, w_e, 0), piece(SA, w_e, 256), piece(SB, w_e, 1568),
                     (147, [(w_e[:, :, 1824:1984], 0, 160), (w_e[:, :, 1024:1056], 160, 32)], 8, 192),
                     piece(SA, w_e, 1056), piece(SB, w_e, 1312)])
        tx = token_stats(NT, lambda i: X[:, i, :], [[x, hC] for x in x2], False)
        HL = Two(*two_rows(32, 0, T), [])
        hL = split_major(NT, lambda i: X[:, i, :], [tx, hC, t_x2, ada_end], True, HL, SCL["l0"], SH["l0"], [t_scl],
                         at=(122, 126, 130, 134, 138, 163, 167, 171))
        hLC = [hL, hC]
        CH = [(HC, 0, 0, 256), (HL, 0, 256, 512), (HL, 512, 768, 512)]

        def cm_lc(w, col, m, evac, ctx_too=True):
            for src, t0, o, n in CH if ctx_too else CH[1:]:
                b, ps, last = proj3(w, col, src, 0, m=m, n=n, tok=t0)
                PB.free[b] = evac(ps[0:m, 0:n], o, n, last)
            return last

        gq_d, gk_d, gv_d, lk_d, gg_d, cq_d, ckv_d, mg_d = [], [], [], [], [], [], [], []
        alt = [0]

        def put(dst, lst, scale=None, func=None):
            def f(ps, o, n, last):
                if func is not None:
                    d = act(dst(o, n), ps, func, last)
                elif scale is not None:
                    d = ts(dst(o, n), ps, scale, None, MUL, None, last)
                else:
                    alt[0] ^= 1
                    d = cp((VE, AC)[alt[0]], dst(o, n), ps, last)
                lst.append(d)
                return d
            return f

        def token_major(w, i, evac):
            src, t0 = (HC, 128 * i) if i < 2 else (HL, 128 * (i - 2))
            b, ps, fr = PB.take()
            for c in range(8):
                last = mm3(ps[:, :], src, w, c, slice(t0, t0 + 128), slice(0, 512), c == 0, c == 7, fr, w.m, src.m)
            PB.free[b] = evac(ps[:, :], last)
            return last

        w = joined(WS.get(), WS.get())
        for i in range(10):
            last = token_major(w, i, lambda ps, m, i=i: cp((VE, AC)[i % 2], GV[:, i, :], ps, m))
            gv_d.append(PB.free[PB.order[(PB.at - 1) % 8]])
            if i in (3, 6):
                WS.split()
        WS.done(last)
        WS.done(last)
        w = joined(WS.get(), WS.get())
        for i in range(8):
            last = token_major(w, i + 2, lambda ps, m, i=i: act(MG[:, i, :], ps, ACT.Silu, m))
            mg_d.append(PB.free[PB.order[(PB.at - 1) % 8]])
            if i == 5:
                WS.split()
        WS.done(last)
        WS.done(last)

        def both(w, f):
            for q in range(2):
                last = f(w, q)
                if q == 0:
                    WS.split()
            WS.done(last)
            return last

        both(WS.get(), lambda w, j: cm_lc(w, 128 * j, 128, put(lambda o, n, j=j: GQ[:, j, o - 256:o - 256 + n], gq_d, scale=0.125), False))
        both(WS.get(), lambda w, j: cm_lc(w, 128 * j, 128, put(lambda o, n, j=j: GK[:, j, o:o + n], gk_d)))
        both(WS.get(), lambda w, j: cm_lc(w, 128 * j, 128, put(lambda o, n, j=j: CQ[:, j, o - 256:o - 256 + n], cq_d), False))
        w = WS.get()
        for k in range(2):
            cm_lc(w, 160 + 16 * k, 16, put(lambda o, n, k=k: LK[32 * k:32 * k + 16, o:o + n], lk_d))
        WS.split()
        cm_lc(w, 0, 128, put(lambda o, n: CKV[:, o:o + n], ckv_d))
        WS.done(cm_lc(w, 128, 32, put(lambda o, n: LK[64:96, o:o + n], lk_d)))
        for e in range(2):
            last = both(WS.get(), lambda w, j: cm_lc(w, 128 * j, 128, put(lambda o, n, j=2 * e + j: GG[:, j, o - 256:o - 256 + n], gg_d,
                                                                     func=ACT.Silu), False))
        pr_end = last
        l_x3 = [xL[i](SY, X[:, i, :], x2d[i], pr_end, t_x2) for i in range(NT)]

        YG = mem(32, [4, 1024])
        GB, QM, KM, QE, KD = mem(48, [1280]), mem(53, [1024]), mem(57, [1024]), mem(64, [1024]), mem(72, [1280])
        KDT, SS = mem(77, [10, 128]), mem(82, [16, 128])
        E1, E2 = mem(90, [1280]), mem(95, [1024])
        RM = mem(99, [1024])
        W2G = mem(193, [256])
        l_w2g = [dma(SY, W2G[32 * k:32 * k + 16, :], A["gla_w2_2"][0, k], ex, pr_end) for k in range(2)]
        ATT = [[mem(61, [512]), mem(68, [512])], [mem(70, [512]), mem(194, [512])]]
        DC = small(16)
        tz = []
        for k in range(2):
            for q in range(2):
                tz.append(VE(lambda e, k=k, q=q: e.memset(ATT[k][q], 0.0), pr_end))
        d = VE(lambda e: e.memset(RM, 1.0), pr_end)
        d = VE(lambda e: e.memset(RM[:, ::64], 0.0), d)
        tz.append(d)
        PG = Banks(banks, [0, 1, 2, 3])
        PG.free = dict(PB.free)
        gla_all = [gq_d, gk_d, gv_d, lk_d, gg_d, pr_end, tz]
        o_free = [PB.free.get(4 + i) for i in range(4)]
        prev_pe = None
        prev_all = [pr_end]
        attf = [[None, None], [None, None]]
        yg_d = []
        AC(lambda e: e.preload_act_table_set("natural_log_exp_and_others"))
        for tau in range(2):
            for k in range(2):
                g_d = []
                for o, n in ((0, 256), (256, 512), (768, 512)):
                    b, ps, fr = PG.take()
                    m1 = mm(ps[:, 0:n], W2G[32 * k:32 * k + 16, 128 * tau:128 * tau + 128], LK[32 * k:32 * k + 16, o:o + n],
                            True, True, fr, l_w2g, lk_d)
                    bias = gbc[:, 2 * k + tau:2 * k + tau + 1]
                    a0 = act(E1[:, o:o + n], ps[:, 0:n], ACT.Abs, m1, prev_all, t_cp2, bias=bias)
                    a = act(E1[:, o:o + n], E1[:, o:o + n], ACT.Exp, a0, scale=-1.0)
                    a = act(E1[:, o:o + n], E1[:, o:o + n], ACT.Ln, a, bias=1.0)
                    d = ts(KD[:, o:o + n], ps[:, 0:n], bias, 0.0, ADD, MIN, m1, a0, prev_all, t_cp2)
                    PG.free[b] = [d, a]
                    d = tt(KD[:, o:o + n], KD[:, o:o + n], E1[:, o:o + n], SUB, d, a)
                    g_d.append(d)
                o1_ = VE(lambda e: e.memset(E2[:, 0:256], 1.0), prev_all)
                if k == 0:
                    d = VE(lambda e: e.tensor_tensor_scan(GB[:, 0:256], E2[:, 0:256], KD[:, 0:256], 0.0, MUL, ADD), g_d, o1_, prev_all)
                    d2 = VE(lambda e: e.tensor_tensor_scan(GB[:, 256:1280], RM, KD[:, 256:1280], 0.0, MUL, ADD), tz, g_d, prev_all)
                else:
                    d = VE(lambda e: e.tensor_tensor_scan(GB[:, 0:256][:, ::-1], E2[:, 0:256], KD[:, 0:256][:, ::-1], 0.0, MUL, ADD), g_d, o1_, prev_all)
                    d2 = VE(lambda e: e.tensor_tensor_scan(GB[:, 256:1280][:, ::-1], RM, KD[:, 256:1280][:, ::-1], 0.0, MUL, ADD), tz, g_d)
                BL = GB[:, 256:1280].rearrange("p (c s) -> p c s", c=16)
                mid, end = (31, 63) if k == 0 else (32, 0)
                e1v = E1[:, 256:1280].rearrange("p (c s) -> p c s", c=16)
                bmid = BL[:, :, mid:mid + 1].broadcast_to([128, 16, 64])
                bend = BL[:, :, end:end + 1].broadcast_to([128, 16, 64])
                GKl, GQl = GK[:, tau, 256:1280], GQ[:, tau, :]
                a = tt(e1v, BL, bmid, SUB, d2)
                q1 = act(QM, E1[:, 256:1280], ACT.Exp, a, prev_all, scale=1.0 / 16)
                q1 = tt(QM, QM, GQl, MUL, q1, gq_d)
                k1 = act(KM, E1[:, 256:1280], ACT.Exp, a, prev_all, scale=-1.0 / 16)
                k1 = tt(KM, KM, GKl, MUL, k1, gk_d)
                q2 = act(QE, GB[:, 256:1280], ACT.Exp, d2, prev_all, scale=1.0 / 16)
                q2 = tt(QE, QE, GQl, MUL, q2, gq_d)
                a = tt(KD[:, 256:1280].rearrange("p (c s) -> p c s", c=16), bend, BL, SUB, d2, d)
                ce = 255 if k == 0 else 0
                a2 = tt(KD[:, 0:256], GB[:, ce:ce + 1].broadcast_to([128, 256]), GB[:, 0:256], SUB, d)
                a = act(KD, KD, ACT.Exp, a, a2, scale=1.0 / 16)
                k2 = tt(KD, KD, GK[:, tau, :], MUL, a, gk_d)
                dc = act(DC, BL[:, :, end], ACT.Exp, d2, prev_all, scale=1.0 / 16)
                kdt = []
                for q in range(3):
                    m_ = 4 if q < 2 else 2
                    b, ps, fr = PG.take()
                    for j in range(m_):
                        i = 4 * q + j
                        last = tr(ps[:, 128 * j:128 * j + 128], KD[:, 128 * i:128 * i + 128], cst("ident"), k2, fr)
                    d = cp(AC, KDT[:, 4 * q:4 * q + m_, :], ps[:, 0:128 * m_].rearrange("p (a b) -> p a b", a=m_), last, prev_all)
                    PG.free[b] = d
                    kdt.append(d)
                b, ps, fr = PG.take()
                for hh in range(2):
                    hv = slice(128 * (2 * tau + hh), 128 * (2 * tau + hh) + 128)
                    for i in range(2):
                        last = mm(ps[64 * hh:64 * hh + 64, 0:128], KDT[:, i, 64 * hh:64 * hh + 64], GV[:, i, hv], i == 0, i == 1,
                                  kdt, fr, gv_d)
                order = list(range(16)) if k == 0 else list(range(15, -1, -1))
                s_d = cp(VE, SS[:, order[0], :], ps[:, 0:128], last, prev_all)
                PG.free[b] = s_d
                s_at = {order[0]: s_d}
                for q in range(2):
                    grp = order[8 * q:8 * q + 8]
                    bk = {}
                    for par in range(2):
                        b, ps, fr = PG.take()
                        bk[par] = (b, ps)
                        for n_, c in enumerate([c for c in grp if c % 2 == par]):
                            p0, i = 64 * par, 2 + c // 2
                            for hh in range(2):
                                hv = slice(128 * (2 * tau + hh), 128 * (2 * tau + hh) + 128)
                                last = mm(ps[64 * hh:64 * hh + 64, 128 * n_:128 * n_ + 128],
                                          KDT[p0:p0 + 64, i, 64 * hh:64 * hh + 64], GV[p0:p0 + 64, i, hv], True, True, kdt, fr)
                    for n_, c in enumerate(grp):
                        nx = order.index(c) + 1
                        if nx < 16:
                            c0 = 128 * (n_ // 2)
                            s_d = stt(SS[:, order[nx], :], SS[:, c, :], DC[:, c:c + 1], bk[c % 2][1][:, c0:c0 + 128], MUL, ADD,
                                      last, s_d, dc)
                            s_at[order[nx]] = s_d
                    PG.free[bk[0][0]] = PG.free[bk[1][0]] = s_d
                msk = cst("glaf" if k == 0 else "glar").unsqueeze(1).broadcast_to([128, 4, 128]).bitcast(I32)
                for g_ in range(4):
                    b, ps, fr = PG.take()
                    for n_ in range(4):
                        i, hh = 4 * (g_ // 2) + n_, g_ % 2
                        last = mm(ps[:, 128 * n_:128 * n_ + 128], KM[64 * hh:64 * hh + 64, 128 * i:128 * i + 128],
                                  QM[64 * hh:64 * hh + 64, 128 * i:128 * i + 128], True, True, q1, k1, fr)
                    at_ = ATT[k][g_ % 2]
                    d = VE(lambda e, at_=at_, ps=ps, msk=msk: e.copy_predicated(
                        at_.rearrange("p (a b) -> p a b", a=4), msk, ps[:, :].rearrange("p (a b) -> p a b", a=4)),
                        last, attf[k][g_ % 2], tz)
                    PG.free[b] = d
                    for n_ in range(4):
                        i, hh = 4 * (g_ // 2) + n_, g_ % 2
                        h = 2 * tau + hh
                        ob = banks[4 + 2 * hh + i // 4]
                        c0 = 128 * (i % 4)
                        mm(ob[:, c0:c0 + 128], GV[:, 2 + i, 128 * h:128 * h + 128], at_[:, 128 * n_:128 * n_ + 128], k == 0 and n_ == 0, False,
                           d, o_free if k == 0 else None)
                        for c in (2 * i, 2 * i + 1):
                            last = mm(ob[:, c0 + 64 * (c % 2):c0 + 64 * (c % 2) + 64], SS[64 * hh:64 * hh + 64, c, :],
                                      QE[64 * hh:64 * hh + 64, 64 * c:64 * c + 64], False, k == 1, s_at[c], q2)
                    attf[k][g_ % 2] = last
                prev_all = [last]
            fr4 = []
            for hh in range(2):
                h = 2 * tau + hh
                for half in range(2):
                    s0 = slice(512 * half, 512 * half + 512)
                    ob = banks[4 + 2 * hh + half]
                    sq = act(E2[:, 0:512], ob[:, :], ACT.Square, last, prev_all)
                    b, ps, fr = PG.take()
                    m1 = mm(ps[:, :], cst("ones"), E2[:, 0:512], True, True, sq, fr)
                    r = rsq(E1[:, 0:512], ps[:, :], 128, m1, prev_all)
                    PG.free[b] = r
                    d = stt(YG[:, h, s0], ob[:, :], gnc[:, 0:1], E1[:, 0:512], MUL, MUL, r, t_cp2)
                    fr4.append(d)
                    d = tt(YG[:, h, s0], YG[:, h, s0], GG[:, h, s0], MUL, d, gg_d)
                    yg_d.append(d)
                    prev_all = [d, m1]
            o_free = fr4
        for b in range(4):
            PB.free[b] = PG.free.get(b)
            PB.free[4 + b] = fr4
        gla_end = [yg_d[-1], m1]

        QT, KT, MV = mem(48, [8, 1024], p=96), mem(80, [8, 1280], p=96), mem(122, [10, 512])
        WQN, WQR, WKN, WKVV = mem(147, [2, 512]), mem(151, [2, 256]), mem(153, [512]), mem(155, [512])
        ROP = mem(192, [2, 1024])
        MSQ = [mem(157, [512]), mem(159, [512])]
        MR = mem(161, [512])
        uq = A["mla_w_uq_2"][0].rearrange("(j p) (h x) -> p j h x", p=128, h=8)
        ukv = A["mla_w_ukv_2"][0].rearrange("p (h x) -> p h x", h=8)
        wml = Load(sem())
        for j in range(2):
            dma(SY, WQN[:, j, :].rearrange("p (h x) -> p h x", h=8), uq[:, j, :, 0:64], gla_end, load=wml)
            dma(SY, WQR[:, j, :].rearrange("p (h x) -> p h x", h=8), uq[:, j, :, 64:96], load=wml)
        dma(SY, WKN.rearrange("p (h x) -> p h x", h=8), ukv[:, :, 0:64], load=wml)
        l_uq = l_kv = dma(SY, WKVV.rearrange("p (h x) -> p h x", h=8), ukv[:, :, 64:128], load=wml)
        l_rp = dma(SY, ROP, A["k_rope"].rearrange("a p n -> p a n"), gla_end)
        mrf = gla_end
        msf = [gla_end, gla_end]
        cqn, kvn = [], []
        k = 0
        for src, gain, nj, chunks, dn, lst in ((CKV.unsqueeze(1), kvc, 1, ((0, 256), (256, 512), (768, 512)), ckv_d, kvn),
                                               (CQ, qnc, 2, ((0, 512), (512, 512)), cq_d, cqn)):
            for o, n in chunks:
                b, ps, fr = PB.take()
                for j in range(nj):
                    q = act(MSQ[k % 2][:, 0:n], src[:, j, o:o + n], ACT.Square, dn, msf[k % 2])
                    last = mm(ps[:, 0:n], cst("ones"), MSQ[k % 2][:, 0:n], j == 0, j == nj - 1, q, fr)
                    msf[k % 2] = last
                    k += 1
                r = rsq(MR[:, 0:n], ps[:, 0:n], 128 * nj, last, mrf)
                PB.free[b] = r
                for j in range(nj):
                    d = stt(src[:, j, o:o + n], src[:, j, o:o + n], gain[:, j:j + 1], MR[:, 0:n], MUL, MUL, r, t_cp2)
                mrf = d
                lst.append(d)
        qt_d, kt_d, mv_d = [], [], []
        RQ = [mem(157, [512]), mem(159, [512])]
        RT1 = mem(161, [512])
        RT2 = mem(142 + 5 - 5, [512])
        rqf = [mrf, mrf]
        rtf = mrf
        kr0 = cp(AC, KT[64:96, 0, 0:256], LK[64:96, 0:256], lk_d, gla_end)
        krl = [kr0]
        for half in range(2):
            s0 = slice(512 * half, 512 * half + 512)
            lk = LK[64:96, 256 + 512 * half:768 + 512 * half]
            b, ps, fr = PB.take()
            m1 = mm(ps[64:96, :], cst("perm")[64:96, 64:96], lk, True, True, fr, lk_d, gla_end)
            d = tt(RT1[64:96, :], ps[64:96, :], ROP[64:96, 1, s0], MUL, m1, l_rp, rtf)
            PB.free[b] = d
            ko = KT[64:96, 0, 256 + 512 * half:768 + 512 * half]
            a = tt(ko, lk, ROP[64:96, 0, s0], MUL, l_rp, gla_end)
            d = tt(ko, ko, RT1[64:96, :], ADD, d, a)
            rtf = d
            krl.append(d)
        for h in range(1, 8):
            kt_d.append(cp(GP, KT[64:96, h, :], KT[64:96, 0, :], krl))
        kt_d += krl
        for hp in range(4):
            for o, n in ((0, 256), (256, 512), (768, 512)):
                b, ps, fr = PB.take()
                last = mm(ps[:, 0:n], WKN[:, 128 * hp:128 * hp + 128], CKV[:, o:o + n], True, True, fr, l_kv, kvn)
                d1 = cp(VE, KT[0:64, 2 * hp, o:o + n], ps[0:64, 0:n], last, gla_end)
                d2 = cp(AC, KT[0:64, 2 * hp + 1, o:o + n], ps[64:128, 0:n], last, gla_end)
                PB.free[b] = [d1, d2]
                kt_d += [d1, d2]
        for hp in range(4):
            for half in range(2):
                s0 = slice(512 * half, 512 * half + 512)
                b, ps, fr = PB.take()
                for j in range(2):
                    last = mm(ps[:, :], WQN[:, j, 128 * hp:128 * hp + 128], CQ[:, j, s0], j == 0, j == 1, fr, l_uq, cqn)
                d1 = cp(VE, QT[0:64, 2 * hp, s0], ps[0:64, :], last, gla_end)
                d2 = cp(AC, QT[0:64, 2 * hp + 1, s0], ps[64:128, :], last, gla_end)
                PB.free[b] = [d1, d2]
                qt_d += [d1, d2]
        k = 0
        for g_ in range(2):
            for half in range(2):
                s0 = slice(512 * half, 512 * half + 512)
                b, ps, fr = PB.take()
                for j in range(2):
                    last = mm(ps[:, :], WQR[:, j, 128 * g_:128 * g_ + 128], CQ[:, j, s0], j == 0, j == 1, fr, l_uq, cqn)
                r = cp(AC, RQ[k % 2], ps[:, :], last, rqf[k % 2])
                b2, ps2, fr2 = PB.take()
                m2 = mm(ps2[:, :], cst("perm"), RQ[k % 2], True, True, r, fr2)
                d = tt(RT1, ps2[:, :], ROP[:, 1, s0], MUL, m2, rtf)
                PB.free[b2] = d
                a = tt(RQ[k % 2], RQ[k % 2], ROP[:, 0, s0], MUL, m2)
                PB.free[b] = r
                a = tt(RQ[k % 2], RQ[k % 2], RT1, ADD, a, d)
                rtf = a
                for q in range(4):
                    c_ = cp(AC if q % 2 else VE, QT[64:96, 4 * g_ + q, s0], RQ[k % 2][32 * q:32 * q + 32, :], a, gla_end)
                    qt_d.append(c_)
                rqf[k % 2] = qt_d[-2:]
                k += 1
        for i in range(10):
            b, ps, fr = PB.take()
            last = mm(ps[:, :], CKV[:, 128 * i:128 * i + 128], WKVV, True, True, fr, l_kv, kvn)
            d = cp((VE, AC)[i % 2], MV[:, i, :], ps[:, :], last, gla_end)
            PB.free[b] = d
            mv_d.append(d)
        up_end = [last, rtf]

        YM = mem(147, [4, 1024])
        PP = [mem(163, [1280]), mem(168, [1280])]
        PT = [mem(192, [10, 128]), mem(142, [10, 128])]
        OT = [mem(173, [512]), mem(197, [512])]
        NM, RS2, RI = small(8), [small(8), small(8)], small(8)
        SCALE = 96.0 ** -0.5
        ready = [qt_d, kt_d, mv_d, up_end]
        start = [PB.free.get(b) for b in range(8)]
        sfree = [start, start]
        tfree = [start]
        ppf, ptf = [up_end, up_end], [up_end, up_end]
        otf = [up_end, up_end]
        ym_d = []
        its = [(qt, h) for qt in range(8) for h in range(8)]
        st = {}

        def score_part(s, q):
            qt, h = its[s]
            o, n = ((0, 512), (512, 512), (1024, 256))[q]
            return mm(PSM[:, 3 * (s % 2) + q, 0:n], QT[:, h, 128 * qt:128 * qt + 128], KT[:, h, o:o + n], True, True,
                      sfree[s % 2], ready)

        def soften(s, last):
            qt, h = its[s]
            k = s % 2
            ps = PSM[:, 3 * k:3 * k + 3, :].rearrange("p a b -> p (a b)")[:, 0:1280]
            d = VE(lambda e: e.tensor_reduce(NM[:, h:h + 1], ps, AX, MAX), last, st.get(("e", s - 8)))
            d = ts(NM[:, h:h + 1], NM[:, h:h + 1], -SCALE, None, MUL, None, d)
            e_ = AC(lambda e: e.activation(PP[k], ps, ACT.Exp, bias=NM[:, h:h + 1], scale=SCALE,
                                           accum_out=RS2[qt % 2][:, h:h + 1]), d, ppf[k], st.get(("o", qt - 2)))
            sfree[k] = e_
            st[("e", s)] = e_

        tb = banks[6]

        def turn_part(s, q):
            k = s % 2
            m_ = 4 if q < 2 else 2
            for j in range(m_):
                i = 4 * q + j
                last = tr(tb[:, 128 * j:128 * j + 128], PP[k][:, 128 * i:128 * i + 128], cst("ident"), st[("e", s)], tfree[0])
            d = cp((VE, AC, VE)[q], PT[k][:, 4 * q:4 * q + m_, :], tb[:, 0:128 * m_].rearrange("p (a b) -> p a b", a=m_), last, ptf[k])
            tfree[0] = d
            ppf[k] = last
            return d

        def mix(s, pt):
            qt, h = its[s]
            k = s % 2
            for i in range(10):
                last = mm(banks[7][:, 64 * h:64 * h + 64], PT[k][:, i, :], MV[:, i, 64 * h:64 * h + 64], i == 0, i == 9,
                          pt[i // 4], of[0] if h == 0 else None)
            ptf[k] = last
            if h == 7:
                kk = qt % 2
                r = VE(lambda e: e.reciprocal(RI, RS2[kk]), st[("e", s)])
                d = tt(OT[kk].rearrange("p (a b) -> p a b", a=8), banks[7][:, :].rearrange("p (a b) -> p a b", a=8),
                       RI.unsqueeze(2).broadcast_to([128, 8, 64]), MUL, last, r, otf[kk])
                of[0] = d
                st[("o", qt)] = r
                return tt(OT[kk], OT[kk], MG[:, qt, :], MUL, d, mg_d)

        def turn_out(qt, d):
            kk = qt % 2
            for j in range(4):
                last = tr(tb[:, 128 * j:128 * j + 128], OT[kk][:, 128 * j:128 * j + 128], cst("ident"), d, tfree[0])
            otf[kk] = last
            d = cp(AC, YM[:, :, 128 * qt:128 * qt + 128], tb[:, :].rearrange("p (a b) -> p a b", a=4), last, up_end)
            tfree[0] = d
            ym_d.append(d)

        of = [start]
        late = None
        for s in range(66):
            pt = []
            for q in range(3):
                if s >= 2:
                    pt.append(turn_part(s - 2, q))
                if s < 64:
                    last = score_part(s, q)
            if s < 64:
                soften(s, last)
            if late:
                turn_out(*late)
                late = None
            if s >= 2:
                d = mix(s - 2, pt)
                if its[s - 2][1] == 7:
                    late = (its[s - 2][0], d)
        turn_out(*late)
        for b in range(8):
            PB.free[b] = [sfree, tfree, of]
        ml_end = [ym_d[-1], ptf]

        GROW, PLG, PLB = mem(120 - 8, [1024]), mem(116, [1024]), mem(122, [1024])

        def post(layer, l_x, W, lw, tile_of, yd, G_, P1_, P2_, w0, tmps):
            l1 = dma(SY, G_, ada_d[layer, 0:1, 2048:3072].broadcast_to([128, 1024]), w0)
            l2 = dma(SY, P1_, A["post_ln_g_2"][layer:layer + 1, :].broadcast_to([128, 1024]), w0)
            l3 = dma(SY, P2_, A["post_ln_b_2"][layer:layer + 1, :].broadcast_to([128, 1024]), w0)
            done = []
            alpha = float(4 ** 0.25)
            fr_t = [w0, w0]
            bnf = None
            for i in range(NT):
                xi = X[:, i, :]
                ds_ = []
                for q in range(2):
                    b, ps, fr = PB.take()
                    for j in range(8):
                        last = mm(ps[:, :], tile_of(j)[:, 128 * i:128 * i + 128], W[:, j, 512 * q:512 * q + 512], j == 0, j == 7,
                                  fr, lw, yd)
                    s_ = slice(512 * q, 512 * q + 512)
                    d = tt(tmps[q], ps[:, :], G_[:, s_], MUL, last, l1, fr_t[q])
                    PB.free[b] = d
                    d = stt(xi[:, s_], xi[:, s_], alpha, tmps[q], MUL, ADD, d, l_x[i])
                    fr_t[q] = d
                    ds_.append(d)
                mvi = mvv[:, i, :]
                d = stats(xi, 1024, bnb, mvi, [ds_, bnf])
                bnf = d
                r = rsq(rs8[:, i:i + 1], mvi[:, 1:2], 1, d)
                n_ = stt(nb8[:, i:i + 1], mvi[:, 0:1], -1.0, rs8[:, i:i + 1], MUL, MUL, r)
                a = act(xi, xi, ACT.Identity, n_, scale=rs8[:, i:i + 1], bias=nb8[:, i:i + 1])
                a = tt(xi, xi, P1_, MUL, a, l2, lane=GP)
                a = tt(xi, xi, P2_, ADD, a, l3, lane=GP)
                done.append(a)
            return done, last

        WO2 = mem(48, [8, 1024])
        w2v = A["even_w_out_2"][0].rearrange("(j p) n -> p j n", p=128)
        l_wo2 = [dma(SY, WO2[:, 4 * q:4 * q + 4, :], w2v[:, 4 * q:4 * q + 4, :], ml_end) for q in range(2)]
        x3, po_end = post(0, l_x3, WO2, l_wo2, lambda j: YG[:, j, :] if j < 4 else YM[:, j - 4, :], [ym_d, yg_d], GROW, PLG, PLB, ml_end,
                          [mem(126, [512]), mem(128, [512])])

        OS = [64, 80, 96]
        for kb in OS:
            slots[kb] = Slot(kb)
            slots[kb].used = [po_end, x3]
        FT, FGT, UT, VT = mem(112, [4, 1024]), mem(128, [4, 1024]), mem(144, [4, 1024]), mem(160, [8, 512])
        w_d = A["odd_w_in_2"][0].rearrange("(p c) n -> p c n", c=8)
        x3d = nc.dram_tensor("x3d", [NT, 128, D], F32).ap()
        x3l = Load(sem())
        dft = [A["k_dft"][part].rearrange("(t p) k -> p t k", p=128) for part in range(2)]
        cols = [0, 256, 1024, 1280, 2048, 2304, 512, 768]
        seq = wide(OS[0], OS[1], w_d, 1536) + [piece(OS[(i + 2) % 3], w_d, c) for i, c in enumerate(cols)]
        dseq = [(part, half, q) for half in range(2) for part in range(2) for q in range(2)]
        seq += [(OS[(i + 10) % 3], [(dft[part][:, 4 * q:4 * q + 4, 512 * half:512 * half + 512], 0, 512)], 4, 512)
                for i, (part, half, q) in enumerate(dseq)]
        WS = Stream(seq)
        for i in range(NT):
            t_x3 = dma(AC, x3d[i], X[:, i, :], x3[i], load=x3l)
        DFC, SGB, SGW, SGT = mem(192, [256]), mem(193, [512]), mem(195, [4, 128]), mem(197, [4, 128])
        l_dfc = dma(SY, DFC, A["k_small"][:, NC - 256:NC], po_end, x3)
        l_sgb = dma(SY, SGB, A["sgu_b_2"].rearrange("a g t -> a (g t)").broadcast_to([128, 512]), po_end, x3)
        l_sgw = dma(SY, SGW, A["sgu_w_2"][0].rearrange("g t s -> t g s"), po_end, x3)
        tx = token_stats(NT, lambda i: X[:, i, :], x3, False)
        HO = Two(*two_rows(32, 0, T), [])
        hO = split_major(NT, lambda i: X[:, i, :], [tx, po_end, t_x3], True, HO, SCL["l1"], SH["l1"], [po_end])
        b, ps, fr = PB.take()
        for g_ in range(4):
            last = tr(ps[:, 128 * g_:128 * g_ + 128], SGW[:, g_, :], cst("ident"), l_sgw, fr)
        t_sgt = cp(AC, SGT, ps[:, :].rearrange("p (a b) -> p a b", a=4), last, po_end)
        PB.free[b] = t_sgt
        ft_d, fg_d, u_d, v_d = [], [], [], []
        VST = mem(184, [32, 6])
        VMV = mem(185, [32, 2])
        VR, VN = mem(185.5, [32]), mem(185.75, [32])
        w = joined(WS.get(), WS.get())
        vs = None
        for i in range(8):
            b, ps, fr = PB.take()
            for c in range(8):
                last = mm3(ps[:, :], HO, w, c, slice(128 * i, 128 * i + 128), slice(0, 512), c == 0, c == 7, fr, w.m, hO)
            d = act(VT[:, i, :], ps[:, :], ACT.Gelu, last)
            PB.free[b] = d
            for g_ in range(4):
                n_ = 4 * i + g_
                a = VE(lambda e, n_=n_, i=i, g_=g_: e.bn_stats(VST[:, n_, :], VT[:, i, 128 * g_:128 * g_ + 128]), d, hO)
                vs = VE(lambda e, n_=n_: e.bn_aggr(VMV[:, n_, :], VST[:, n_, :]), a)
            if i == 5:
                WS.split()
        WS.done(last)
        WS.done(last)

        def channels(j0, evac):
            w = WS.get()
            for j in range(2):
                for half in range(2):
                    b, ps, last = proj3(w, 128 * j, HO, half)
                    PB.free[b] = evac(j0 + j, slice(512 * half, 512 * half + 512), ps[:, :], last)
                if j == 0:
                    WS.split()
            WS.done(last)
            return last

        def keep(lst, d):
            lst.append(d)
            return d

        for j in (0, 2):
            channels(j, lambda j, s0, ps, m: keep(ft_d, cp(VE, FT[:, j, s0], ps, m)))
        for j in (0, 2):
            channels(j, lambda j, s0, ps, m: keep(u_d, act(UT[:, j, s0], ps, ACT.Gelu, m)))
        r = rsq(VR, VMV[:, :, 1], 1, vs)
        nb_ = stt(VN, VMV[:, :, 0], -1.0, VR, MUL, MUL, r)
        for i in range(8):
            for g_ in range(4):
                n_ = 4 * i + g_
                v = VT[:, i, 128 * g_:128 * g_ + 128]
                v_d.append(ts(v, v, VR[:, n_:n_ + 1], VN[:, n_:n_ + 1], MUL, ADD, nb_))
        SGX = [mem(176, [512]), mem(178, [512])]
        sgf = [hO, hO]
        us_d = []

        def gated(j, s0, ps, m):
            k = len(us_d) % 2
            d = act(SGX[k], ps, ACT.Silu, m, sgf[k])
            sgf[k] = keep(us_d, tt(UT[:, j, s0], UT[:, j, s0], SGX[k], MUL, d, u_d))
            return d

        for j in (0, 2):
            channels(j, gated)
        for j in (0, 2):
            ho_end = channels(j, lambda j, s0, ps, m: keep(fg_d, act(FGT[:, j, s0], ps, ACT.Silu, m)))
        l_x4 = [xL[i](SY, X[:, i, :], x3d[i], ho_end, t_x3) for i in range(NT)]
        ys_d = []
        k = 0
        for g_ in range(4):
            for half in range(2):
                s0 = slice(512 * half, 512 * half + 512)
                b, ps, fr = PB.take()
                for q in range(4):
                    i = 4 * half + q
                    last = mm(ps[:, 128 * q:128 * q + 128], VT[:, i, 128 * g_:128 * g_ + 128], SGT[:, g_, :], True, True,
                              v_d, t_sgt, fr)
                bb = SGB[:, 128 * g_:128 * g_ + 128].unsqueeze(1).broadcast_to([128, 4, 128])
                d = tt(SGX[k % 2].rearrange("p (a b) -> p a b", a=4), ps[:, :].rearrange("p (a b) -> p a b", a=4), bb, ADD,
                       last, l_sgb, sgf[k % 2])
                PB.free[b] = d
                d = tt(UT[:, g_, s0], UT[:, g_, s0], SGX[k % 2], MUL, d, us_d)
                sgf[k % 2] = d
                ys_d.append(d)
                k += 1
        AB = Two(*two_rows(32, 160, T), [])
        for i in range(8):
            for gg_ in range(2):
                b, ps, fr = PB.take()
                for q in range(2):
                    g_ = 2 * gg_ + q
                    last = mm(ps[:, 256 * q:256 * q + 256], FT[:, g_, 128 * i:128 * i + 128], DFC, True, True, ft_d, l_dfc, fr)
                s0 = slice(512 * gg_, 512 * gg_ + 512)
                h = AB.hi[i][:, s0]
                a = act(h, ps[:, :], ACT.Copy, last, ho_end)
                d = tt(AB.lo[i][:, s0], ps[:, :], h.bitcast(F32), SUB, a, ys_d)
                PB.free[b] = d
                AB.m.append(d)
            if i in (2, 5):
                WS.split()
        ab_end = last
        yf_d = []
        for half in range(2):
            s0 = slice(512 * half, 512 * half + 512)
            bk = [PB.take() for _ in range(4)]
            for part in range(2):
                for q in range(2):
                    w = WS.get()
                    for g_ in range(4):
                        _, ps, fr = bk[g_]
                        o = 256 * g_ + 128 * part
                        tb2 = Two(AB.hi[4 * q:4 * q + 4], AB.lo[4 * q:4 * q + 4], None)
                        for i in range(4):
                            last = mm3(ps[:, :], tb2, w, i, slice(o, o + 128), slice(0, 512), part + q + i == 0,
                                       part == 1 and q == 1 and i == 3, AB.m, w.m, fr)
                        if g_ == 1:
                            WS.split()
                    WS.done(last)
            for g_ in range(4):
                b, ps, _ = bk[g_]
                d = tt(FT[:, g_, s0], ps[:, :], FGT[:, g_, s0], MUL, last, fg_d, ab_end)
                PB.free[b] = d
                yf_d.append(d)
        f_last = last
        WO3 = mem(64, [8, 1024])
        w3v = A["odd_w_out_2"][0].rearrange("(j p) n -> p j n", p=128)
        l_wo3 = [dma(SY, WO3[:, 4 * q:4 * q + 4, :], w3v[:, 4 * q:4 * q + 4, :], f_last, ys_d) for q in range(2)]
        x4, pe4 = post(1, l_x4, WO3, l_wo3, lambda j: FT[:, j, :] if j < 4 else UT[:, j - 4, :], [yf_d, ys_d],
                       mem(128, [1024]), mem(132, [1024]), mem(136, [1024]), [yf_d, ys_d, f_last], [mem(176, [512]), mem(178, [512])])
        od = out[0].rearrange("(t p) d -> p t d", p=128)

        for i in range(NT):
            stores.append(dma(SY, od[:, i, :], X[:, i, :], x4[i]))
        stores += [t_x2, t_x3, y_end, t_yz, t_ada, t_h2[-1], t_ini, t_sc]
        for s in stores:
            SY(lambda e: e.nop(), s)
        for l in lanes:
            l.count()
        block = ctx.enter_context(nc.Block())
        block.sync(SY.emit)
        block.tensor(PE.emit)
        block.scalar(AC.emit)
        block.vector(VE.emit)
        block.gpsimd(GP.emit)


_OUT = ((1, 1024, 1024), "float32")


def kernel(**inputs):
    import numpy as _np
    import concourse.bacc as _bacc
    from concourse import mybir as _mybir
    from concourse.bass_utils import run_bass_kernel_spmd as _run

    nc = _bacc.Bacc("TRN2", target_bir_lowering=False, num_devices=1)
    arrays, aps = {}, {}
    for name, a in {**inputs, **constants()}.items():
        a = _np.ascontiguousarray(a)
        arrays[f"in_{name}_dram"] = a
        aps[name] = nc.dram_tensor(f"in_{name}_dram", a.shape, _mybir.dt.from_np(a.dtype), kind="ExternalInput").ap()
    out = nc.dram_tensor("out_0_dram", _OUT[0], _mybir.dt.from_np(_np.dtype(_OUT[1])), kind="ExternalOutput").ap()
    build(nc, aps, out)
    r = _run(nc, [arrays], core_ids=[0])
    return r.results[0]["out_0_dram"]
```

```python
from contextlib import ExitStack

import concourse.bass as bass
from concourse import mybir

F32 = mybir.dt.float32
F32R = mybir.dt.float32r
I32 = mybir.dt.int32
U32 = mybir.dt.uint32
ALU = mybir.AluOpType
ACT = mybir.ActivationFunctionType
AX = mybir.AxisListType.X
ADD, SUB, MUL, MAX, MIN, POW = ALU.add, ALU.subtract, ALU.mult, ALU.max, ALU.min, ALU.pow
EPS = 1e-6


class Mark:

    def __init__(self, sem):
        self.sem, self.needed, self.value = sem, False, 0


class Landed:

    def __init__(self, sem, value):
        self.sem, self.value = sem, value


def marks(waits):
    if isinstance(waits, (list, tuple)):
        return [m for w in waits for m in marks(w)]
    return [] if waits is None else [waits]


class Lane:

    def __init__(self, nc, name, sem, sem_if):
        self.nc, self.name, self.sems, self.inside = nc, name, (sem, sem_if), False
        self.items = []

    def __call__(self, fn, *waits):
        mark = Mark(self.sems[self.inside])
        flat = marks(waits)
        for w in flat:
            if isinstance(w, Mark):
                w.needed = True
        self.items.append((fn, flat, mark))
        return mark

    def count(self):
        n = {}
        for _, _, mark in self.items:
            if mark.needed:
                n[id(mark.sem)] = mark.value = n.get(id(mark.sem), 0) + 1

    def when(self, flag, *waits):
        self(("when", flag), *waits)
        self.inside = True

    def always(self):
        self(("always", None))
        self.inside = False

    def emit(self, eng):
        seen = {}
        for fn, waits, mark in self.items:
            if isinstance(fn, tuple) and fn[0] == "always":
                branch.__exit__(None, None, None)
                seen = before
                continue
            for w in waits:
                if seen.get(id(w.sem), 0) < w.value:
                    seen[id(w.sem)] = w.value
                    eng.wait_ge(w.sem, w.value)
            if isinstance(fn, tuple):
                branch = eng.If(eng.value_load(fn[1], min_val=0, max_val=15) > 0)
                branch.__enter__()
                before = dict(seen)
                continue
            ins = fn(eng)
            if mark.needed:
                ins.then_inc(mark.sem, 1)


class Load:

    def __init__(self, sem):
        self.sem, self.n = sem, 0

    def __call__(self, lane, out, in_, *waits, **kw):
        self.n += 16
        lane(lambda e: e.dma_start(out, in_, **kw).then_inc(self.sem, 16), *waits)
        return Landed(self.sem, self.n)


class Banks:

    def __init__(self, banks, order):
        self.banks, self.order, self.at, self.free = banks, order, 0, {}

    def take(self):
        b = self.order[self.at % len(self.order)]
        self.at += 1
        return b, self.banks[b], self.free.get(b)

T = 1024
NT = 8
D = 1024
CAP = 128
NEXP = 32
NOV = 15
NBLK = NEXP + NOV
K4 = 256


def constants():
    import numpy as np
    p = np.arange(128)
    s, t = p[:, None], p[None, :]
    same = (s // 64) == (t // 64)
    parts = {
        "ident": s == t, "ones": s + t >= 0, "bd64": same, "ntri": -1.0 * (s >= t), "nones": -1.0 * (s + t >= 0),
        "sltu": s < t, "glaf": same & (s <= t), "glar": same & (s >= t),
    }
    ang = np.arange(128) * 2.0 * np.pi / 128
    c2 = np.arange(128)[:, None] * np.arange(128)[None, :] % 128
    parts["perm"] = (s // 32 == t // 32) & (s % 32 == (t + 16) % 32)
    parts["iota"] = t + 0.0 * s
    parts["tok"] = s + 128.0 * np.arange(8)[None, :]
    parts["eidx"] = 128.0 * t[:, :32] + 0.0 * s
    parts["dftc"] = np.concatenate([np.cos(ang)[c2], np.sin(ang)[c2]], 1)
    inv = np.float32(10000.0) ** (-np.arange(8, dtype=np.float32) / 8)
    n = np.arange(T)
    a = np.concatenate([(n // 64).astype(np.float32)[:, None] * inv, (n % 64).astype(np.float32)[:, None] * inv], 1)
    a = a.astype(np.float32)
    cos, sin = np.cos(a).T, np.sin(a).T
    rope_c = np.tile(np.concatenate([cos, cos]), (4, 1))
    rope_s = np.tile(np.concatenate([-sin, sin]), (4, 1))
    flat = []
    for v in parts.values():
        flat.append(v.astype(np.float32))
    angn = np.arange(T) * 2.0 * np.pi / T
    kn = np.arange(T)[:, None] * np.arange(T)[None, :] % T
    sc = 1.0 / np.sqrt(T * 128.0)
    cn = np.stack([np.cos(angn)[kn] * sc, -np.sin(angn)[kn] * sc])
    return {
        "k_small": np.ascontiguousarray(np.concatenate(flat, 1)),
        "k_rope": np.stack([rope_c, rope_s]).astype(np.float32),
        "k_dft": cn.astype(np.float32),
    }


def build(nc, A, out):
    constants_at = {}
    at = 0
    for name, n in (("ident", 128), ("ones", 128), ("bd64", 128), ("ntri", 128), ("nones", 128),
                    ("sltu", 128), ("glaf", 128), ("glar", 128), ("perm", 128), ("iota", 128), ("tok", 8), ("eidx", 32),
                    ("dftc", 256)):
        constants_at[name] = (at, n)
        at += n
    NC = at
    ctx = ExitStack()
    with ctx:
        MEM = ctx.enter_context(nc.sbuf_tensor("mem", [128, 401 * K4 // 2], F32))
        mem_at = nc.sbuf_base - 401 * K4 * 2
        CS = ctx.enter_context(nc.sbuf_tensor("cst", [128, NC - 256], F32))
        SM = ctx.enter_context(nc.sbuf_tensor("small", [128, 540], F32))
        PSM = ctx.enter_context(nc.psum_tensor("psm", [128, 8, 512], F32))
        banks = [PSM[:, i, :] for i in range(8)]
        nsem = [0]

        def sem(name=None):
            nsem[0] += 1
            return ctx.enter_context(nc.semaphore(name or f"s{nsem[0]}"))

        SY = Lane(nc, "sync", sem("sy"), sem("syi"))
        PE = Lane(nc, "tensor", sem("pe"), sem("pei"))
        AC = Lane(nc, "scalar", sem("ac"), sem("aci"))
        VE = Lane(nc, "vector", sem("ve"), sem("vei"))
        GP = Lane(nc, "gpsimd", sem("gp"), sem("gpi"))
        lanes = [SY, PE, AC, VE, GP]
        stores = []

        def mem(kb, shape, dt=F32, p=128):
            n = 1
            for s in shape:
                n *= s
            o = round(kb * K4)
            ap = MEM[0:p, o:o + n]
            if len(shape) == 2:
                ap = ap.rearrange("p (a b) -> p a b", a=shape[0])
            if len(shape) == 3:
                ap = ap.rearrange("p (a b c) -> p a b c", a=shape[0], b=shape[1])
            return ap

        nr = [0]

        def rounded(kb, n):
            nr[0] += 1
            return nc.alloc_sbuf_tensor_at(f"r{nr[0]}", [128, n], F32R, offset=mem_at + round(kb * 1024))[:, :]

        def cst(name):
            o, n = constants_at[name]
            return CS[:, o:o + n]

        small_at = [0]

        def small(n, dt=F32):
            o = small_at[0]
            small_at[0] += n
            assert small_at[0] <= 540, small_at
            return SM[:, o:o + n]

        def mm(o, l, r, start, stop, *w):
            return PE(lambda e: e.matmul(o, l, r, start=start, stop=stop, skip_group_check=True), *w)

        def tr(o, i, idn, *w):
            return PE(lambda e: e.transpose(o, i, idn), *w)

        def act(o, i, f, *w, **k):
            return AC(lambda e: e.activation(o, i, f, **k), *w)

        def tt(o, a, b, op, *w, lane=None):
            return (lane or VE)(lambda e: e.tensor_tensor(o, a, b, op), *w)

        def ts(o, a, s1, s2, op0, op1, *w, lane=None):
            if op1 is None:
                return (lane or VE)(lambda e: e.tensor_scalar(o, a, s1, None, op0), *w)
            return (lane or VE)(lambda e: e.tensor_scalar(o, a, s1, s2, op0, op1), *w)

        def stt(o, a, s, b, op0, op1, *w):
            return VE(lambda e: e.scalar_tensor_tensor(o, a, s, b, op0, op1), *w)

        def cp(lane, o, i, *w):
            if lane is AC:
                return act(o, i, ACT.Copy, *w)
            return lane(lambda e: e.tensor_copy(o, i), *w)

        def dma(lane, o, i, *w, load=None, **k):
            return (load or Load(sem()))(lane, o, i, *w, **k)

        epsc = small(1)
        t_eps = VE(lambda e: e.memset(epsc, EPS))

        def rsq(o, ss, n, *w):
            a = act(o, ss, ACT.Ln, *w, t_eps, scale=1.0 / n, bias=epsc[0:o.shape[0], 0:1])
            return act(o, o, ACT.Exp, a, scale=-0.5)

        X = mem(0, [NT, D])
        HT = mem(32, [8, T])
        W0, W1, W2 = 64, 80, 96

        l_c = dma(SY, CS[:, :], A["k_small"][:, 0:NC - 256])
        xs = A["x"][0].rearrange("(t p) d -> p t d", p=128)
        xL = [Load(sem()) for _ in range(NT)]
        l_x = [xL[i](SY, X[:, i, :], xs[:, i, :]) for i in range(NT)]

        colL = Load(sem())

        def column(src, n, *w):
            o = small(n)
            return o, dma(GP, o, src, *w, load=colL)

        g1, t_ = column(A["norm1_g"][0].rearrange("(p c) -> p c", c=8), 8)
        gq = small(1)
        gk = small(1)
        for g, nm in ((gq, "q_norm_g"), (gk, "k_norm_g")):
            for h in range(2):
                t_ = dma(GP, g[64 * h:64 * h + 64, :], A[nm][0].rearrange("(p c) -> p c", c=1), load=colL)
        rows = mem(150, [256])
        t_ = dma(GP, rows[0:31, :], A["conf_dw_w"][0], load=colL)
        r = 31
        for nm in ("conf_dw_b", "conf_ln_g", "conf_ln_b", "conf_pw_b"):
            t_ = dma(GP, rows[r:r + 1, :], A[nm], load=colL)
            r += 1
        t_ = dma(GP, rows[35:39, :], A["lru_conv_w"][0], load=colL)
        r = 39
        for nm in ("lru_conv_b", "lru_ba", "lru_bx", "lru_lambda"):
            t_ = dma(GP, rows[r:r + 1, :], A[nm], load=colL)
            r += 1
        t_ = dma(GP, rows[43:47, :], A["out_norm_g"][0].rearrange("(m n) -> m n", m=4), load=colL)
        ct = small(94)
        ctv = ct.rearrange("p (j r) -> p j r", j=2)
        l_col = t_

        class Slot:
            def __init__(self, kb):
                self.kb, self.load, self.used = kb, Load(sem()), []

        slots = {}

        def slot(kb):
            if kb not in slots:
                slots[kb] = Slot(kb)
            return slots[kb]

        w_in = A["w_in"][0].rearrange("(p c) n -> p c n", c=8)
        PB = Banks(banks, [0, 1, 2, 3, 4, 5, 6, 7])

        def stats(src, n, bn, mv, w):
            a = VE(lambda e: e.bn_stats(bn[:, 0:6], src[:, 0:512]), w)
            b = VE(lambda e: e.bn_stats(bn[:, 6:12], src[:, 512:1024]))
            return VE(lambda e: e.bn_aggr(mv, bn[:, 0:12]), a, b)

        class Two:

            def __init__(self, hi, lo, m):
                self.hi, self.lo, self.m = hi, lo, m

        def two_rows(kh, kl, n):
            k = n / 256
            return [rounded(kh + k * c, n) for c in range(8)], [rounded(kl + k * c, n) for c in range(8)]

        parts_at = {}

        def parts(kb):
            if kb not in parts_at:
                parts_at[kb] = [rounded(kb + 4 * i, 1024) for i in range(4)]
            return parts_at[kb]

        class Stream:

            def __init__(self, pieces):
                self.pieces, self.raw, self.two, self.at, self.freed = pieces, [], [], 0, 0
                self.fetch()

            def fetch(self):
                n = len(self.raw)
                if n == len(self.pieces) or self.pieces[n][0] in [p[0] for p in self.pieces[self.freed:n]]:
                    return
                kb, srcs, R, n = self.pieces[len(self.raw)]
                s = slot(kb)
                dst = mem(kb + 8, [R, n])
                for src, o, m in srcs:
                    ld = dma(SY, dst[:, :, o:o + m], src, list(s.used), load=s.load)
                s.used = []
                self.raw.append(ld)
                self.fetch()

            def split(self):
                i = len(self.two)
                if i == len(self.raw):
                    return
                kb, _, R, n = self.pieces[i]
                h0, h1, l0, l1 = parts(kb)
                w = R // 2 * n
                hi, lo, m = [], [], []
                for q, (h, l) in enumerate(((h0, l0), (h1, l1))):
                    src = mem(kb + 8, [R * n])[:, w * q:w * q + w]
                    if w == 1024 or q == 0:
                        lv = l[:, 0:w]
                    else:
                        lv = rounded(kb + 8 + w / 256, w)
                    a = act(h[:, 0:w], src, ACT.Copy, self.raw[i])
                    m.append(tt(lv, src, h[:, 0:w].bitcast(F32), SUB, a, self.raw[i]))
                    for r in range(R // 2):
                        hi.append(h[:, r * n:r * n + n])
                        lo.append(lv[:, r * n:r * n + n])
                self.two.append(Two(hi, lo, m))

            def get(self):
                if len(self.two) == self.at:
                    self.split()
                self.at += 1
                return self.two[self.at - 1]

            def done(self, last):
                slots[self.pieces[self.freed][0]].used = [last]
                self.freed += 1
                self.fetch()

        def mm3(o, l, r, c, ls, rs, first, last, *w):
            mm(o, l.hi[c][:, ls], r.hi[c][:, rs], first, False, *w)
            mm(o, l.hi[c][:, ls], r.lo[c][:, rs], False, False)
            return mm(o, l.lo[c][:, ls], r.hi[c][:, rs], False, last)

        def split_major(n, get, tstat, center, dst, scale, shift, w, tok0=0, at=range(112, 144, 4)):
            tmp = [mem(at[i], [D]) for i in range(n)]
            norm = []
            for i in range(n):
                if i % 2:
                    if center:
                        norm.append(ts(tmp[i], get(i), rs8[:, i:i + 1], nb8[:, i:i + 1], MUL, ADD, tstat))
                    else:
                        norm.append(ts(tmp[i], get(i), rs8[:, i:i + 1], None, MUL, None, tstat))
                elif center:
                    norm.append(act(tmp[i], get(i), ACT.Identity, tstat, scale=rs8[:, i:i + 1], bias=nb8[:, i:i + 1]))
                else:
                    norm.append(act(tmp[i], get(i), ACT.Copy, tstat, scale=rs8[:, i:i + 1]))
            for q in range((n + 3) // 4):
                m = min(4, n - 4 * q)
                for c in range(8):
                    b, ps, fr = PB.take()
                    for j in range(m):
                        last = tr(ps[:, 128 * j:128 * j + 128], tmp[4 * q + j][:, c::8], cst("ident"), norm[4 * q + j], fr, w)
                    s_ = slice(tok0 + 512 * q, tok0 + 512 * q + 128 * m)
                    src, h, l = ps[:, 0:128 * m], dst.hi[c][:, s_], dst.lo[c][:, s_]
                    if shift is None:
                        a = act(h, src, ACT.Copy, last, scale=scale[:, c:c + 1])
                        d = stt(l, src, scale[:, c:c + 1], h.bitcast(F32), MUL, SUB, a, norm)
                    else:
                        if c % 2:
                            a = ts(src, src, scale[:, c:c + 1], shift[:, c:c + 1], MUL, ADD, last)
                        else:
                            a = act(src, src, ACT.Identity, last, scale=scale[:, c:c + 1], bias=shift[:, c:c + 1])
                        a = act(h, src, ACT.Copy, a)
                        d = tt(l, src, h.bitcast(F32), SUB, a, norm)
                    PB.free[b] = d
                    dst.m.append(d)
            return dst.m

        bnb = small(12)
        mv = small(16)
        mvv = mv.rearrange("p (t k) -> p t k", k=2)
        rs8 = small(8)
        nb8 = small(8)
        sq8 = small(8)

        def token_stats(n, get, waits, rms):
            last = None
            for i in range(n):
                last = stats(get(i), 1024, bnb, mvv[:, i, :], [waits[i], last])
            if rms:
                a = tt(sq8[:, 0:n], mvv[:, 0:n, 0], mvv[:, 0:n, 0], MUL, last)
                b = tt(sq8[:, 0:n], sq8[:, 0:n], mvv[:, 0:n, 1], ADD, a)
                c = rsq(rs8[:, 0:n], sq8[:, 0:n], 1, b)
                return c
            c = rsq(rs8[:, 0:n], mvv[:, 0:n, 1], 1, last)
            return stt(nb8[:, 0:n], mvv[:, 0:n, 0], -1.0, rs8[:, 0:n], MUL, MUL, c)

        def channel_major(n, get, tstat, tmpkb, dst, gain, w, on_norm):
            done = []
            free = None
            for q in range(n // 4):
                tmp = [mem(tmpkb + 4 * j, [D]) for j in range(4)]
                norm, kept = [], None
                for j in range(4):
                    i = 4 * q + j
                    norm.append(stt(tmp[j], get(i), rs8[:, i:i + 1], gain, MUL, MUL, tstat, free))
                    kept = on_norm(i, tmp[j], norm[-1])
                for c in range(8):
                    b, ps, fr = PB.take()
                    for j in range(4):
                        last = tr(ps[:, 128 * j:128 * j + 128], tmp[j][:, c::8], cst("ident"), norm[j], fr, w)
                    d = cp((AC, VE)[c % 2], dst[:, c, 512 * q:512 * q + 512], ps[:, :], last)
                    PB.free[b] = d
                    done.append(d)
                free = [last, kept]
            return done

        for j in range(2):
            last = tr(banks[7][:, 47 * j:47 * j + 47], rows[0:47, 128 * j:128 * j + 128],
                      cst("ident")[0:47, 0:47], l_c, l_col)
        l_ct = cp(VE, ct, banks[7][:, 0:94], last)
        PB.free[7] = l_ct

        def tap(j, r):
            return ctv[:, j, r:r + 1]

        CDB, CLG, CLB, CPB, LCW, LCB, LBA, LBX, LAM, ONG = 31, 32, 33, 34, 35, 39, 40, 41, 42, 43
        tx = token_stats(NT, lambda i: X[:, i, :], l_x, True)
        HT2 = Two(*two_rows(32, 0, T), [])
        hT = split_major(NT, lambda i: X[:, i, :], tx, False, HT2, g1, None, [l_c, l_col, l_ct])

        QK = mem(112, [8, T])
        V = mem(144, [NT, 512])
        XRP = mem(160, [2, 1027])
        XG = mem(168.25, [2, 1024])
        UP = mem(176.25, [2, 1054])
        TB = 184.5

        CSQ = [small(1), small(1)]
        c1 = ts(CSQ[0], gq, 0.125, None, MUL, None, l_col)
        c2 = ts(CSQ[1], gk, 1.0, None, MUL, None, l_col)
        z1 = GP(lambda e: e.memset(XRP[:, :, 0:3], 0.0))
        z2 = GP(lambda e: e.memset(UP[:, :, 0:30], 0.0))

        gw = mem(TB + 12, [4, 128])
        zg = GP(lambda e: e.memset(gw, 0.0))
        gwl = Load(sem())
        for gi, nm in enumerate(("lru_wa", "lru_wx")):
            for n in range(4):
                q = 64 * (n % 2)
                l_gw = dma(GP, gw[q:q + 64, 2 * gi + n // 2, q:q + 64], A[nm][0][n], zg, load=gwl)

        def w_load(kb, src, *w, cols=512):
            dst = mem(kb, [8, 512])[:, :, 0:cols]
            s = slot(kb)
            m = dma(SY, dst, src, list(s.used), *w, load=s.load)
            s.used = []
            return dst, m

        def proj3(w, col, src, half, m=128, n=512, tok=None):
            b, ps, fr = PB.take()
            t0 = 512 * half if tok is None else tok
            for c in range(8):
                last = mm3(ps[0:m, 0:n], w, src, c, slice(col, col + m), slice(t0, t0 + n), c == 0, c == 7, fr, w.m, src.m)
            return b, ps, last

        def piece(kb, src, col, n=256):
            return kb, [(src[:, :, col:col + n], 0, n)], 8, n

        def wide(k0, k1, src, col):
            return [(kb, [(src[:, 4 * q:4 * q + 4, col:col + 512], 0, 512)], 4, 512) for q, kb in enumerate((k0, k1))]

        def joined(a, b):
            return Two(a.hi + b.hi, a.lo + b.lo, a.m + b.m)

        conf_w = [(kb, [(w_in[:, :, 2048 + 128 * j:2176 + 128 * j], 0, 128),
                        (w_in[:, :, 2304 + 128 * j:2432 + 128 * j], 128, 128)], 8, 256) for j, kb in ((0, W0), (1, W1))]
        WS = Stream([piece(W0, w_in, 1536), piece(W1, w_in, 1792)] + conf_w +
                    [piece((W0, W1)[q % 2], w_in, 256 * q) for q in range(4)] + wide(W2, W0, w_in, 1024))
        WS.split()
        sigb = [mem(TB, [512]), mem(TB + 2, [512])]
        lru_in, xg_in, up_in = [], [], []
        for j in range(4):
            if j % 2 == 0:
                w = WS.get()
            for half in range(2):
                b, ps, last = proj3(w, 128 * (j % 2), HT2, half)
                t0 = 512 * half
                if j < 2:
                    d = cp(VE, XRP[:, j, 3 + t0:3 + t0 + 512], ps[:, :], last)
                    lru_in.append(d)
                else:
                    d = act(XG[:, j - 2, t0:t0 + 512], ps[:, :], ACT.Gelu_apprx_tanh, last)
                    xg_in.append(d)
                PB.free[b] = d
            if j % 2 == 0:
                WS.split()
            else:
                WS.done(last)
        sfree = [None, None]
        k = 0
        for j in range(2):
            w = WS.get()
            for half in range(2):
                t0 = 512 * half
                bg, psg, lg = proj3(w, 128, HT2, half)
                sg = act(sigb[k % 2], psg[:, :], ACT.Sigmoid, lg, sfree[k % 2])
                PB.free[bg] = sg
                bv, psv, lv = proj3(w, 0, HT2, half)
                d = tt(UP[:, j, 30 + t0:30 + t0 + 512], psv[:, :], sigb[k % 2], MUL, lv, sg)
                PB.free[bv] = sfree[k % 2] = d
                up_in.append(d)
                k += 1
                if half == 0:
                    WS.split()
            WS.done(lv)
        XR0 = mem(160, [1024])
        YB = XG
        YC = mem(176.25, [2, 1024])
        br = {}

        def lru():
            la8, la8n, lt1, lt2 = small(2), small(2), small(2), small(2)
            lamc = ctv[:, :, LAM]
            a = act(lt1, lamc, ACT.Abs, l_ct)
            a = act(lt1, lt1, ACT.Exp, a, scale=-1.0)
            a = act(lt1, lt1, ACT.Ln, a, bias=1.0)
            b = ts(lt2, lamc, -1.0, 0.0, MUL, MAX, l_ct)
            a = tt(lt1, lt1, lt2, ADD, a, b)
            t_lan = ts(la8n, lt1, 8.0, None, MUL, None, a)
            t_la = ts(la8, lt1, -8.0, None, MUL, None, a)
            LX = [mem(W2, [1024]), mem(W2 + 4, [1024])]
            LA, LI, LTM = mem(W2 + 8, [1024]), mem(W2 + 12, [1024]), mem(TB + 14, [512])
            xconv = []
            for j in range(2):
                d = ts(LX[j], XRP[:, j, 3:1027], tap(j, LCW + 3), tap(j, LCB), MUL, ADD, lru_in, z1)
                for i in range(3):
                    d = stt(LX[j], XRP[:, j, i:i + 1024], tap(j, LCW + i), LX[j], MUL, ADD, d)
                xconv.append(d)
                yield
            lrf = gf = None
            done = []
            for j in range(2):
                LT = XRP[:, j, 0:1024]
                ends = []
                for half in range(2):
                    s0 = slice(512 * half, 512 * half + 512)
                    b1, ps1, f1 = PB.take()
                    m1 = mm(ps1[:, :], gw[:, j, :], LX[j][:, s0], True, True, l_gw, xconv[j], f1)
                    r = act(LA[:, s0], ps1[:, :], ACT.Sigmoid, m1, lrf, bias=tap(j, LBA))
                    PB.free[b1] = r
                    b2, ps2, f2 = PB.take()
                    m2 = mm(ps2[:, :], gw[:, 2 + j, :], LX[j][:, s0], True, True, f2)
                    g = act(LI[:, s0], ps2[:, :], ACT.Sigmoid, m2, lrf, bias=tap(j, LBX))
                    PB.free[b2] = g
                    ends += [r, g]
                t1 = act(LT, LA, ACT.Tanh, ends, t_lan, xconv, scale=la8n[:, j:j + 1])
                t2 = act(LA, LA, ACT.Exp, t1, t_la, scale=la8[:, j:j + 1])
                yield
                for half in range(2):
                    s0 = slice(512 * half, 512 * half + 512)
                    d = ts(LTM, LT[:, s0], 1.0, None, ADD, None, t1, gf)
                    d = VE(lambda e: e.reciprocal(LTM, LTM), d)
                    gf = d = stt(LT[:, s0], LT[:, s0], 2.0, LTM, MUL, MUL, d)
                    yield
                d = act(LT, LT, ACT.Sqrt, d)
                yield
                d = tt(LT, LT, LI, MUL, d)
                d = tt(LT, LT, LX[j], MUL, d)
                yield
                d = VE(lambda e, LT=LT: e.tensor_tensor_scan(LI, LA, LT, 0.0, MUL, ADD), d, t2)
                lrf = tt(YB[:, j, :], LI, XG[:, j, :], MUL, d, xg_in)
                done.append(lrf)
                yield
            br["yb"] = done
            br["lru_end"] = [done[-1], m1, m2]

        def conformer():
            CA, CQ, CR = mem(TB, [2, 1024]), mem(TB + 8, [2, 512]), mem(TB + 12, [512])
            pw = mem(TB + 14, [2, 256])
            o = mem(144, [1024])
            d = ts(o, UP[:, 0, 30:1054], tap(0, 30), tap(0, CDB), MUL, ADD, up_in, z2)
            for i in range(29):
                yield
                d = stt(o, UP[:, 0, i:i + 1024], tap(0, i), o, MUL, ADD, d)
            yield
            cc = [stt(CA[:, 0, :], UP[:, 0, 29:1053], tap(0, 29), o, MUL, ADD, d, br["qk_end"])]
            br["moved"] = cc[0]
            yield
            l_pw = dma(GP, pw, A["conf_pw_w"][0].rearrange("(j p) e -> p j e", p=128), br["qk_end"])
            ends = []
            for half in range(2):
                o = CA[:, 1, 512 * half:512 * half + 512]
                u = UP[:, 1, 512 * half:512 * half + 542]
                d = ts(o, u[:, 30:542], tap(1, 30), tap(1, CDB), MUL, ADD, up_in, z2, br["qk_end"])
                for i in range(30):
                    yield
                    d = stt(o, u[:, i:i + 512], tap(1, i), o, MUL, ADD, d)
                ends.append(d)
            cc.append(ends)
            yield
            cf = None
            done = []
            take = br["banks"].take
            freed = br["banks"].free
            for half in range(2):
                s0 = slice(512 * half, 512 * half + 512)
                b, cb, free = take()
                mm(cb[:, :], cst("ones"), CA[:, 0, s0], True, False, cc, free)
                m1 = mm(cb[:, :], cst("ones"), CA[:, 1, s0], False, True)
                yield
                freed[b] = xc = [stt(CA[:, j, s0], cb[:, :], -1.0 / 256, CA[:, j, s0], MUL, ADD, m1) for j in range(2)]
                yield
                sq = [act(CQ[:, j, :], CA[:, j, s0], ACT.Square, xc[j], cf) for j in range(2)]
                yield
                b, cb, free = take()
                mm(cb[:, :], cst("ones"), CQ[:, 0, :], True, False, sq[0], free)
                m2 = mm(cb[:, :], cst("ones"), CQ[:, 1, :], False, True, sq[1])
                yield
                freed[b] = r = rsq(CR, cb[:, :], 256, m2, cf)
                yield
                sl = []
                for j in range(2):
                    d = tt(CA[:, j, s0], CA[:, j, s0], CR, MUL, r)
                    d = ts(CA[:, j, s0], CA[:, j, s0], tap(j, CLG), tap(j, CLB), MUL, ADD, d)
                    yield
                    a = act(CQ[:, j, :], CA[:, j, s0], ACT.Exp, d, m2, scale=-1.0)
                    yield
                    a = ts(CQ[:, j, :], CQ[:, j, :], 1.0, None, ADD, None, a)
                    a = VE(lambda e, j=j: e.reciprocal(CQ[:, j, :], CQ[:, j, :]), a)
                    sl.append(tt(CA[:, j, s0], CA[:, j, s0], CQ[:, j, :], MUL, a))
                    yield
                for j in range(2):
                    b, cb, free = take()
                    mm(cb[:, :], pw[:, 0, 128 * j:128 * j + 128], CA[:, 0, s0], True, False, sl, l_pw, free)
                    m3 = mm(cb[:, :], pw[:, 1, 128 * j:128 * j + 128], CA[:, 1, s0], False, True)
                    yield
                    freed[b] = d = act(YC[:, j, s0], cb[:, :], ACT.Identity, m3, cc, bias=tap(j, CPB))
                    done.append(d)
                    yield
                cf = [sl, m2]
            br["yc"] = done
            br["end"] = [m3, d]

        def run(steps, n=1):
            for _ in range(n):
                next(steps, None)

        branch = lru()
        conf = conformer()
        sqb = [mem(TB + 4, [512]), mem(TB + 6, [512])]
        rb = [mem(TB + 8, [512]), mem(TB + 10, [512])]
        qk_done = {}
        sqf, rf = [None, None], [None, None]
        pend = None
        k = 0

        def qk_tail(p):
            e, half, b, ps, sq, k = p
            b2, ps2, fr2 = PB.take()
            m2 = mm(ps2[:, :], cst("bd64"), sqb[k % 2], True, True, sq, fr2)
            sqf[k % 2] = m2
            r = rsq(rb[k % 2], ps2[:, :], 64, m2, rf[k % 2])
            PB.free[b2] = r
            d = stt(QK[:, e, 512 * half:512 * half + 512], ps[:, :], CSQ[e // 4][:, 0:1], rb[k % 2], MUL, MUL, r, c1, c2)
            rf[k % 2] = d
            PB.free[b] = d
            qk_done[(e, half)] = d

        for e in range(8):
            if e % 2 == 0:
                w = WS.get()
            for half in range(2):
                b, ps, last = proj3(w, 128 * (e % 2), HT2, half)
                sq = act(sqb[k % 2], ps[:, :], ACT.Square, last, sqf[k % 2])
                if pend:
                    qk_tail(pend)
                run(conf, k < 14)
                run(branch)
                run(conf, k < 14)
                run(branch)
                pend = (e, half, b, ps, sq, k)
                k += 1
            if e % 2 == 0:
                WS.split()
            else:
                if e == 3:
                    run(branch, 100)
                    slots[W2] = Slot(W2)
                    slots[W2].used = [br["yb"], br["lru_end"]]
                WS.done(last)
        qk_tail(pend)
        run(branch, 100)
        br["qk_end"] = [list(qk_done.values()), sqf]
        while "moved" not in br:
            run(conf, 1)
        yb_done = br["yb"]
        a, b = WS.get(), WS.get()
        w = joined(a, b)
        v_done = []
        for i in range(NT):
            b, ps, fr = PB.take()
            for c in range(8):
                last = mm3(ps[:, :], HT2, w, c, slice(128 * i, 128 * i + 128), slice(0, 512), c == 0, c == 7, fr, hT, w.m)
            d = cp(AC, V[:, i, :], ps[:, :], last, br["moved"])
            PB.free[b] = d
            v_done.append(d)
        WS.done(last)
        WS.done(last)
        ht_free = last
        YT = HT
        PT1 = [mem(48 + 2 * i, [512]) for i in range(2)]
        PSP = [mem(52 + 2 * i, [512]) for i in range(3)]
        PW_ = [mem(58 + 2 * i, [512]) for i in range(3)]
        PRS = [mem(160 + 2 * i, [512]) for i in range(4)]
        items = [(hp, qc, kb, h) for hp in range(4) for qc in range(2) for kb in range(4 * qc + 3, -1, -1)
                 for h in (2 * hp, 2 * hp + 1)]
        att_w = [br["lru_end"], yb_done, list(qk_done.values()), ht_free]
        br["banks"] = AZ = Banks(banks, [0, 1, 2, 3, 4, 5])
        AZ.free = dict(PB.free)
        z_, sp_, w_, lane_r = {}, {}, {}, {}
        t1f, spf, wf = [att_w] * 2, [att_w] * 3, [att_w] * 3
        rsum = {}
        ya_done = []
        ofree = [PB.free.get(6), PB.free.get(7)]
        rf_ = [att_w] * 4

        def ext(i):
            hp, qc, kb, h = items[i]
            lo = max(0, kb - 4 * qc) * 128
            return hp, qc, kb, h, lo

        def stage_z(i):
            hp, qc, kb, h, lo = ext(i)
            b, ps, fr = AZ.take()
            q0 = 64 * (h % 2)
            m = mm(ps[:, lo:512], QK[q0:q0 + 64, 4 + hp, 128 * kb:128 * kb + 128],
                   QK[q0:q0 + 64, hp, 512 * qc + lo:512 * qc + 512], True, True, fr, att_w if i < 6 else None)
            z_[i] = (b, ps, m)

        def stage_sp(i):
            hp, qc, kb, h, lo = ext(i)
            b, ps, m = z_[i]
            k = i % 2
            t1 = act(PT1[k][:, lo:], ps[:, lo:512], ACT.Abs, m, t1f[k])
            t2 = act(PT1[k][:, lo:], PT1[k][:, lo:], ACT.Exp, t1, scale=-1.0)
            t3 = act(PT1[k][:, lo:], PT1[k][:, lo:], ACT.Ln, t2, bias=1.0)
            j = i % 3
            d = stt(PSP[j][:, lo:], ps[:, lo:512], 0.0, PT1[k][:, lo:], MAX, ADD, t3, spf[j])
            t1f[k] = d
            if kb >= 4 * qc:
                v = PSP[j][:, lo:lo + 128]
                d = GP(lambda e: e.affine_select(out=v, in_=v, compare_op=ALU.is_gt, fill=0.0, base=0,
                                                 pattern=[[1, 128]], channel_multiplier=-1), d)
            sp_[i] = d

        def stage_c(i):
            hp, qc, kb, h, lo = ext(i)
            b, ps, m = z_[i]
            k = i % 3
            top = 4 * qc + 3
            m = mm(ps[:, lo:512], cst("ntri"), PSP[k][:, lo:], False, kb == top, sp_[i])
            rk = 2 * (qc % 2) + h % 2
            R = PRS[rk]
            if kb < top:
                prev = max(0, kb + 1 - 4 * qc) * 128
                m = mm(ps[:, prev:512], cst("nones"), R[:, prev:], False, True, rsum[rk])
            if kb > 0:
                if kb == top:
                    if lo > 0:
                        GP(lambda e: e.memset(R[:, 0:lo], 0.0), rf_[rk])
                    g = cp(GP, R[:, lo:], PSP[k][:, lo:], sp_[i], rf_[rk], m)
                    rsum[rk] = g
                else:
                    g = tt(R[:, lo:], R[:, lo:], PSP[k][:, lo:], ADD, m, sp_[i], rsum[rk], lane=GP)
                    rsum[rk] = g
                spf[k] = [m, g]
            else:
                rf_[rk] = m
                spf[k] = m
            w = act(PW_[k][:, lo:], ps[:, lo:512], ACT.Exp, m, wf[k])
            AZ.free[b] = w
            if kb >= 4 * qc:
                v = PW_[k][:, lo:lo + 128]
                w = GP(lambda e: e.affine_select(out=v, in_=v, compare_op=ALU.is_gt, fill=0.0, base=0,
                                                 pattern=[[1, 128]], channel_multiplier=-1), w)
            w_[i] = w

        def stage_pv(i):
            hp, qc, kb, h, lo = ext(i)
            k = i % 3
            ob = banks[6 + qc % 2]
            q0 = 64 * (h % 2)
            top = 4 * qc + 3
            m = mm(ob[q0:q0 + 64, lo:512], V[:, kb, 64 * h:64 * h + 64], PW_[k][:, lo:], kb == top, kb == 0,
                   w_[i], v_done, ofree[qc % 2] if kb == top else None)
            wf[k] = m
            if kb == 0:
                d = cp(VE, YT[q0:q0 + 64, hp, 512 * qc:512 * qc + 512], ob[q0:q0 + 64, :], m, ht_free)
                ofree[qc % 2] = [ofree[qc % 2], d] if h % 2 else d
                ya_done.append(d)

        zrow = mem(W2 + 12, [512])
        tz0 = GP(lambda e: e.memset(zrow, 0.0), att_w)
        ysl = nc.dram_tensor("ysl", [NBLK * 128, D], F32).ap()
        yzl = Load(sem())
        for b in range(NEXP, NBLK):
            t_yz = dma(SY, ysl[128 * b:128 * b + 128, :].rearrange("p (q n) -> p q n", q=2),
                       zrow.unsqueeze(1).broadcast_to([128, 2, 512]), tz0, load=yzl)
        l_xr = [xL[i](SY, X[:, i, :], xs[:, i, :], ht_free) for i in range(NT)]
        w_o = A["w_out"][0].rearrange("(j p) n -> p j n", p=128)
        WO = mem(W0, [8, 1024])
        l_wo = []
        for q in range(2):
            s = slots[(W0, W1)[q]]
            l_wo.append(dma(SY, WO[:, 4 * q:4 * q + 4, :], w_o[:, 4 * q:4 * q + 4, :], s.used, load=s.load))
            s.used = []
        WH = [rounded((96 + 4 * j) if j < 4 else (32 + 4 * j), 1024) for j in range(8)]
        WL = [rounded(W0 + 4 * j, 1024) for j in range(8)]
        wo_m = []

        def split_wo(j, *w):
            a = act(WH[j], WO[:, j, :], ACT.Copy, l_wo, w)
            wo_m.append(tt(WL[j], WO[:, j, :], WH[j].bitcast(F32), SUB, a))

        LAG1, LAG2 = 3, 5
        AC(lambda e: e.preload_act_table_set("natural_log_exp_and_others"))
        n = len(items)
        for s in range(n + LAG2):
            if s < n:
                stage_z(s)
                stage_sp(s)
            run(conf, 1)
            if 0 <= s - LAG1 + 1 < n:
                stage_c(s - LAG1 + 1)
            if 0 <= s - LAG2 + 1 < n:
                stage_pv(s - LAG2 + 1)
            run(conf, 1)
            if s in (60, 64, 68, 72):
                split_wo((s - 60) // 4, t_yz, br["lru_end"])
        run(conf, 100)
        yc_done = br["yc"]
        for b in range(6):
            PB.free[b] = AZ.free.get(b)
        PB.free[6], PB.free[7] = ofree

        att_end = ya_done[-1]

        def yt(j):
            return YT[:, j, :] if j < 4 else YB[:, j - 4, :] if j < 6 else YC[:, j - 6, :]

        NSQ = [mem(TB + 2 * i, [512]) for i in range(8)]
        NR = [mem(112 + 2 * i, [512]) for i in range(6)]
        YH = [rounded(124 + 4 * j, 1024) for j in range(8)]
        YL = [rounded(32 + 4 * j if j < 4 else 152.25 + 4 * j if j < 6 else 152.25 + 4 * j, 1024) for j in range(8)]
        nf = [None] * 8
        yn = []
        k = 0
        def out_norm(half):
            s0 = slice(512 * half, 512 * half + 512)
            groups = ((4, 6, yb_done), (6, 8, yc_done), (0, 4, ya_done))
            rs = []
            for t, (j0, j1, dn) in enumerate(groups):
                b, ps, fr = PB.take()
                for j in range(j0, j1):
                    q = act(NSQ[j], yt(j)[:, s0], ACT.Square, dn, att_end, yc_done, nf[j])
                    nf[j] = last = mm(ps[:, :], cst("ones"), NSQ[j], j == j0, j == j1 - 1, q, fr)
                if t:
                    rs.append(rsq(NR[3 * half + t - 1], pv, 128 * (jp1 - jp0), lastp))
                    PB.free[bp] = rs[-1]
                pv, jp0, jp1, lastp, bp = ps[:, :], j0, j1, last, b
            rs.append(rsq(NR[3 * half + 2], pv, 512, lastp))
            PB.free[bp] = rs[-1]
            ys = []
            for t, (j0, j1, dn) in enumerate(groups):
                for j in range(j0, j1):
                    y = yt(j)[:, s0]
                    d = stt(y, y, ctv[:, j % 2, ONG + j // 2:ONG + j // 2 + 1], NR[3 * half + t], MUL, MUL, rs[t])
                    ys.append((j, y, act(YH[j][:, s0], y, ACT.Copy, d)))
            ends = [tt(YL[j][:, s0], y, YH[j][:, s0].bitcast(F32), SUB, a) for j, y, a in ys]
            yn.append(ends)

        out_norm(0)
        for j in range(4, 8):
            split_wo(j, ya_done, wf)
        Y2, WO2_ = Two(YH, YL, None), Two(WH, WL, None)
        x1 = []
        for i in range(NT):
            for q in range(2):
                b, ps, fr = PB.take()
                for j in range(8):
                    last = mm3(ps[:, :], Y2, WO2_, j, slice(128 * i, 128 * i + 128), slice(512 * q, 512 * q + 512),
                               j == 0, j == 7, fr, wo_m, yn[i // 4])
                d = tt(X[:, i, 512 * q:512 * q + 512], ps[:, :], X[:, i, 512 * q:512 * q + 512], ADD, last, l_xr)
                PB.free[b] = d
            x1.append(d)
            if i == 0:
                out_norm(1)
        slots[W0].used = slots[W1].used = [last]
        yt_free = last

        ada_d = nc.dram_tensor("ada_d", [2, 2, 3072], F32).ap()
        cnd = small(16)
        SCND = small(16)
        cl = Load(sem())
        dma(GP, cnd[:, 0:8], A["c_2"][0].rearrange("(p c) -> p c", c=8), load=cl)
        t_cl = dma(GP, cnd[:, 8:16], A["c_ctx_2"].rearrange("(p c) -> p c", c=8), load=cl)
        t_scnd = act(SCND, cnd, ACT.Silu, t_cl)
        sc2 = SCND.rearrange("p (m c) -> p c m", m=2)
        ARW = [mem(192, [512], p=2), mem(194, [512], p=2)]
        ABI = [mem(196, [512], p=2), mem(198, [512], p=2)]
        aw_l = [Load(sem()), Load(sem())]
        ab_l = [Load(sem()), Load(sem())]
        as_l = [Load(sem()), Load(sem())]
        asf, abf = [att_end, att_end], [att_end, att_end]
        t_ada = [None, None]
        ada_w = {}
        ADA_AT = [(W0, W1), (112, 128)]

        def ada_load(n):
            l, ch, k = n // 6, n % 6, n % 2
            kb = ADA_AT[l][k]
            dst, m = w_load(kb, A["ada_w_2"][l].rearrange("(p c) n -> p c n", c=8)[:, :, 512 * ch:512 * ch + 512])
            bi = dma(SY, ABI[k], A["ada_b_2"][l:l + 1, 512 * ch:512 * ch + 512].broadcast_to([2, 512]), abf[k], load=ab_l[k])
            ada_w[n] = (dst, m, bi)

        def ada_chunk(n):
            l, ch, k = n // 6, n % 6, n % 2
            dst, m, bi = ada_w[n]
            b, ps, fr = PB.take()
            for c in range(8):
                last = mm(ps[0:2, :], sc2[:, c, :], dst[:, c, :], c == 0, c == 7, fr, t_scnd, m)
            slots[ADA_AT[l][k]].used = [last]
            d = tt(ARW[k], ps[0:2, :], ABI[k], ADD, last, bi, asf[k])
            PB.free[b] = d
            abf[k] = d
            t_ada[k] = asf[k] = dma(SY, ada_d[l, :, 512 * ch:512 * ch + 512], ARW[k], d, load=as_l[k])


        def ada_chunks(n0, n1):
            for n in range(n0, n1):
                if n % 6 == 0:
                    ada_load(n)
                    ada_load(n + 1)
                ada_chunk(n)
                if n % 6 < 4:
                    ada_load(n + 2)

        h2d = nc.dram_tensor("h2d", [T + 1, D], F32).ap()
        std = nc.dram_tensor("std", [NBLK * 128, 1], I32).ap()
        H2T = mem(128, [8, T])
        WR = mem(33, [8, 36])
        zr = mem(56, [1024], p=1)
        l_wr = Load(sem())
        dma(SY, WR[:, :, 0:4], A["router_coarse"][0].rearrange("(p c) g -> p c g", c=8), yt_free, load=l_wr)
        t_wr = dma(SY, WR[:, :, 4:36], A["router_fine"][0].rearrange("(p c) g -> p c g", c=8), load=l_wr)
        d = VE(lambda e: e.memset(zr, 0.0), yt_free)
        h2_st = Load(sem())
        t_h2 = [dma(AC, h2d[T:T + 1, :], zr, d, load=h2_st)]
        tx = token_stats(NT, lambda i: X[:, i, :], x1, True)

        def keep_row(i, tmp, norm):
            t_h2.append(dma(AC, h2d[128 * i:128 * i + 128, :], tmp, norm, load=h2_st))
            return t_h2[-1]

        G2R = mem(W2, [1024])
        l_g2r = dma(SY, G2R, A["norm2_g"].broadcast_to([128, 1024]), yt_free, t_yz, att_end)
        h2T = channel_major(NT, lambda i: X[:, i, :], [tx, yn[-1], att_end, l_g2r], 112, H2T, G2R, [], keep_row)
        b, ps, fr = PB.take()
        for i in range(NT):
            for c in range(8):
                last = mm(ps[:, 36 * i:36 * i + 36], H2T[:, c, 128 * i:128 * i + 128], WR[:, c, :], c == 0, c == 7,
                          fr, t_wr, h2T)
        lg_end = last
        ada_chunks(0, 4)
        rt_at = [34.5]

        def tmp(*shape):
            n = 1
            for s in shape:
                n *= s
            ap = mem(rt_at[0], list(shape))
            rt_at[0] += n / 256
            return ap

        L = tmp(8, 36)
        d = cp(VE, L, ps[:, 0:288].rearrange("p (a b) -> p a b", a=8), last)
        PB.free[b] = d
        LC, LF = L[:, :, 0:4], L[:, :, 4:36]
        i4 = cst("iota")[:, 0:4].unsqueeze(1).broadcast_to([128, 8, 4])
        i32_ = cst("iota")[:, 0:32].unsqueeze(1).broadcast_to([128, 8, 32])

        def bc(v, n):
            return v.unsqueeze(2).broadcast_to([128, 8, n])

        def red(o, i, op, *w):
            return VE(lambda e: e.tensor_reduce(o, i, AX, op), *w)

        def onehot(o, i, v, n, iota, *w):
            idx = tmp(8)
            a = tt(o, i, bc(v, n), ALU.is_equal, *w)
            a = ts(o, o, -64.0, 64.0, MUL, ADD, a)
            a = tt(o, o, iota, ADD, a)
            a = red(idx, o, MIN, a)
            return tt(o, iota, bc(idx, n), ALU.is_equal, a)

        mc, ec, oc, sc, wg_ = tmp(8), tmp(8, 4), tmp(8, 4), tmp(8), tmp(8)
        a = red(mc, LC, MAX, d)
        b_ = tt(ec, LC, bc(mc, 4), SUB, a)
        b_ = act(ec, ec, ACT.Exp, b_)
        b_ = red(sc, ec, ADD, b_)
        t_wg = VE(lambda e: e.reciprocal(wg_, sc), b_)
        a = onehot(oc, LC, mc, 4, i4, a)
        mask, pen, LM = tmp(8, 32), tmp(8, 32), tmp(8, 32)
        a = cp(VE, mask.rearrange("p a (g e) -> p a g e", g=4), oc.unsqueeze(3).broadcast_to([128, 8, 4, 8]), a)
        a1 = ts(pen, mask, -1.0, 1e30, ADD, MUL, a)
        a = tt(LM, LF, mask, MUL, a)
        a = tt(LM, LM, pen, ADD, a, a1)
        m1, m2, o1, o2 = tmp(8), tmp(8), tmp(8, 32), tmp(8, 32)
        d1 = red(m1, LM, MAX, a)
        a = onehot(o1, LM, m1, 32, i32_, d1)
        a1 = ts(pen, o1, -1e30, None, MUL, None, a)
        a1 = tt(LM, LM, pen, ADD, a1)
        d2 = red(m2, LM, MAX, a1)
        a2 = onehot(o2, LM, m2, 32, i32_, d2)
        G1 = small(8)
        G2 = small(8)
        e2, s2 = tmp(8), tmp(8)
        a3 = tt(e2, m2, m1, SUB, d2)
        a3 = act(e2, e2, ACT.Exp, a3)
        a3 = ts(s2, e2, 1.0, None, ADD, None, a3)
        a3 = VE(lambda e: e.reciprocal(s2, s2), a3)
        a3 = tt(G1, s2, wg_, MUL, a3, t_wg)
        t_g = tt(G2, G1, e2, MUL, a3)
        OO = tmp(8, 32)
        PR = tmp(8, 32)
        a = tt(OO, o1, o2, ADD, a2)
        z_a = VE(lambda e: e.memset(PR[:, 0, :], 0.0), a)
        pr = z_a
        for i in range(1, 8):
            pr = tt(PR[:, i, :], PR[:, i - 1, :], OO[:, i - 1, :], ADD, pr)
        TOT = tmp(32)
        pr2 = tt(TOT, PR[:, 7, :], OO[:, 7, :], ADD, pr)
        b, ps, fr = PB.take()
        mm(ps[:, 0:256], cst("sltu"), OO.rearrange("p a b -> p (a b)"), True, False, a, fr)
        last = mm(ps[:, 0:256], cst("ones"), PR.rearrange("p a b -> p (a b)"), False, True, pr)
        b2, ps2, fr2 = PB.take()
        last2 = mm(ps2[:, 0:32], cst("ones"), TOT, True, True, pr2, fr2)
        NV, NVI, TMPV = tmp(32), tmp(32), tmp(32)
        CN = tmp(32)
        d = cp(VE, CN, ps2[:, 0:32], last2)
        PB.free[b2] = d
        a = ts(NV, CN, float(CAP), None, ALU.is_gt, None, d)
        for k in range(2, 8):
            a = stt(NV, CN, float(CAP * k), NV, ALU.is_gt, ADD, a)
        ON = tmp(32)
        o_ = VE(lambda e: e.memset(ON, 1.0))
        a = VE(lambda e: e.tensor_tensor_scan(NVI, ON, NV, 0.0, MUL, ADD), a, o_)
        BO = tmp(32)
        c = tt(BO, NVI, NV, SUB, a)
        c = ts(BO, BO, 31.0, 128.0, ADD, MUL, c)
        c = tt(BO, BO, cst("eidx"), SUB, c)
        PO = tmp(8, 32)
        OV = tmp(8, 32)
        d = cp(VE, PO, ps[:, 0:256].rearrange("p (a b) -> p a b", a=8), last)
        PB.free[b] = d
        e_ = ts(OV, PO, float(CAP), None, ALU.is_ge, None, d)
        e_ = tt(OV, OV, BO.unsqueeze(1).broadcast_to([128, 8, 32]), MUL, e_, c)
        e_ = tt(PO, PO, OV, ADD, e_)
        e_ = tt(PO, PO, cst("eidx").unsqueeze(1).broadcast_to([128, 8, 32]), ADD, e_)
        PS_ = tmp(8, 2)
        for k, o in enumerate((o1, o2)):
            a = tt(OV, PO, o, MUL, e_)
            e_ = red(PS_[:, :, k], OV, ADD, a)
        POSI = small(16).bitcast(I32).rearrange("p (a b) -> p a b", a=8)
        t_pos = cp(VE, POSI, PS_, e_)
        TOKI = small(8).bitcast(I32)
        t_tok = cp(VE, TOKI, cst("tok"), l_c)
        EB = tmp(15, 32)
        EF = tmp(16)
        io15 = cst("iota")[:, 0:15].unsqueeze(2).broadcast_to([128, 15, 32])
        a = tt(EB, NVI.unsqueeze(1).broadcast_to([128, 15, 32]), io15, ALU.is_le, c)
        a = red(EF[:, 0:15], EB, ADD, a)
        a = ts(EF[:, 0:15], EF[:, 0:15], 31.0, None, MIN, None, a)
        b_ = cp(VE, EF[:, 15:16], NVI[:, 31:32], c)
        EI = small(16).bitcast(I32)
        t_ei = cp(VE, EI, EF, a, b_)
        INI = mem(60, [128], p=NBLK).bitcast(I32)
        d = VE(lambda e: e.memset(INI, T), yt_free)
        stdL = Load(sem())
        t_ini = dma(GP, std[:, :].rearrange("(b s) o -> b (s o)", s=128), INI, d, load=stdL)
        stdS = Load(sem())

        def indirect(load, lane, *w, **kw):
            load.n += 16
            lane(lambda e: e.indirect_dma_start(**kw).then_inc(load.sem, 16), *w)
            return Landed(load.sem, load.n)

        for i in range(NT):
            for k in range(2):
                t_sc = indirect(stdS, GP, t_ini, t_pos, t_tok, out=std[:, :],
                                out_offset=bass.IndirectOffsetOnAxis(ap=POSI[:, i, k:k + 1].bitcast(U32), axis=0),
                                in_=TOKI[:, i:i + 1], in_offset=None)
        ada_chunks(4, 6)
        STI = mem(60.5, [128], p=NBLK).bitcast(I32)
        STF = mem(61, [128], p=NBLK)
        t_st = dma(GP, STI, std[:, :].rearrange("(b s) o -> b (s o)", s=128), t_sc, h2T)
        d = cp(VE, STF, STI, t_st)
        b, ps, fr = PB.take()
        last = tr(ps[:, 0:NBLK], STF, cst("ident")[0:NBLK, 0:NBLK], d, fr)
        TAB = small(NBLK).bitcast(I32)
        t_tab = cp(VE, TAB, ps[:, 0:NBLK], last)
        PB.free[b] = t_tab
        routed = [t_tab, t_ei, t_g, t_pos]

        RING = [96, 64, 80, 112, 128, 144, 160]
        for kb in RING:
            slot(kb)
        slots[96].used = [yn[-1], att_end, t_yz, yt_free, h2T, t_h2[-1]]
        slots[112].used = [h2T[-1], h2T[-2], h2T[-3], t_h2[-1], lg_end]
        slots[128].used = slots[144].used = h2T + [lg_end]
        slots[160].used = [yt_free]
        GW, UW, DW = ("exp_w_gate", 8, 512), ("exp_w_up", 8, 512), ("exp_w_down", 4, 1024)
        turns = [(0, GW)]
        for e in range(NEXP):
            turns += [(e, UW), (e + 1, GW), (e, DW)]
        pieces = []
        for e, (nm, c, n) in turns:
            if e < NEXP:
                for q in range(2):
                    r = slice(c // 2 * q, c // 2 * q + c // 2)
                    pieces.append((RING[len(pieces) % len(RING)], [(A[nm][0, e].rearrange("(p c) n -> p c n", c=c)[:, r, :], 0, n)],
                                   c // 2, n))

        XGB = [mem(32, [1024]), mem(36, [1024])]
        XTB = [mem(40, [8, 128]), mem(44, [8, 128])]
        SGB = [mem(48, [512]), mem(50, [512])]
        HDB = [mem(52, [512]), mem(54, [512])]
        HTB = [mem(56, [4, 128]), mem(58, [4, 128])]
        YB = [mem(60, [1024]), mem(192, [1024])]

        class Experts:

            def __init__(self, start):
                self.xg, self.xt = [start] * 2, [start] * 2
                self.sg, self.hd, self.ht, self.y = [start] * 2, [start] * 2, [start] * 2, [start] * 2
                self.bank = [[PB.free.get(b), start] for b in range(8)]
                self.gl = [Load(sem()), Load(sem())]
                self.yl = [Load(sem()), Load(sem())]

            def gather(self, n, blk):
                k = n % 2
                return indirect(self.gl[k], GP, self.xg[k], t_tab, t_h2[-1], out=XGB[k], out_offset=None, in_=h2d,
                                in_offset=bass.IndirectOffsetOnAxis(ap=TAB[:, blk:blk + 1].bitcast(U32), axis=0))

            def turn(self, n, t_g):
                k = n % 2
                done = []
                for q in range(2):
                    ps = banks[q]
                    for c in range(4):
                        last = tr(ps[:, 128 * c:128 * c + 128], XGB[k][:, 4 * q + c::8], cst("ident"), t_g, self.bank[q])
                    d = cp(VE, XTB[k][:, 4 * q:4 * q + 4, :], ps[:, :].rearrange("p (a b) -> p a b", a=4), last, self.xt[k])
                    self.bank[q] = d
                    done.append(d)
                self.xg[k] = last
                return done

            def up(self, n, xt, w):
                k = n % 2
                for v in range(2):
                    dst, ld, s = w[v]
                    for c in range(8):
                        last = mm(banks[2 + v][:, :], XTB[k][:, c, :], dst[:, c, :], c == 0, c == 7, xt, ld, self.bank[2 + v])
                    s.used = [last]
                    if v == 0:
                        sg = act(SGB[k], banks[2][:, :], ACT.Silu, last, self.sg[k])
                        self.bank[2] = sg
                self.xt[k] = last
                hd = tt(HDB[k], banks[3][:, :], SGB[k], MUL, last, sg, self.hd[k])
                self.bank[3] = self.sg[k] = hd
                return hd

            def down(self, n, hd, w, blk):
                k = n % 2
                for j in range(4):
                    last = tr(banks[4][:, 128 * j:128 * j + 128], HDB[k][:, j::4], cst("ident"), hd, self.bank[4])
                self.hd[k] = last
                ht = cp(AC, HTB[k], banks[4][:, :].rearrange("p (a b) -> p a b", a=4), last, self.ht[k])
                self.bank[4] = ht
                dst, ld, s = w[2]
                ev = []
                for q in range(2):
                    for j in range(4):
                        last = mm(banks[5 + q][:, :], HTB[k][:, j, :], dst[:, j, 512 * q:512 * q + 512], j == 0, j == 3,
                                  ht, ld, self.bank[5 + q])
                    e = cp((VE, AC)[q], YB[k][:, 512 * q:512 * q + 512], banks[5 + q][:, :], last, self.y[k])
                    self.bank[5 + q] = e
                    ev.append(e)
                s.used = [last]
                self.ht[k] = last
                self.y[k] = dma(AC, ysl[128 * blk:128 * blk + 128, :], YB[k], ev, load=self.yl[k])
                return self.y[k]

        class Split(Experts):

            def __init__(self, start):
                super().__init__(start)
                self.WS = Stream(pieces)
                self.xh = [[rounded(o + 2 * q, 512) for q in range(4)] for o in (40, 176)]
                self.hh = [[rounded(o + 2 * q, 512) for q in range(2)] for o in (56, 184)]

            def take(self):
                w = self.WS.get()
                while len(self.WS.two) < min(self.WS.at + 3, len(self.WS.raw)):
                    self.WS.split()
                return w

            def turn(self, n, t_g):
                k = n % 2
                hi, lo, done = [], [], []
                for q in range(2):
                    ps = banks[q]
                    for c in range(4):
                        last = tr(ps[:, 128 * c:128 * c + 128], XGB[k][:, 4 * q + c::8], cst("ident"), t_g, self.bank[q])
                    h, l = self.xh[k][q], self.xh[k][2 + q]
                    a = act(h, ps[:, :], ACT.Copy, last, self.xt[k])
                    d = tt(l, ps[:, :], h.bitcast(F32), SUB, a, self.xt[k])
                    self.bank[q] = d
                    done.append(d)
                    hi += [h[:, 128 * c:128 * c + 128] for c in range(4)]
                    lo += [l[:, 128 * c:128 * c + 128] for c in range(4)]
                self.xg[k] = last
                return Two(hi, lo, done)

            def product(self, n, v, xt, mid):
                k = n % 2
                for q in range(2):
                    w = self.take()
                    x = Two(xt.hi[4 * q:4 * q + 4], xt.lo[4 * q:4 * q + 4], None)
                    for c in range(4):
                        last = mm3(banks[2 + v][:, :], x, w, c, slice(0, 128), slice(0, 512), q + c == 0, q == 1 and c == 3,
                                   xt.m, w.m, self.bank[2 + v])
                    self.WS.done(last)
                    if q == 0:
                        mid()
                if v == 0:
                    self.bank[2] = self.silu = act(SGB[k], banks[2][:, :], ACT.Silu, last, self.sg[k])
                    return None
                self.xt[k] = last
                hd = tt(HDB[k], banks[3][:, :], SGB[k], MUL, last, self.silu, self.hd[k])
                self.bank[3] = self.sg[k] = hd
                return hd

            def turn_hidden(self, n, hd):
                k = n % 2
                for j in range(4):
                    last = tr(banks[4][:, 128 * j:128 * j + 128], HDB[k][:, j::4], cst("ident"), hd, self.bank[4])
                self.hd[k] = last
                h, l = self.hh[k]
                a = act(h, banks[4][:, :], ACT.Copy, last, self.ht[k])
                self.bank[4] = self.hid = tt(l, banks[4][:, :], h.bitcast(F32), SUB, a, self.ht[k])

            def down(self, n, blk):
                k = n % 2
                h, l = self.hh[k]
                for q in range(2):
                    w = self.take()
                    x = Two([h[:, 128 * j:128 * j + 128] for j in (2 * q, 2 * q + 1)],
                            [l[:, 128 * j:128 * j + 128] for j in (2 * q, 2 * q + 1)], None)
                    for o in range(2):
                        for j in range(2):
                            last = mm3(banks[5 + o][:, :], x, w, j, slice(0, 128), slice(512 * o, 512 * o + 512),
                                       q + j == 0, q == 1 and j == 1, self.hid, w.m, self.bank[5 + o])
                        if q == 1:
                            self.bank[5 + o] = cp(AC, YB[k][:, 512 * o:512 * o + 512], banks[5 + o][:, :], last, self.y[k])
                    self.WS.done(last)
                self.ht[k] = last
                self.y[k] = dma(AC, ysl[128 * blk:128 * blk + 128, :], YB[k], self.bank[5:7], load=self.yl[k])
                return self.y[k]

        X1 = Split([yt_free, routed, t_wg, t_ada])
        gs = [X1.gather(0, 0), X1.gather(1, 1)]
        for _ in range(3):
            X1.WS.split()
        xt = {0: X1.turn(0, gs[0])}

        def turn_next(e):
            if e < NEXP:
                xt[e] = X1.turn(e, gs[e])

        X1.product(0, 0, xt[0], lambda: None)
        for e in range(NEXP):
            hd = X1.product(e, 1, xt[e], lambda: turn_next(e + 1))
            if e + 2 < NEXP:
                gs.append(X1.gather(e + 2, e + 2))
            if e + 1 < NEXP:
                X1.product(e + 1, 0, xt[e + 1], lambda: X1.turn_hidden(e, hd))
            else:
                X1.turn_hidden(e, hd)
            X1.down(e, e)
        y_end = [X1.y[0], X1.y[1]]
        pe_end = PE(lambda e: e.nop(), X1.ht)

        for l in lanes:
            l.when(EI[0:1, 15:16], t_ei, pe_end, y_end, t_yz)
        X2 = Experts(None)
        X2.bank = [None] * 8
        owl = [Load(sem()) for _ in range(3)]
        last_use = None
        for blk in range(NOV):
            w = []

            class Used:
                used = []

            reg = {}

            def expert_of(e, blk=blk, reg=reg):
                reg["e"] = e.value_load(EI[0:1, blk:blk + 1], min_val=0, max_val=31)
                return e.nop()

            SY(expert_of, last_use)
            for v, (nm, c, n, kb) in enumerate((("exp_w_gate", 8, 512, 96), ("exp_w_up", 8, 512, 64), ("exp_w_down", 4, 1024, 80))):
                dst = mem(kb, [c, n])
                owl[v].n += 16
                SY(lambda e, reg=reg, v=v, nm=nm, c=c, dst=dst: e.dma_start(
                    dst, A[nm][0, bass.ds(reg["e"], 1)].rearrange("a (p c) n -> p (a c) n", c=c)).then_inc(owl[v].sem, 16),
                   last_use)
                w.append((dst, Landed(owl[v].sem, owl[v].n), Used()))
            g_ = X2.gather(blk, NEXP + blk)
            xt = X2.turn(blk, g_)
            hd = X2.up(blk, xt, w)
            y_ = X2.down(blk, hd, w, NEXP + blk)
            last_use = X2.ht[blk % 2]
            if blk >= 1:
                AC(lambda e: e.nop(), X2.y[(blk - 1) % 2])
        for l in (SY, PE, AC, VE, GP):
            l(lambda e: e.nop(), X2.y[0], X2.y[1], last_use)
        for l in lanes:
            l.always()
        ex = [l(lambda e: e.nop()) for l in lanes]
        for l in lanes:
            l(lambda e: e.nop(), ex)
        for b in range(8):
            PB.free[b] = X1.bank[b]
        for s in slots.values():
            s.used = list(s.used) + ex

        asf, abf = [ex, ex], [ex, ex]
        CB = [mem(32 + 4 * i, [1024]) for i in range(8)]
        cbl = [Load(sem()) for _ in range(8)]
        cbf = [None] * 8
        x2 = []
        x2d = nc.dram_tensor("x2d", [NT, 128, D], F32).ap()
        x2l = Load(sem())
        k = 0
        for i in range(NT):
            d = x1[i]
            for q, G in enumerate((G1, G2)):
                ld = indirect(cbl[k % 8], GP, cbf[k % 8], ex, y_end, t_yz, t_pos, out=CB[k % 8], out_offset=None, in_=ysl,
                              in_offset=bass.IndirectOffsetOnAxis(ap=POSI[:, i, q:q + 1].bitcast(U32), axis=0))
                d = stt(X[:, i, :], CB[k % 8], G[:, i:i + 1], X[:, i, :], MUL, ADD, ld, d, t_g)
                cbf[k % 8] = d
                k += 1
            x2.append(d)
            t_x2 = dma(AC, x2d[i], X[:, i, :], d, load=x2l)
        for kb in ADA_AT[1]:
            slots[kb].used = [ex, slots[kb].used]
        ada_chunks(6, 12)

        cp2 = Load(sem())
        m = small_at[0]
        gbc, gnc, qnc, kvc = small(4), small(1), small(2), small(1)
        for o, v, n in ((gbc, A["gla_b_2"][0].rearrange("k (j p) -> p (k j)", p=128), 4),
                        (gnc, A["gla_norm_g_2"][0].rearrange("(p j) -> p j", j=1), 1),
                        (qnc, A["mla_q_norm_g_2"][0].rearrange("(j p) -> p j", p=128), 2),
                        (kvc, A["mla_kv_norm_g_2"][0].rearrange("(p j) -> p j", j=1), 1)):
            t_cp2 = dma(SY, o, v, load=cp2, allow_slow_non_contiguous=True)
        SH, SCL = {}, {}
        adl = Load(sem())
        for key, l, r in (("l0", 0, 0), ("c0", 0, 1), ("l1", 1, 0)):
            SH[key], SCL[key] = small(8), small(8)
            t_ad = dma(SY, SH[key], ada_d[l, r, 0:1024].rearrange("(p c) -> p c", c=8), t_ada, load=adl)
            t_ad = dma(SY, SCL[key], ada_d[l, r, 1024:2048].rearrange("(p c) -> p c", c=8), load=adl)
        for key in SH:
            t_scl = ts(SCL[key], SCL[key], 1.0, None, ADD, None, t_ad)

        GQ, GK, GV = mem(104, [2, 1024]), mem(112, [2, 1280]), mem(122, [10, 512])
        LK, GG = mem(142, [1280]), mem(147, [4, 1024])
        CQ, CKV, MG = mem(163, [2, 1024]), mem(171, [1280]), mem(176, [8, 512])
        SA, SB = 72, 88
        for kb in (SA, SB):
            slots[kb] = Slot(kb)
            slots[kb].used = list(slots[96].used)
        w_e = A["even_w_in_2"][0].rearrange("(p c) n -> p c n", c=8)
        CXR = mem(72, [2, 1024])
        l_cx = dma(SY, CXR, A["ctx_2"][0].rearrange("(t p) d -> p t d", p=128), ex)
        ada_end = [t_ada, slots[112].used, slots[128].used]
        tc_ = token_stats(2, lambda i: CXR[:, i, :], [[l_cx, x2[-1]], None], False)
        HC = Two(*two_rows(64, 192, 256), [])
        hC = split_major(2, lambda i: CXR[:, i, :], [tc_, ada_end], True, HC, SCL["c0"], SH["c0"], [t_scl, ex], at=(147, 151))
        for kb in (SA, 104, 147):
            slots[kb] = Slot(kb)
            slots[kb].used = [hC]
        WS = Stream(wide(104, 147, w_e, 512) + wide(SA, SB, w_e, 1984) +
                    [piece(147, w_e, 1568),
                     (SA, [(w_e[:, :, 1824:1984], 0, 160), (w_e[:, :, 1024:1056], 160, 32)], 8, 192),
                     piece(SB, w_e, 0), piece(SA, w_e, 256), piece(SB, w_e, 1056), piece(SA, w_e, 1312)])
        tx = token_stats(NT, lambda i: X[:, i, :], [[x, hC] for x in x2], False)
        HL = Two(*two_rows(32, 0, T), [])
        hL = split_major(NT, lambda i: X[:, i, :], [tx, hC, t_x2, ada_end], True, HL, SCL["l0"], SH["l0"], [t_scl],
                         at=(122, 126, 130, 134, 138, 163, 167, 171))
        hLC = [hL, hC]
        CH = [(HC, 0, 0, 256), (HL, 0, 256, 512), (HL, 512, 768, 512)]

        def cm_lc(w, col, m, evac, ctx_too=True):
            for src, t0, o, n in CH if ctx_too else CH[1:]:
                b, ps, last = proj3(w, col, src, 0, m=m, n=n, tok=t0)
                PB.free[b] = evac(ps[0:m, 0:n], o, n, last)
                run(beside[0])
            return last

        beside = [iter(())]

        gq_d, gk_d, gv_d, lk_d, gg_d, cq_d, ckv_d, mg_d = [], [], [], [], [], [], [], []
        alt = [0]

        def put(dst, lst, scale=None, func=None):
            def f(ps, o, n, last):
                if func is not None:
                    d = act(dst(o, n), ps, func, last)
                elif scale is not None:
                    d = ts(dst(o, n), ps, scale, None, MUL, None, last)
                else:
                    alt[0] ^= 1
                    d = cp((VE, AC)[alt[0]], dst(o, n), ps, last)
                lst.append(d)
                return d
            return f

        def token_major(w, i, evac):
            src, t0 = (HC, 128 * i) if i < 2 else (HL, 128 * (i - 2))
            b, ps, fr = PB.take()
            for c in range(8):
                last = mm3(ps[:, :], src, w, c, slice(t0, t0 + 128), slice(0, 512), c == 0, c == 7, fr, w.m, src.m)
            PB.free[b] = evac(ps[:, :], last)
            return last

        w = joined(WS.get(), WS.get())
        for i in range(10):
            last = token_major(w, i, lambda ps, m, i=i: cp((VE, AC)[i % 2], GV[:, i, :], ps, m))
            gv_d.append(PB.free[PB.order[(PB.at - 1) % 8]])
            if i in (3, 6):
                WS.split()
        WS.done(last)
        WS.done(last)
        w = joined(WS.get(), WS.get())
        for i in range(8):
            last = token_major(w, i + 2, lambda ps, m, i=i: act(MG[:, i, :], ps, ACT.Silu, m))
            mg_d.append(PB.free[PB.order[(PB.at - 1) % 8]])
            if i == 5:
                WS.split()
        WS.done(last)
        WS.done(last)

        def both(w, f):
            for q in range(2):
                last = f(w, q)
                if q == 0:
                    WS.split()
            WS.done(last)
            return last

        both(WS.get(), lambda w, j: cm_lc(w, 128 * j, 128, put(lambda o, n, j=j: CQ[:, j, o - 256:o - 256 + n], cq_d), False))
        w = WS.get()
        for k in range(2):
            cm_lc(w, 160 + 16 * k, 16, put(lambda o, n, k=k: LK[32 * k:32 * k + 16, o:o + n], lk_d))
        WS.split()
        cm_lc(w, 0, 128, put(lambda o, n: CKV[:, o:o + n], ckv_d))
        ckv_last = cm_lc(w, 128, 32, put(lambda o, n: LK[64:96, o:o + n], lk_d))
        WS.done(ckv_last)

        def latent_norms():
            MSQ, MR = [mem(147 + 2 * i, [512]) for i in range(4)], [mem(155, [512]), mem(157, [512])]
            msf, mrf = [ckv_last] * 4, [ckv_last] * 2
            k = t = 0
            for src, gain, nj, chunks, dn, lst in ((CKV.unsqueeze(1), kvc, 1, ((0, 256), (256, 512), (768, 512)), ckv_d, kvn),
                                                   (CQ, qnc, 2, ((0, 512), (512, 512)), cq_d, cqn)):
                for o, n in chunks:
                    qs = []
                    for j in range(nj):
                        i = (k + j) % 4
                        qs.append(act(MSQ[i][:, 0:n], src[:, j, o:o + n], ACT.Square, dn, msf[i]))
                    yield
                    b, ps, fr = PB.take()
                    for j in range(nj):
                        last = mm(ps[:, 0:n], cst("ones"), MSQ[k % 4][:, 0:n], j == 0, j == nj - 1, qs[j], fr)
                        msf[k % 4] = last
                        k += 1
                    r = rsq(MR[t][:, 0:n], ps[:, 0:n], 128 * nj, last, mrf[t])
                    PB.free[b] = r
                    yield
                    for j in range(nj):
                        d = stt(src[:, j, o:o + n], src[:, j, o:o + n], gain[:, j:j + 1], MR[t][:, 0:n], MUL, MUL, r, t_cp2)
                    mrf[t] = d
                    t = 1 - t
                    lst.append(d)

        cqn, kvn = [], []
        beside[0] = norms = latent_norms()

        both(WS.get(), lambda w, j: cm_lc(w, 128 * j, 128, put(lambda o, n, j=j: GQ[:, j, o - 256:o - 256 + n], gq_d, scale=0.125), False))
        both(WS.get(), lambda w, j: cm_lc(w, 128 * j, 128, put(lambda o, n, j=j: GK[:, j, o:o + n], gk_d)))
        run(norms, 100)
        norm_end = [cqn, kvn]
        for e in range(2):
            last = both(WS.get(), lambda w, j: cm_lc(w, 128 * j, 128, put(lambda o, n, j=2 * e + j: GG[:, j, o - 256:o - 256 + n], gg_d,
                                                                     func=ACT.Silu), False))
        pr_end = last

        YG = mem(32, [4, 1024])
        SETS = [(mem(48, [1280]), mem(53, [1024]), mem(57, [1024]), mem(64, [1024]), mem(72, [1280]), mem(90, [1280]),
                 mem(95, [1024]), small(16)),
                (mem(0, [1280]), mem(5, [1024]), mem(9, [1024]), mem(13, [1024]), mem(17, [1280]), mem(22, [1280]),
                 mem(27, [1024]), small(16))]
        KDT, SS = mem(77, [10, 128]), mem(82, [16, 128])
        RM = mem(99, [1024])
        W2G = mem(193, [256])
        l_w2g = [dma(SY, W2G[32 * k:32 * k + 16, :], A["gla_w2_2"][0, k], ex, pr_end) for k in range(2)]
        ATT = [[mem(61, [512]), mem(68, [512])], [mem(70, [512]), mem(194, [512])]]
        tz = []
        for k in range(2):
            for q in range(2):
                tz.append(VE(lambda e, k=k, q=q: e.memset(ATT[k][q], 0.0), pr_end))
        d = VE(lambda e: e.memset(RM, 1.0), pr_end)
        d = VE(lambda e: e.memset(RM[:, ::64], 0.0), d)
        tz.append(d)
        PG = Banks(banks, [0, 1, 2, 3])
        PG.free = dict(PB.free)
        gla_all = [gq_d, gk_d, gv_d, lk_d, gg_d, pr_end, tz]
        o_free = [PB.free.get(4 + i) for i in range(4)]
        free_set = [[pr_end], [pr_end]]
        prev_all = [pr_end]
        attf = [[None, None], [None, None]]
        yg_d = []
        AC(lambda e: e.preload_act_table_set("natural_log_exp_and_others"))
        units = {}

        def decays(u):
            tau, k = u // 2, u % 2
            GB, QM, KM, QE, KD, E1, E2, DC = SETS[k]
            free = free_set[k]
            g_d = []
            for o, n in ((0, 256), (256, 512), (768, 512)):
                b, ps, fr = PG.take()
                m1 = mm(ps[:, 0:n], W2G[32 * k:32 * k + 16, 128 * tau:128 * tau + 128], LK[32 * k:32 * k + 16, o:o + n],
                        True, True, fr, l_w2g, lk_d)
                bias = gbc[:, 2 * k + tau:2 * k + tau + 1]
                a0 = act(E1[:, o:o + n], ps[:, 0:n], ACT.Abs, m1, free, t_cp2, bias=bias)
                a = act(E1[:, o:o + n], E1[:, o:o + n], ACT.Exp, a0, scale=-1.0)
                a = act(E1[:, o:o + n], E1[:, o:o + n], ACT.Ln, a, bias=1.0)
                d = ts(KD[:, o:o + n], ps[:, 0:n], bias, 0.0, ADD, MIN, m1, a0, free, t_cp2)
                PG.free[b] = [d, a]
                d = tt(KD[:, o:o + n], KD[:, o:o + n], E1[:, o:o + n], SUB, d, a)
                g_d.append(d)
                yield
            o1_ = VE(lambda e: e.memset(E2[:, 0:256], 1.0), free)
            yield
            if k == 0:
                d = VE(lambda e: e.tensor_tensor_scan(GB[:, 0:256], E2[:, 0:256], KD[:, 0:256], 0.0, MUL, ADD), g_d, o1_, free)
                d2 = VE(lambda e: e.tensor_tensor_scan(GB[:, 256:1280], RM, KD[:, 256:1280], 0.0, MUL, ADD), tz, g_d, free)
            else:
                d = VE(lambda e: e.tensor_tensor_scan(GB[:, 0:256][:, ::-1], E2[:, 0:256], KD[:, 0:256][:, ::-1], 0.0, MUL, ADD), g_d, o1_, free)
                d2 = VE(lambda e: e.tensor_tensor_scan(GB[:, 256:1280][:, ::-1], RM, KD[:, 256:1280][:, ::-1], 0.0, MUL, ADD), tz, g_d)
            BL = GB[:, 256:1280].rearrange("p (c s) -> p c s", c=16)
            mid, end = (31, 63) if k == 0 else (32, 0)
            e1v = E1[:, 256:1280].rearrange("p (c s) -> p c s", c=16)
            bmid = BL[:, :, mid:mid + 1].broadcast_to([128, 16, 64])
            bend = BL[:, :, end:end + 1].broadcast_to([128, 16, 64])
            GKl, GQl = GK[:, tau, 256:1280], GQ[:, tau, :]
            a = tt(e1v, BL, bmid, SUB, d2)
            yield
            q1 = act(QM, E1[:, 256:1280], ACT.Exp, a, free, scale=1.0 / 16)
            q1 = tt(QM, QM, GQl, MUL, q1, gq_d)
            yield
            k1 = act(KM, E1[:, 256:1280], ACT.Exp, a, free, scale=-1.0 / 16)
            k1 = tt(KM, KM, GKl, MUL, k1, gk_d)
            yield
            q2 = act(QE, GB[:, 256:1280], ACT.Exp, d2, free, scale=1.0 / 16)
            q2 = tt(QE, QE, GQl, MUL, q2, gq_d)
            yield
            a = tt(KD[:, 256:1280].rearrange("p (c s) -> p c s", c=16), bend, BL, SUB, d2, d)
            ce = 255 if k == 0 else 0
            a2 = tt(KD[:, 0:256], GB[:, ce:ce + 1].broadcast_to([128, 256]), GB[:, 0:256], SUB, d)
            yield
            a = act(KD, KD, ACT.Exp, a, a2, scale=1.0 / 16)
            k2 = tt(KD, KD, GK[:, tau, :], MUL, a, gk_d)
            dc = act(DC, BL[:, :, end], ACT.Exp, d2, free, scale=1.0 / 16)
            units[u] = (k2, dc, q1, k1, q2)

        NBUF = [mem(196, [512]), mem(198, [512])]
        nbf = [pr_end, pr_end]
        run(decays(0), 100)
        for tau in range(2):
            for k in range(2):
                u = 2 * tau + k
                k2, dc, q1, k1, q2 = units[u]
                GB, QM, KM, QE, KD, E1, E2, DC = SETS[k]
                ahead = decays(u + 1) if u < 3 else iter(())
                kdt = []
                for q in range(3):
                    m_ = 4 if q < 2 else 2
                    b, ps, fr = PG.take()
                    for j in range(m_):
                        i = 4 * q + j
                        last = tr(ps[:, 128 * j:128 * j + 128], KD[:, 128 * i:128 * i + 128], cst("ident"), k2, fr)
                    d = cp(AC, KDT[:, 4 * q:4 * q + m_, :], ps[:, 0:128 * m_].rearrange("p (a b) -> p a b", a=m_), last, prev_all)
                    PG.free[b] = d
                    kdt.append(d)
                b, ps, fr = PG.take()
                for hh in range(2):
                    hv = slice(128 * (2 * tau + hh), 128 * (2 * tau + hh) + 128)
                    for i in range(2):
                        last = mm(ps[64 * hh:64 * hh + 64, 0:128], KDT[:, i, 64 * hh:64 * hh + 64], GV[:, i, hv], i == 0, i == 1,
                                  kdt, fr, gv_d)
                order = list(range(16)) if k == 0 else list(range(15, -1, -1))
                s_d = cp(VE, SS[:, order[0], :], ps[:, 0:128], last, prev_all)
                PG.free[b] = s_d
                s_at = {order[0]: s_d}
                for q in range(2):
                    grp = order[8 * q:8 * q + 8]
                    bk = {}
                    for par in range(2):
                        b, ps, fr = PG.take()
                        bk[par] = (b, ps)
                        for n_, c in enumerate([c for c in grp if c % 2 == par]):
                            p0, i = 64 * par, 2 + c // 2
                            for hh in range(2):
                                hv = slice(128 * (2 * tau + hh), 128 * (2 * tau + hh) + 128)
                                last = mm(ps[64 * hh:64 * hh + 64, 128 * n_:128 * n_ + 128],
                                          KDT[p0:p0 + 64, i, 64 * hh:64 * hh + 64], GV[p0:p0 + 64, i, hv], True, True, kdt, fr)
                    for n_, c in enumerate(grp):
                        nx = order.index(c) + 1
                        if nx < 16:
                            c0 = 128 * (n_ // 2)
                            s_d = stt(SS[:, order[nx], :], SS[:, c, :], DC[:, c:c + 1], bk[c % 2][1][:, c0:c0 + 128], MUL, ADD,
                                      last, s_d, dc)
                            s_at[order[nx]] = s_d
                    PG.free[bk[0][0]] = PG.free[bk[1][0]] = s_d
                if u == 3:
                    set_free = [kdt, k2, dc, q1, k1, q2, s_at[order[0]]]
                msk = cst("glaf" if k == 0 else "glar").unsqueeze(1).broadcast_to([128, 4, 128]).bitcast(I32)

                def scores(g_):
                    b, ps, fr = PG.take()
                    for n_ in range(4):
                        i, hh = 4 * (g_ // 2) + n_, g_ % 2
                        last = mm(ps[:, 128 * n_:128 * n_ + 128], KM[64 * hh:64 * hh + 64, 128 * i:128 * i + 128],
                                  QM[64 * hh:64 * hh + 64, 128 * i:128 * i + 128], True, True, q1, k1, fr)
                    at_ = ATT[k][g_ % 2]
                    PG.free[b] = d = VE(lambda e, msk=msk: e.copy_predicated(
                        at_.rearrange("p (a b) -> p a b", a=4), msk, ps[:, :].rearrange("p (a b) -> p a b", a=4)),
                        last, attf[k][g_ % 2], tz)
                    return d

                d_next = scores(0)
                for g_ in range(4):
                    run(ahead, 3)
                    d = d_next
                    if g_ < 3:
                        d_next = scores(g_ + 1)
                    at_ = ATT[k][g_ % 2]
                    for n_ in range(4):
                        i, hh = 4 * (g_ // 2) + n_, g_ % 2
                        h = 2 * tau + hh
                        ob = banks[4 + 2 * hh + i // 4]
                        c0 = 128 * (i % 4)
                        mm(ob[:, c0:c0 + 128], GV[:, 2 + i, 128 * h:128 * h + 128], at_[:, 128 * n_:128 * n_ + 128], k == 0 and n_ == 0, False,
                           d, o_free if k == 0 else None)
                        for c in (2 * i, 2 * i + 1):
                            last = mm(ob[:, c0 + 64 * (c % 2):c0 + 64 * (c % 2) + 64], SS[64 * hh:64 * hh + 64, c, :],
                                      QE[64 * hh:64 * hh + 64, 64 * c:64 * c + 64], False, k == 1, s_at[c], q2)
                    attf[k][g_ % 2] = last
                prev_all = [last]
                free_set[k] = [last, s_d]
                run(ahead, 100)
            fr4 = []
            pend = []
            for n_, (hh, half) in enumerate([(0, 0), (0, 1), (1, 0), (1, 1)]):
                ob = banks[4 + 2 * hh + half]
                sq = act(NBUF[n_ % 2], ob[:, :], ACT.Square, last, nbf[n_ % 2])
                b, ps, fr = PG.take()
                m1 = mm(ps[:, :], cst("ones"), NBUF[n_ % 2], True, True, sq, fr)
                r = rsq(NBUF[n_ % 2], ps[:, :], 128, m1)
                PG.free[b] = r
                h, s0 = 2 * tau + hh, slice(512 * half, 512 * half + 512)
                d = stt(YG[:, h, s0], ob[:, :], gnc[:, 0:1], NBUF[n_ % 2], MUL, MUL, r, t_cp2)
                nbf[n_ % 2] = d
                fr4.append(d)
                yg_d.append(tt(YG[:, h, s0], YG[:, h, s0], GG[:, h, s0], MUL, d, gg_d))
            o_free = fr4
        for b in range(4):
            PB.free[b] = PG.free.get(b)
            PB.free[4 + b] = fr4
        gla_end = [yg_d[-1], m1]

        QT, KT, MV = mem(48, [8, 1024], p=96), mem(80, [8, 1280], p=96), mem(122, [10, 512])
        WQN, WQR, WKN, WKVV = mem(17, [2, 512]), mem(21, [2, 256]), mem(23, [512]), mem(25, [512])
        ROP = mem(192, [2, 1024])
        MSQ = [mem(157, [512]), mem(159, [512])]
        MR = mem(161, [512])
        uq = A["mla_w_uq_2"][0].rearrange("(j p) (h x) -> p j h x", p=128, h=8)
        ukv = A["mla_w_ukv_2"][0].rearrange("p (h x) -> p h x", h=8)
        wml = Load(sem())
        for j in range(2):
            dma(SY, WQN[:, j, :].rearrange("p (h x) -> p h x", h=8), uq[:, j, :, 0:64], set_free, load=wml)
            dma(SY, WQR[:, j, :].rearrange("p (h x) -> p h x", h=8), uq[:, j, :, 64:96], load=wml)
        dma(SY, WKN.rearrange("p (h x) -> p h x", h=8), ukv[:, :, 0:64], load=wml)
        l_uq = l_kv = dma(SY, WKVV.rearrange("p (h x) -> p h x", h=8), ukv[:, :, 64:128], load=wml)
        l_rp = dma(SY, ROP, A["k_rope"].rearrange("a p n -> p a n"), gla_end)
        mrf = gla_end
        qt_d, kt_d, mv_d = [], [], []
        RQ = [mem(157, [512]), mem(159, [512])]
        RT1 = mem(161, [512])
        RT2 = mem(142 + 5 - 5, [512])
        rqf = [mrf, mrf]
        rtf = mrf
        kr0 = cp(AC, KT[64:96, 0, 0:256], LK[64:96, 0:256], lk_d, gla_end)
        krl = [kr0]
        for half in range(2):
            s0 = slice(512 * half, 512 * half + 512)
            lk = LK[64:96, 256 + 512 * half:768 + 512 * half]
            b, ps, fr = PB.take()
            m1 = mm(ps[64:96, :], cst("perm")[64:96, 64:96], lk, True, True, fr, lk_d, gla_end)
            d = tt(RT1[64:96, :], ps[64:96, :], ROP[64:96, 1, s0], MUL, m1, l_rp, rtf)
            PB.free[b] = d
            ko = KT[64:96, 0, 256 + 512 * half:768 + 512 * half]
            a = tt(ko, lk, ROP[64:96, 0, s0], MUL, l_rp, gla_end)
            d = tt(ko, ko, RT1[64:96, :], ADD, d, a)
            rtf = d
            krl.append(d)
        for h in range(1, 8):
            kt_d.append(cp(GP, KT[64:96, h, :], KT[64:96, 0, :], krl))
        kt_d += krl
        for hp in range(4):
            for o, n in ((0, 256), (256, 512), (768, 512)):
                b, ps, fr = PB.take()
                last = mm(ps[:, 0:n], WKN[:, 128 * hp:128 * hp + 128], CKV[:, o:o + n], True, True, fr, l_kv, kvn)
                d1 = cp(VE, KT[0:64, 2 * hp, o:o + n], ps[0:64, 0:n], last, gla_end)
                d2 = cp(AC, KT[0:64, 2 * hp + 1, o:o + n], ps[64:128, 0:n], last, gla_end)
                PB.free[b] = [d1, d2]
                kt_d += [d1, d2]
        for hp in range(4):
            for half in range(2):
                s0 = slice(512 * half, 512 * half + 512)
                b, ps, fr = PB.take()
                for j in range(2):
                    last = mm(ps[:, :], WQN[:, j, 128 * hp:128 * hp + 128], CQ[:, j, s0], j == 0, j == 1, fr, l_uq, cqn)
                d1 = cp(VE, QT[0:64, 2 * hp, s0], ps[0:64, :], last, gla_end)
                d2 = cp(AC, QT[0:64, 2 * hp + 1, s0], ps[64:128, :], last, gla_end)
                PB.free[b] = [d1, d2]
                qt_d += [d1, d2]
        k = 0
        for g_ in range(2):
            for half in range(2):
                s0 = slice(512 * half, 512 * half + 512)
                b, ps, fr = PB.take()
                for j in range(2):
                    last = mm(ps[:, :], WQR[:, j, 128 * g_:128 * g_ + 128], CQ[:, j, s0], j == 0, j == 1, fr, l_uq, cqn)
                r = cp(AC, RQ[k % 2], ps[:, :], last, rqf[k % 2])
                b2, ps2, fr2 = PB.take()
                m2 = mm(ps2[:, :], cst("perm"), RQ[k % 2], True, True, r, fr2)
                d = tt(RT1, ps2[:, :], ROP[:, 1, s0], MUL, m2, rtf)
                PB.free[b2] = d
                a = tt(RQ[k % 2], RQ[k % 2], ROP[:, 0, s0], MUL, m2)
                PB.free[b] = r
                a = tt(RQ[k % 2], RQ[k % 2], RT1, ADD, a, d)
                rtf = a
                for q in range(4):
                    c_ = cp(AC if q % 2 else VE, QT[64:96, 4 * g_ + q, s0], RQ[k % 2][32 * q:32 * q + 32, :], a, gla_end)
                    qt_d.append(c_)
                rqf[k % 2] = qt_d[-2:]
                k += 1
        for i in range(10):
            b, ps, fr = PB.take()
            last = mm(ps[:, :], CKV[:, 128 * i:128 * i + 128], WKVV, True, True, fr, l_kv, kvn)
            d = cp((VE, AC)[i % 2], MV[:, i, :], ps[:, :], last, gla_end)
            PB.free[b] = d
            mv_d.append(d)
        up_end = [last, rtf]
        l_x3 = [xL[i](SY, X[:, i, :], x2d[i], gla_end, up_end, t_x2) for i in range(NT)]

        YM = mem(147, [4, 1024])
        PP = [mem(163, [1280]), mem(168, [1280])]
        PT = [mem(192, [10, 128]), mem(142, [10, 128])]
        OT = [mem(173, [512]), mem(197, [512])]
        NM, RS2, RI = small(8), [small(8), small(8)], small(8)
        SCALE = 96.0 ** -0.5
        ready = [qt_d, kt_d, mv_d, up_end]
        start = [PB.free.get(b) for b in range(8)]
        sfree = [start, start]
        tfree = [start]
        ppf, ptf = [up_end, up_end], [up_end, up_end]
        otf = [up_end, up_end]
        ym_d = []
        its = [(qt, h) for qt in range(8) for h in range(8)]
        st = {}

        def score_part(s, q):
            qt, h = its[s]
            o, n = ((0, 512), (512, 512), (1024, 256))[q]
            return mm(PSM[:, 3 * (s % 2) + q, 0:n], QT[:, h, 128 * qt:128 * qt + 128], KT[:, h, o:o + n], True, True,
                      sfree[s % 2], ready)

        def row_max(s, last):
            qt, h = its[s]
            ps = PSM[:, 3 * (s % 2):3 * (s % 2) + 3, :].rearrange("p a b -> p (a b)")[:, 0:1280]
            d = VE(lambda e: e.tensor_reduce(NM[:, h:h + 1], ps, AX, MAX), last, st.get(("e", s - 8)))
            return ts(NM[:, h:h + 1], NM[:, h:h + 1], -SCALE, None, MUL, None, d)

        def soften(s, d):
            qt, h = its[s]
            k = s % 2
            ps = PSM[:, 3 * k:3 * k + 3, :].rearrange("p a b -> p (a b)")[:, 0:1280]
            e_ = AC(lambda e: e.activation(PP[k], ps, ACT.Exp, bias=NM[:, h:h + 1], scale=SCALE,
                                           accum_out=RS2[qt % 2][:, h:h + 1]), d, ppf[k], st.get(("o", qt - 2)))
            sfree[k] = e_
            st[("e", s)] = e_

        tb = banks[6]

        def turn_part(s, q):
            k = s % 2
            m_ = 4 if q < 2 else 2
            for j in range(m_):
                i = 4 * q + j
                last = tr(tb[:, 128 * j:128 * j + 128], PP[k][:, 128 * i:128 * i + 128], cst("ident"), st[("e", s)], tfree[0])
            d = cp((VE, AC, VE)[q], PT[k][:, 4 * q:4 * q + m_, :], tb[:, 0:128 * m_].rearrange("p (a b) -> p a b", a=m_), last, ptf[k])
            tfree[0] = d
            ppf[k] = last
            return d

        def mix(s, pt):
            qt, h = its[s]
            k = s % 2
            for i in range(10):
                last = mm(banks[7][:, 64 * h:64 * h + 64], PT[k][:, i, :], MV[:, i, 64 * h:64 * h + 64], i == 0, i == 9,
                          pt[i // 4], of[0] if h == 0 else None)
            ptf[k] = last
            if h == 7:
                kk = qt % 2
                r = VE(lambda e: e.reciprocal(RI, RS2[kk]), st[("e", s)])
                d = tt(OT[kk].rearrange("p (a b) -> p a b", a=8), banks[7][:, :].rearrange("p (a b) -> p a b", a=8),
                       RI.unsqueeze(2).broadcast_to([128, 8, 64]), MUL, last, r, otf[kk])
                of[0] = d
                st[("o", qt)] = r
                return tt(OT[kk], OT[kk], MG[:, qt, :], MUL, d, mg_d)

        def turn_out(qt, d):
            kk = qt % 2
            for j in range(4):
                last = tr(tb[:, 128 * j:128 * j + 128], OT[kk][:, 128 * j:128 * j + 128], cst("ident"), d, tfree[0])
            otf[kk] = last
            d = cp(AC, YM[:, :, 128 * qt:128 * qt + 128], tb[:, :].rearrange("p (a b) -> p a b", a=4), last, up_end)
            tfree[0] = d
            ym_d.append(d)

        of = [start]
        late = None
        pts = {}
        for s in range(67):
            if 2 <= s < 66:
                pts[s - 2] = []
            for q in range(3):
                if 2 <= s < 66:
                    pts[s - 2].append(turn_part(s - 2, q))
                if q == 0 and 1 <= s < 65:
                    top = row_max(s - 1, last)
                if q == 1 and 1 <= s < 65:
                    soften(s - 1, top)
                if s < 64:
                    new = score_part(s, q)
            last = new
            if late:
                turn_out(*late)
                late = None
            if s >= 3:
                d = mix(s - 3, pts.pop(s - 3))
                if its[s - 3][1] == 7:
                    late = (its[s - 3][0], d)
        turn_out(*late)
        for b in range(8):
            PB.free[b] = [sfree, tfree, of]
        ml_end = [ym_d[-1], ptf]

        GROW, PLG, PLB = mem(120 - 8, [1024]), mem(116, [1024]), mem(122, [1024])

        def post(layer, l_x, W, lw, tile_of, yd, G_, P1_, P2_, w0, tmps):
            l1 = dma(SY, G_, ada_d[layer, 0:1, 2048:3072].broadcast_to([128, 1024]), w0)
            l2 = dma(SY, P1_, A["post_ln_g_2"][layer:layer + 1, :].broadcast_to([128, 1024]), w0)
            l3 = dma(SY, P2_, A["post_ln_b_2"][layer:layer + 1, :].broadcast_to([128, 1024]), w0)
            done = []
            alpha = float(4 ** 0.25)
            fr_t = [w0, w0]
            bnf = None
            for i in range(NT):
                xi = X[:, i, :]
                ds_ = []
                for q in range(2):
                    b, ps, fr = PB.take()
                    for j in range(8):
                        last = mm(ps[:, :], tile_of(j)[:, 128 * i:128 * i + 128], W[:, j, 512 * q:512 * q + 512], j == 0, j == 7,
                                  fr, lw, yd)
                    s_ = slice(512 * q, 512 * q + 512)
                    d = tt(tmps[q], ps[:, :], G_[:, s_], MUL, last, l1, fr_t[q])
                    PB.free[b] = d
                    d = stt(xi[:, s_], xi[:, s_], alpha, tmps[q], MUL, ADD, d, l_x[i])
                    fr_t[q] = d
                    ds_.append(d)
                mvi = mvv[:, i, :]
                d = stats(xi, 1024, bnb, mvi, [ds_, bnf])
                bnf = d
                r = rsq(rs8[:, i:i + 1], mvi[:, 1:2], 1, d)
                n_ = stt(nb8[:, i:i + 1], mvi[:, 0:1], -1.0, rs8[:, i:i + 1], MUL, MUL, r)
                a = act(xi, xi, ACT.Identity, n_, scale=rs8[:, i:i + 1], bias=nb8[:, i:i + 1])
                a = tt(xi, xi, P1_, MUL, a, l2, lane=GP)
                a = tt(xi, xi, P2_, ADD, a, l3, lane=GP)
                done.append(a)
            return done, last

        WO2 = mem(48, [8, 1024])
        w2v = A["even_w_out_2"][0].rearrange("(j p) n -> p j n", p=128)
        l_wo2 = [dma(SY, WO2[:, 4 * q:4 * q + 4, :], w2v[:, 4 * q:4 * q + 4, :], ml_end) for q in range(2)]
        x3, po_end = post(0, l_x3, WO2, l_wo2, lambda j: YG[:, j, :] if j < 4 else YM[:, j - 4, :], [ym_d, yg_d], GROW, PLG, PLB, ml_end,
                          [mem(126, [512]), mem(128, [512])])

        OS = [64, 80, 96]
        for kb in OS:
            slots[kb] = Slot(kb)
            slots[kb].used = [po_end, x3]
        FT, FGT, UT, VT = mem(112, [4, 1024]), mem(128, [4, 1024]), mem(144, [4, 1024]), mem(160, [8, 512])
        w_d = A["odd_w_in_2"][0].rearrange("(p c) n -> p c n", c=8)
        x3d = nc.dram_tensor("x3d", [NT, 128, D], F32).ap()
        x3l = Load(sem())
        dft = [A["k_dft"][part].rearrange("(t p) k -> p t k", p=128) for part in range(2)]
        cols = [0, 256, 1024, 1280, 2048, 2304, 512, 768]
        seq = wide(OS[0], OS[1], w_d, 1536) + [piece(OS[(i + 2) % 3], w_d, c) for i, c in enumerate(cols)]
        dseq = [(part, half, q) for half in range(2) for part in range(2) for q in range(2)]
        seq += [(OS[(i + 10) % 3], [(dft[part][:, 4 * q:4 * q + 4, 512 * half:512 * half + 512], 0, 512)], 4, 512)
                for i, (part, half, q) in enumerate(dseq)]
        WS = Stream(seq)
        for i in range(NT):
            t_x3 = dma(AC, x3d[i], X[:, i, :], x3[i], load=x3l)
        DFC, SGB, SGW, SGT = mem(192, [256]), mem(193, [512]), mem(195, [4, 128]), mem(197, [4, 128])
        l_dfc = dma(SY, DFC, A["k_small"][:, NC - 256:NC], po_end, x3)
        l_sgb = dma(SY, SGB, A["sgu_b_2"].rearrange("a g t -> a (g t)").broadcast_to([128, 512]), po_end, x3)
        l_sgw = dma(SY, SGW, A["sgu_w_2"][0].rearrange("g t s -> t g s"), po_end, x3)
        tx = token_stats(NT, lambda i: X[:, i, :], x3, False)
        HO = Two(*two_rows(32, 0, T), [])
        hO = split_major(NT, lambda i: X[:, i, :], [tx, po_end, t_x3], True, HO, SCL["l1"], SH["l1"], [po_end])
        b, ps, fr = PB.take()
        for g_ in range(4):
            last = tr(ps[:, 128 * g_:128 * g_ + 128], SGW[:, g_, :], cst("ident"), l_sgw, fr)
        t_sgt = cp(AC, SGT, ps[:, :].rearrange("p (a b) -> p a b", a=4), last, po_end)
        PB.free[b] = t_sgt
        ft_d, fg_d, u_d, v_d = [], [], [], []
        VST = mem(184, [32, 6])
        VMV = mem(185, [32, 2])
        VR, VN = mem(185.5, [32]), mem(185.75, [32])
        w = joined(WS.get(), WS.get())
        vs = None
        for i in range(8):
            b, ps, fr = PB.take()
            for c in range(8):
                last = mm3(ps[:, :], HO, w, c, slice(128 * i, 128 * i + 128), slice(0, 512), c == 0, c == 7, fr, w.m, hO)
            d = act(VT[:, i, :], ps[:, :], ACT.Gelu, last)
            PB.free[b] = d
            for g_ in range(4):
                n_ = 4 * i + g_
                a = VE(lambda e, n_=n_, i=i, g_=g_: e.bn_stats(VST[:, n_, :], VT[:, i, 128 * g_:128 * g_ + 128]), d, hO)
                vs = VE(lambda e, n_=n_: e.bn_aggr(VMV[:, n_, :], VST[:, n_, :]), a)
            if i == 5:
                WS.split()
        WS.done(last)
        WS.done(last)

        def channels(j0, evac):
            w = WS.get()
            for j in range(2):
                for half in range(2):
                    b, ps, last = proj3(w, 128 * j, HO, half)
                    PB.free[b] = evac(j0 + j, slice(512 * half, 512 * half + 512), ps[:, :], last)
                if j == 0:
                    WS.split()
            WS.done(last)
            return last

        def keep(lst, d):
            lst.append(d)
            return d

        for j in (0, 2):
            channels(j, lambda j, s0, ps, m: keep(ft_d, cp(VE, FT[:, j, s0], ps, m)))
        for j in (0, 2):
            channels(j, lambda j, s0, ps, m: keep(u_d, act(UT[:, j, s0], ps, ACT.Gelu, m)))
        r = rsq(VR, VMV[:, :, 1], 1, vs)
        nb_ = stt(VN, VMV[:, :, 0], -1.0, VR, MUL, MUL, r)
        for i in range(8):
            for g_ in range(4):
                n_ = 4 * i + g_
                v = VT[:, i, 128 * g_:128 * g_ + 128]
                v_d.append(ts(v, v, VR[:, n_:n_ + 1], VN[:, n_:n_ + 1], MUL, ADD, nb_))
        SGX = [mem(176, [512]), mem(178, [512])]
        sgf = [hO, hO]
        us_d = []

        def gated(j, s0, ps, m):
            k = len(us_d) % 2
            d = act(SGX[k], ps, ACT.Silu, m, sgf[k])
            sgf[k] = keep(us_d, tt(UT[:, j, s0], UT[:, j, s0], SGX[k], MUL, d, u_d))
            return d

        for j in (0, 2):
            channels(j, gated)
        for j in (0, 2):
            ho_end = channels(j, lambda j, s0, ps, m: keep(fg_d, act(FGT[:, j, s0], ps, ACT.Silu, m)))
        l_x4 = [xL[i](SY, X[:, i, :], x3d[i], ho_end, t_x3) for i in range(NT)]
        ys_d = []
        k = 0
        for g_ in range(4):
            for half in range(2):
                s0 = slice(512 * half, 512 * half + 512)
                b, ps, fr = PB.take()
                for q in range(4):
                    i = 4 * half + q
                    last = mm(ps[:, 128 * q:128 * q + 128], VT[:, i, 128 * g_:128 * g_ + 128], SGT[:, g_, :], True, True,
                              v_d, t_sgt, fr)
                bb = SGB[:, 128 * g_:128 * g_ + 128].unsqueeze(1).broadcast_to([128, 4, 128])
                d = tt(SGX[k % 2].rearrange("p (a b) -> p a b", a=4), ps[:, :].rearrange("p (a b) -> p a b", a=4), bb, ADD,
                       last, l_sgb, sgf[k % 2])
                PB.free[b] = d
                d = tt(UT[:, g_, s0], UT[:, g_, s0], SGX[k % 2], MUL, d, us_d)
                sgf[k % 2] = d
                ys_d.append(d)
                k += 1
        AB = Two(*two_rows(32, 160, T), [])
        for i in range(8):
            for gg_ in range(2):
                b, ps, fr = PB.take()
                for q in range(2):
                    g_ = 2 * gg_ + q
                    last = mm(ps[:, 256 * q:256 * q + 256], FT[:, g_, 128 * i:128 * i + 128], DFC, True, True, ft_d, l_dfc, fr)
                s0 = slice(512 * gg_, 512 * gg_ + 512)
                h = AB.hi[i][:, s0]
                a = act(h, ps[:, :], ACT.Copy, last, ho_end)
                d = tt(AB.lo[i][:, s0], ps[:, :], h.bitcast(F32), SUB, a, ys_d)
                PB.free[b] = d
                AB.m.append(d)
            if i in (2, 5):
                WS.split()
        ab_end = last
        yf_d = []
        for half in range(2):
            s0 = slice(512 * half, 512 * half + 512)
            bk = [PB.take() for _ in range(4)]
            for part in range(2):
                for q in range(2):
                    w = WS.get()
                    for g_ in range(4):
                        _, ps, fr = bk[g_]
                        o = 256 * g_ + 128 * part
                        tb2 = Two(AB.hi[4 * q:4 * q + 4], AB.lo[4 * q:4 * q + 4], None)
                        for i in range(4):
                            last = mm3(ps[:, :], tb2, w, i, slice(o, o + 128), slice(0, 512), part + q + i == 0,
                                       part == 1 and q == 1 and i == 3, AB.m, w.m, fr)
                        if g_ == 1:
                            WS.split()
                    WS.done(last)
            for g_ in range(4):
                b, ps, _ = bk[g_]
                d = tt(FT[:, g_, s0], ps[:, :], FGT[:, g_, s0], MUL, last, fg_d, ab_end)
                PB.free[b] = d
                yf_d.append(d)
        f_last = last
        WO3 = mem(64, [8, 1024])
        w3v = A["odd_w_out_2"][0].rearrange("(j p) n -> p j n", p=128)
        l_wo3 = [dma(SY, WO3[:, 4 * q:4 * q + 4, :], w3v[:, 4 * q:4 * q + 4, :], f_last, ys_d) for q in range(2)]
        x4, pe4 = post(1, l_x4, WO3, l_wo3, lambda j: FT[:, j, :] if j < 4 else UT[:, j - 4, :], [yf_d, ys_d],
                       mem(128, [1024]), mem(132, [1024]), mem(136, [1024]), [yf_d, ys_d, f_last], [mem(176, [512]), mem(178, [512])])
        od = out[0].rearrange("(t p) d -> p t d", p=128)

        for i in range(NT):
            stores.append(dma(SY, od[:, i, :], X[:, i, :], x4[i]))
        stores += [t_x2, t_x3, y_end, t_yz, t_ada, t_h2[-1], t_ini, t_sc]
        for s in stores:
            SY(lambda e: e.nop(), s)
        for l in lanes:
            l.count()
        block = ctx.enter_context(nc.Block())
        block.sync(SY.emit)
        block.tensor(PE.emit)
        block.scalar(AC.emit)
        block.vector(VE.emit)
        block.gpsimd(GP.emit)


_OUT = ((1, 1024, 1024), "float32")


def kernel(**inputs):
    import numpy as _np
    import concourse.bacc as _bacc
    from concourse import mybir as _mybir
    from concourse.bass_utils import run_bass_kernel_spmd as _run

    nc = _bacc.Bacc("TRN2", target_bir_lowering=False, num_devices=1)
    arrays, aps = {}, {}
    for name, a in {**inputs, **constants()}.items():
        a = _np.ascontiguousarray(a)
        arrays[f"in_{name}_dram"] = a
        aps[name] = nc.dram_tensor(f"in_{name}_dram", a.shape, _mybir.dt.from_np(a.dtype), kind="ExternalInput").ap()
    out = nc.dram_tensor("out_0_dram", _OUT[0], _mybir.dt.from_np(_np.dtype(_OUT[1])), kind="ExternalOutput").ap()
    build(nc, aps, out)
    r = _run(nc, [arrays], core_ids=[0])
    return r.results[0]["out_0_dram"]
```
